# Optimizing a Trainium2 kernel written in Bass

```python
import jax, jax.numpy as jnp
from jax import lax
import numpy as np
import math

D_MODEL = 1024
BATCH = 1
SEQ = 256
DEPTH = 1

CHUNK = 64
RWKV_HEAD_DIM = 64
RWKV_WIDTH = D_MODEL
RWKV_HEADS = RWKV_WIDTH // RWKV_HEAD_DIM
CONV_WIDTH = D_MODEL
CONV_KERNEL = 31
DECAY_LORA = D_MODEL // 16
A_LORA = D_MODEL // 16
V_LORA = D_MODEL // 32
G_LORA = D_MODEL // 8
D_FF = -(-8 * D_MODEL // (3 * 256)) * 256
N_IN_COLS = 3 * RWKV_WIDTH + 2 * CONV_WIDTH + 2 * D_MODEL
RMS_EPS = 1e-6
LN_EPS = 1e-5
GN_EPS = 64e-5


def rms_norm(x, g):
    xf = x.astype(jnp.float32)
    y = xf * lax.rsqrt(jnp.mean(xf * xf, axis=-1, keepdims=True) + RMS_EPS)
    return (y * g.astype(jnp.float32)).astype(x.dtype)

def layer_norm(x, w, b):
    xf = x.astype(jnp.float32)
    mu = jnp.mean(xf, axis=-1, keepdims=True)
    var = jnp.mean(jnp.square(xf - mu), axis=-1, keepdims=True)
    y = (xf - mu) * lax.rsqrt(var + LN_EPS)
    return (y * w.astype(jnp.float32) + b.astype(jnp.float32)).astype(x.dtype)

def token_shift(x):
    return jnp.pad(x[:, :-1], ((0, 0), (1, 0), (0, 0)))

def lerp_shift(x, mu):
    return x + (token_shift(x) - x) * mu

def wkv7(r, w, k, v, a, b):
    B, T, H, N = r.shape
    seq = tuple(jnp.moveaxis(t.astype(jnp.float32), 1, 0) for t in (r, w, k, v, a, b))

    def step(S, inp):
        r_t, w_t, k_t, v_t, a_t, b_t = inp
        sa = jnp.einsum('bhvk,bhk->bhv', S, a_t)
        S = S * w_t[:, :, None, :] + sa[..., None] * b_t[:, :, None, :] + v_t[..., None] * k_t[:, :, None, :]
        y = jnp.einsum('bhvk,bhk->bhv', S, r_t)
        return S, y

    S0 = jnp.zeros((B, H, N, N), jnp.float32)
    _, ys = lax.scan(step, S0, seq)
    return jnp.moveaxis(ys, 0, 1)

def rwkv7_time_mix(h, p_r, p_k, p_v, v_first, vres, mu_rkv, mu_wag, w0, w1, w2, a0, a1, a2,
                   g1, g2, kk_scale, ka_scale, r_k, gn_w, gn_b, w_o):
    B, T, _ = h.shape
    xx = token_shift(h) - h
    xw = h + xx * mu_wag[0]
    xa = h + xx * mu_wag[1]
    xg = h + xx * mu_wag[2]
    r = lerp_shift(p_r, mu_rkv[0])
    k = lerp_shift(p_k, mu_rkv[1])
    v = lerp_shift(p_v, mu_rkv[2])
    w_log = -jax.nn.softplus(-(w0 + jnp.tanh(xw @ w1) @ w2).astype(jnp.float32)) - 0.5
    decay = jnp.exp(-jnp.exp(w_log))
    if vres is None:
        v_first = v
    else:
        mu_v, v0, v1, v2 = vres
        xv = h + xx * mu_v
        v = v + (v_first - v) * jax.nn.sigmoid(v0 + (xv @ v1) @ v2)
    a = jax.nn.sigmoid(a0 + (xa @ a1) @ a2)
    g = jax.nn.sigmoid(xg @ g1) @ g2

    def heads(t):
        return t.reshape(B, T, RWKV_HEADS, RWKV_HEAD_DIM)

    kk = heads(k * kk_scale).astype(jnp.float32)
    kk = kk / jnp.maximum(jnp.sqrt(jnp.sum(kk * kk, axis=-1, keepdims=True)), 1e-12)
    k = k * (1.0 + (a - 1.0) * ka_scale)
    rh, kh, vh, ah = heads(r), heads(k), heads(v), heads(a)
    y = wkv7(rh, heads(decay), kh, vh, -kk, kk * ah.astype(jnp.float32))
    mu = jnp.mean(y, axis=-1, keepdims=True)
    var = jnp.mean(jnp.square(y - mu), axis=-1, keepdims=True)
    y = ((y - mu) * lax.rsqrt(var + GN_EPS)).reshape(B, T, RWKV_WIDTH)
    y = y * gn_w.astype(jnp.float32) + gn_b.astype(jnp.float32)
    bonus = (jnp.sum((rh * kh * r_k).astype(jnp.float32), axis=-1, keepdims=True) * vh.astype(jnp.float32))
    y = ((y + bonus.reshape(B, T, RWKV_WIDTH)) * g.astype(jnp.float32)).astype(h.dtype)
    return y @ w_o, v_first

def conformer_conv(p_c, dw, dw_b, ln_w, ln_b, w_o):
    u, gate = jnp.split(p_c, 2, axis=-1)
    c = u * jax.nn.sigmoid(gate)
    c = lax.conv_general_dilated(c, dw[:, None, :].astype(c.dtype), window_strides=(1,),
                                 padding=[(CONV_KERNEL - 1, 0)],
                                 dimension_numbers=('NWC', 'WIO', 'NWC'),
                                 feature_group_count=CONV_WIDTH) + dw_b
    c = jax.nn.silu(layer_norm(c, ln_w, ln_b))
    return c @ w_o

def first_inputs(seed: int = 0) -> dict:
    key = jax.random.key(seed)
    ks = iter(jax.random.split(key, 48))

    def nrm(shape, scale):
        return jax.random.normal(next(ks), shape, jnp.float32) * scale

    def unif(shape, lo, hi):
        return jax.random.uniform(next(ks), shape, jnp.float32, lo, hi)

    L, D, RW, CW = DEPTH, D_MODEL, RWKV_WIDTH, CONV_WIDTH
    Lv = DEPTH - 1
    return {
        'x': nrm((BATCH, SEQ, D), 1.0),
        'pre_mix_norm': 1.0 + nrm((L, D), 0.05),
        'post_mix_norm': 1.0 + nrm((L, D), 0.05),
        'pre_ffn_norm': 1.0 + nrm((L, D), 0.05),
        'post_ffn_norm': 1.0 + nrm((L, D), 0.05),
        'w_in': nrm((L, D, N_IN_COLS), D ** -0.5),
        'mu_rkv': unif((L, 3, RW), 0.0, 1.0),
        'mu_wag': unif((L, 3, D), 0.0, 1.0),
        'decay_w0': unif((L, RW), -6.0, -1.0),
        'decay_w1': nrm((L, D, DECAY_LORA), D ** -0.5),
        'decay_w2': nrm((L, DECAY_LORA, RW), 0.5 * DECAY_LORA ** -0.5),
        'a_0': nrm((L, RW), 0.5),
        'a_1': nrm((L, D, A_LORA), D ** -0.5),
        'a_2': nrm((L, A_LORA, RW), 0.5 * A_LORA ** -0.5),
        'g_1': nrm((L, D, G_LORA), D ** -0.5),
        'g_2': nrm((L, G_LORA, RW), G_LORA ** -0.5),
        'vres_mu': unif((Lv, D), 0.0, 1.0),
        'vres_0': nrm((Lv, RW), 0.5),
        'vres_1': nrm((Lv, D, V_LORA), D ** -0.5),
        'vres_2': nrm((Lv, V_LORA, RW), 0.5 * V_LORA ** -0.5),
        'k_k': 0.85 + nrm((L, RW), 0.05),
        'k_a': 1.0 + nrm((L, RW), 0.05),
        'r_k': nrm((L, RWKV_HEADS, RWKV_HEAD_DIM), 0.1),
        'gn_w': 1.0 + nrm((L, RW), 0.05),
        'gn_b': nrm((L, RW), 0.01),
        'w_rwkv_out': nrm((L, RW, D), RW ** -0.5),
        'conv_dw': nrm((L, CONV_KERNEL, CW), CONV_KERNEL ** -0.5),
        'conv_b': nrm((L, CW), 0.01),
        'conv_ln_w': 1.0 + nrm((L, CW), 0.05),
        'conv_ln_b': nrm((L, CW), 0.01),
        'w_conv_out': nrm((L, CW, D), CW ** -0.5),
        'w_out': nrm((L, D, D), D ** -0.5),
        'ffn_w_gate': nrm((L, D, D_FF), D ** -0.5),
        'ffn_w_up': nrm((L, D, D_FF), D ** -0.5),
        'ffn_w_down': nrm((L, D_FF, D), D_FF ** -0.5),
    }

def first_block(x, pre_mix_norm, post_mix_norm, pre_ffn_norm, post_ffn_norm, w_in, mu_rkv, mu_wag,
              decay_w0, decay_w1, decay_w2, a_0, a_1, a_2, g_1, g_2, vres_mu, vres_0, vres_1, vres_2,
              k_k, k_a, r_k, gn_w, gn_b, w_rwkv_out, conv_dw, conv_b, conv_ln_w, conv_ln_b, w_conv_out,
              w_out, ffn_w_gate, ffn_w_up, ffn_w_down):
    splits = [RWKV_WIDTH, 2 * RWKV_WIDTH, 3 * RWKV_WIDTH,
              3 * RWKV_WIDTH + 2 * CONV_WIDTH, 3 * RWKV_WIDTH + 2 * CONV_WIDTH + D_MODEL]
    v_first = None
    for i in range(DEPTH):
        h = rms_norm(x, pre_mix_norm[i])
        proj = h @ w_in[i]
        p_r, p_k, p_v, p_c, z_rwkv, z_conv = jnp.split(proj, splits, axis=-1)
        vres = None if i == 0 else (vres_mu[i - 1], vres_0[i - 1], vres_1[i - 1], vres_2[i - 1])
        y_rwkv, v_first = rwkv7_time_mix(
            h, p_r, p_k, p_v, v_first, vres, mu_rkv[i], mu_wag[i],
            decay_w0[i], decay_w1[i], decay_w2[i], a_0[i], a_1[i], a_2[i], g_1[i], g_2[i],
            k_k[i], k_a[i], r_k[i], gn_w[i], gn_b[i], w_rwkv_out[i])
        y_conv = conformer_conv(p_c, conv_dw[i], conv_b[i], conv_ln_w[i], conv_ln_b[i], w_conv_out[i])
        merged = jax.nn.sigmoid(z_rwkv) * y_rwkv + jax.nn.sigmoid(z_conv) * y_conv
        x = x + rms_norm(merged @ w_out[i], post_mix_norm[i])
        h = rms_norm(x, pre_ffn_norm[i])
        f = (jax.nn.silu(h @ ffn_w_gate[i]) * (h @ ffn_w_up[i])) @ ffn_w_down[i]
        x = x + rms_norm(f, post_ffn_norm[i])
    return x


DEPTH_2 = 2

N_MIXERS = 2
N_SSD = (DEPTH_2 + 1) // 2
N_FOX = DEPTH_2 // 2
EPS = 1e-6

SSD_EXPAND = 2
SSD_D_INNER = SSD_EXPAND * D_MODEL
SSD_HEAD_DIM = 64
SSD_HEADS = SSD_D_INNER // SSD_HEAD_DIM
SSD_GROUPS = 4
SSD_HPG = SSD_HEADS // SSD_GROUPS
SSD_STATE = 128
SSD_CONV = 4
SSD_CHUNK = 128
SSD_CONV_DIM = SSD_D_INNER + 2 * SSD_GROUPS * SSD_STATE
SSD_IN_DIM = SSD_D_INNER + SSD_CONV_DIM + SSD_HEADS

FOX_HEAD_DIM = 64
FOX_HEADS = D_MODEL // FOX_HEAD_DIM
FOX_D = FOX_HEADS * FOX_HEAD_DIM
FOX_IN_DIM = 4 * FOX_D + FOX_HEADS
Q_BLOCK = 128

D_FF_2 = 2816
FFN_CONV = 3


def rmsnorm(x, g):
    xf = x.astype(jnp.float32)
    y = xf * lax.rsqrt(jnp.mean(xf * xf, axis=-1, keepdims=True) + EPS)
    return (y * g.astype(jnp.float32)).astype(x.dtype)

def causal_dwconv(x, w, b):
    k_w, c = w.shape
    y = lax.conv_general_dilated(x, w[:, None, :].astype(x.dtype), window_strides=(1,),
                                 padding=[(k_w - 1, 0)],
                                 dimension_numbers=('NWC', 'WIO', 'NWC'),
                                 feature_group_count=c)
    return y + b.astype(x.dtype)

def ssd_chunked(xs, dt, a, bm, cm):
    bsz, s_len = xs.shape[0], xs.shape[1]
    nc, l_c = s_len // SSD_CHUNK, SSD_CHUNK
    x = xs.reshape(bsz, nc, l_c, SSD_GROUPS, SSD_HPG, SSD_HEAD_DIM)
    dtc = dt.reshape(bsz, nc, l_c, SSD_GROUPS, SSD_HPG)
    bc = bm.reshape(bsz, nc, l_c, SSD_GROUPS, SSD_STATE)
    cc = cm.reshape(bsz, nc, l_c, SSD_GROUPS, SSD_STATE)
    da = jnp.moveaxis(dtc * a.reshape(SSD_GROUPS, SSD_HPG), 2, -1)
    a_cs = jnp.cumsum(da, axis=-1)
    xdt = x * dtc[..., None]
    causal = jnp.tril(jnp.ones((l_c, l_c), dtype=bool))
    decay = jnp.exp(jnp.where(causal, a_cs[..., :, None] - a_cs[..., None, :], -jnp.inf))
    cb = jnp.einsum('bclgn,bcsgn->bcgls', cc, bc)
    y_diag = jnp.einsum('bcgrls,bcsgrp->bclgrp', cb[:, :, :, None] * decay, xdt)
    decay_states = jnp.exp(a_cs[..., -1:] - a_cs)
    states = jnp.einsum('bclgn,bcgrl,bclgrp->bcgrpn', bc, decay_states, xdt).astype(jnp.float32)
    chunk_decay = jnp.exp(a_cs[..., -1])

    def step(h, inp):
        st, dec = inp
        return h * dec[..., None, None] + st, h

    h0 = jnp.zeros((bsz, SSD_GROUPS, SSD_HPG, SSD_HEAD_DIM, SSD_STATE), jnp.float32)
    _, prev = lax.scan(step, h0, (jnp.moveaxis(states, 1, 0), jnp.moveaxis(chunk_decay, 1, 0)))
    prev = jnp.moveaxis(prev, 0, 1)
    y_off = jnp.einsum('bclgn,bcgrpn,bcgrl->bclgrp', cc, prev, jnp.exp(a_cs))
    return (y_diag + y_off).reshape(bsz, s_len, SSD_HEADS, SSD_HEAD_DIM).astype(xs.dtype)

def mamba2_mixer(h, w_in, conv_w, conv_b, dt_bias, a_log, d_skip, norm_g, w_out):
    bsz, s_len, _ = h.shape
    proj = h @ w_in
    z = proj[..., :SSD_D_INNER]
    xbc = proj[..., SSD_D_INNER:SSD_D_INNER + SSD_CONV_DIM]
    dt_raw = proj[..., SSD_D_INNER + SSD_CONV_DIM:]
    xbc = jax.nn.silu(causal_dwconv(xbc, conv_w, conv_b))
    gn = SSD_GROUPS * SSD_STATE
    xs = xbc[..., :SSD_D_INNER].reshape(bsz, s_len, SSD_HEADS, SSD_HEAD_DIM)
    bm = xbc[..., SSD_D_INNER:SSD_D_INNER + gn].reshape(bsz, s_len, SSD_GROUPS, SSD_STATE)
    cm = xbc[..., SSD_D_INNER + gn:].reshape(bsz, s_len, SSD_GROUPS, SSD_STATE)
    dt = jax.nn.softplus((dt_raw + dt_bias).astype(jnp.float32))
    a = -jnp.exp(a_log.astype(jnp.float32))
    y = ssd_chunked(xs, dt, a, bm, cm) + xs * d_skip[:, None]
    y = y.reshape(bsz, s_len, SSD_D_INNER)
    yz = (y * jax.nn.silu(z)).astype(jnp.float32).reshape(bsz, s_len, SSD_GROUPS, SSD_D_INNER // SSD_GROUPS)
    yz = yz * lax.rsqrt(jnp.mean(yz * yz, axis=-1, keepdims=True) + EPS)
    y = (yz.reshape(bsz, s_len, SSD_D_INNER) * norm_g.astype(jnp.float32)).astype(h.dtype)
    return y @ w_out

def fox_attention(h, w_in, b_f, q_norm_g, k_norm_g, w_out):
    bsz, s_len, _ = h.shape
    proj = h @ w_in
    q = rmsnorm(proj[..., :FOX_D].reshape(bsz, s_len, FOX_HEADS, FOX_HEAD_DIM), q_norm_g)
    k = rmsnorm(proj[..., FOX_D:2 * FOX_D].reshape(bsz, s_len, FOX_HEADS, FOX_HEAD_DIM), k_norm_g)
    v = proj[..., 2 * FOX_D:3 * FOX_D].reshape(bsz, s_len, FOX_HEADS, FOX_HEAD_DIM)
    gate = proj[..., 3 * FOX_D:4 * FOX_D]
    log_f = jax.nn.log_sigmoid((proj[..., 4 * FOX_D:] + b_f).astype(jnp.float32))
    cum = jnp.transpose(jnp.cumsum(log_f, axis=1), (0, 2, 1))
    q, k, v = (jnp.transpose(t, (0, 2, 1, 3)) for t in (q, k, v))
    scale = FOX_HEAD_DIM ** -0.5
    outs = []
    for i in range(s_len // Q_BLOCK):
        qs, qe = i * Q_BLOCK, (i + 1) * Q_BLOCK
        sc = jnp.einsum('bhqd,bhkd->bhqk', q[:, :, qs:qe], k[:, :, :qe]).astype(jnp.float32) * scale
        sc = sc + cum[:, :, qs:qe, None] - cum[:, :, None, :qe]
        mask = (qs + jnp.arange(Q_BLOCK))[:, None] >= jnp.arange(qe)[None, :]
        p = jax.nn.softmax(jnp.where(mask, sc, -jnp.inf), axis=-1)
        outs.append(jnp.einsum('bhqk,bhkd->bhqd', p.astype(v.dtype), v[:, :, :qe]))
    o = jnp.transpose(jnp.concatenate(outs, axis=2), (0, 2, 1, 3)).reshape(bsz, s_len, FOX_D)
    return (o * jax.nn.sigmoid(gate)) @ w_out

def conv_glu_ffn(h, w_up, conv_w, conv_b, w_down):
    u = h @ w_up
    gate = causal_dwconv(u[..., :D_FF_2], conv_w, conv_b)
    return (jax.nn.silu(gate) * u[..., D_FF_2:]) @ w_down

def second_inputs(seed: int = 0) -> dict:
    key = jax.random.key(seed)
    ks = jax.random.split(key, 24)
    f32 = jnp.float32

    def nrm(k, shape, scale):
        return jax.random.normal(k, shape, f32) * scale

    res_scale = (2 * DEPTH_2) ** -0.5
    dt_init = jnp.exp(jax.random.uniform(ks[4], (N_SSD, SSD_HEADS), f32, math.log(1e-3), math.log(1e-1)))
    return {
        'x': nrm(ks[0], (BATCH, SEQ, D_MODEL), 1.0),
        'mix_norm_g': 1.0 + nrm(ks[1], (DEPTH_2, D_MODEL), 0.02),
        'ffn_norm_g': 1.0 + nrm(ks[2], (DEPTH_2, D_MODEL), 0.02),
        'ssd_w_in': nrm(ks[3], (N_SSD, D_MODEL, SSD_IN_DIM), D_MODEL ** -0.5),
        'ssd_conv_w': nrm(ks[5], (N_SSD, SSD_CONV, SSD_CONV_DIM), SSD_CONV ** -0.5),
        'ssd_conv_b': nrm(ks[6], (N_SSD, SSD_CONV_DIM), 0.02),
        'ssd_dt_bias': dt_init + jnp.log(-jnp.expm1(-dt_init)),
        'ssd_a_log': jnp.log(jax.random.uniform(ks[7], (N_SSD, SSD_HEADS), f32, 1.0, 16.0)),
        'ssd_d': 1.0 + nrm(ks[8], (N_SSD, SSD_HEADS), 0.1),
        'ssd_norm_g': 1.0 + nrm(ks[9], (N_SSD, SSD_D_INNER), 0.02),
        'ssd_w_out': nrm(ks[10], (N_SSD, SSD_D_INNER, D_MODEL), SSD_D_INNER ** -0.5 * res_scale),
        'fox_w_in': nrm(ks[11], (N_FOX, D_MODEL, FOX_IN_DIM), D_MODEL ** -0.5),
        'fox_b_f': jax.random.uniform(ks[12], (N_FOX, FOX_HEADS), f32, 2.0, 6.0),
        'fox_q_norm_g': 1.0 + nrm(ks[13], (N_FOX, FOX_HEAD_DIM), 0.02),
        'fox_k_norm_g': 1.0 + nrm(ks[14], (N_FOX, FOX_HEAD_DIM), 0.02),
        'fox_w_out': nrm(ks[15], (N_FOX, FOX_D, D_MODEL), FOX_D ** -0.5 * res_scale),
        'ffn_w_up': nrm(ks[16], (DEPTH_2, D_MODEL, 2 * D_FF_2), D_MODEL ** -0.5),
        'ffn_conv_w': nrm(ks[17], (DEPTH_2, FFN_CONV, D_FF_2), FFN_CONV ** -0.5),
        'ffn_conv_b': nrm(ks[18], (DEPTH_2, D_FF_2), 0.02),
        'ffn_w_down': nrm(ks[19], (DEPTH_2, D_FF_2, D_MODEL), D_FF_2 ** -0.5 * res_scale),
        'final_norm_g': 1.0 + nrm(ks[20], (D_MODEL,), 0.02),
    }

def second_block(x, mix_norm_g, ffn_norm_g,
              ssd_w_in, ssd_conv_w, ssd_conv_b, ssd_dt_bias, ssd_a_log, ssd_d, ssd_norm_g, ssd_w_out,
              fox_w_in, fox_b_f, fox_q_norm_g, fox_k_norm_g, fox_w_out,
              ffn_w_up, ffn_conv_w, ffn_conv_b, ffn_w_down, final_norm_g):
    h = x
    for i in range(DEPTH_2):
        hn = rmsnorm(h, mix_norm_g[i])
        j = i // N_MIXERS
        if i % N_MIXERS == 0:
            h = h + mamba2_mixer(hn, ssd_w_in[j], ssd_conv_w[j], ssd_conv_b[j], ssd_dt_bias[j],
                                 ssd_a_log[j], ssd_d[j], ssd_norm_g[j], ssd_w_out[j])
        else:
            h = h + fox_attention(hn, fox_w_in[j], fox_b_f[j], fox_q_norm_g[j], fox_k_norm_g[j], fox_w_out[j])
        h = h + conv_glu_ffn(rmsnorm(h, ffn_norm_g[i]), ffn_w_up[i], ffn_conv_w[i], ffn_conv_b[i], ffn_w_down[i])
    return rmsnorm(h, final_norm_g)


def setup_inputs(seed=0):
    out = dict(first_inputs(seed))
    for name, value in second_inputs(seed + 1).items():
        if name != "x":
            out[name + "_2"] = value
    return out


def reference(
    x, pre_mix_norm, post_mix_norm, pre_ffn_norm, post_ffn_norm, w_in, mu_rkv, mu_wag, decay_w0,
    decay_w1, decay_w2, a_0, a_1, a_2, g_1, g_2, vres_mu, vres_0, vres_1, vres_2, k_k, k_a, r_k,
    gn_w, gn_b, w_rwkv_out, conv_dw, conv_b, conv_ln_w, conv_ln_b, w_conv_out, w_out,
    ffn_w_gate, ffn_w_up, ffn_w_down, mix_norm_g_2, ffn_norm_g_2, ssd_w_in_2, ssd_conv_w_2,
    ssd_conv_b_2, ssd_dt_bias_2, ssd_a_log_2, ssd_d_2, ssd_norm_g_2, ssd_w_out_2, fox_w_in_2,
    fox_b_f_2, fox_q_norm_g_2, fox_k_norm_g_2, fox_w_out_2, ffn_w_up_2, ffn_conv_w_2,
    ffn_conv_b_2, ffn_w_down_2, final_norm_g_2,
):
    x = first_block(
        x, pre_mix_norm, post_mix_norm, pre_ffn_norm, post_ffn_norm, w_in, mu_rkv, mu_wag,
        decay_w0, decay_w1, decay_w2, a_0, a_1, a_2, g_1, g_2, vres_mu, vres_0, vres_1, vres_2,
        k_k, k_a, r_k, gn_w, gn_b, w_rwkv_out, conv_dw, conv_b, conv_ln_w, conv_ln_b,
        w_conv_out, w_out, ffn_w_gate, ffn_w_up, ffn_w_down,
    )
    return second_block(
        x, mix_norm_g_2, ffn_norm_g_2, ssd_w_in_2, ssd_conv_w_2, ssd_conv_b_2, ssd_dt_bias_2,
        ssd_a_log_2, ssd_d_2, ssd_norm_g_2, ssd_w_out_2, fox_w_in_2, fox_b_f_2, fox_q_norm_g_2,
        fox_k_norm_g_2, fox_w_out_2, ffn_w_up_2, ffn_conv_w_2, ffn_conv_b_2, ffn_w_down_2,
        final_norm_g_2,
    )


_drawn_inputs = setup_inputs


def setup_inputs(seed=0):
    import zlib

    import numpy as np

    out = dict(_drawn_inputs(seed))
    spreads = {}
    factors = {'decay_w1': 4.08,
     'decay_w2': 4.126,
     'k_k': 2.744,
     'gn_b': 8.0,
     'conv_b': 4.208,
     'conv_ln_b': 8.0,
     'mix_norm_g_2': 6.533,
     'ffn_norm_g_2': 8.0,
     'ssd_conv_b_2': 7.052,
     'ssd_d_2': 145.309,
     'ssd_norm_g_2': 8.0,
     'fox_b_f_2': 12.407,
     'fox_q_norm_g_2': 88.845,
     'fox_k_norm_g_2': 34.262,
     'ffn_conv_b_2': 8.0,
     'final_norm_g_2': 22.673}
    for name, (base, spread) in spreads.items():
        noise = np.random.default_rng([zlib.crc32(name.encode()), seed]).standard_normal(out[name].shape)
        drawn = base * np.exp(spread * noise) if base else spread * noise
        out[name] = __import__('jax').numpy.asarray(drawn.astype(out[name].dtype))
    for name, factor in factors.items():
        out[name] = (out[name] * factor).astype(out[name].dtype)
    return out
```

```python
from contextlib import ExitStack

import concourse.bass as bass
from concourse import mybir

F32 = mybir.dt.float32
F32R = mybir.dt.float32r
ALU = mybir.AluOpType
ACT = mybir.ActivationFunctionType
AX_X = mybir.AxisListType.X

P = 128
T = 256
D = 1024
KC = D // P
FF = 2816
FC = FF // P
UNIT_COLS = 512
M_PER_UNIT = UNIT_COLS // P
LOOKAHEAD = 3
EXP_MINUS_HALF = 0.6065306597126334
RMS_EPS, LN_EPS, GN_EPS = 1e-6, 1e-5, 64e-5

RWKV_HEADS, HEAD = 16, 64
CHUNK = 32
NCHUNK = T // CHUNK
CONV_TAPS = 31
SSD_INNER, SSD_HEADS, SSD_GROUPS, SSD_TAPS = 2048, 32, 4, 4
SSD_Z, SSD_XBC = SSD_INNER // P, (SSD_INNER + 2 * SSD_GROUPS * P) // P
FOX_HEADS = 16
GLU_TAPS = 3
MASKED = -1e30


class Layer:

    def __init__(self, name, sources, nkc, k_split=1, dmas=1):
        self.name, self.sources, self.nkc, self.k_split, self.dmas = name, sources, nkc, k_split, dmas

    def __len__(self):
        return len(self.nkc)

    def first_k(self, u):
        g = u % self.k_split
        return sum(self.nkc[:g])


def params_of(a):
    out = []
    for name in ("pre_mix_norm", "post_mix_norm", "pre_ffn_norm", "post_ffn_norm", "mu_rkv", "mu_wag", "decay_w0",
                 "a_0", "k_k", "k_a", "r_k", "gn_w", "gn_b", "conv_dw", "conv_b", "conv_ln_w", "conv_ln_b",
                 "mix_norm_g_2", "ffn_norm_g_2", "ssd_conv_w_2", "ssd_conv_b_2", "ssd_norm_g_2",
                 "ffn_conv_w_2", "ffn_conv_b_2", "final_norm_g_2"):
        ap = a[name]
        names = " ".join(f"d{i}" for i in range(len(ap.shape)))
        flat = ap.rearrange(f"{names} -> ({names})")
        n = flat.shape[0] // P
        out.append((name, n, flat.rearrange("(n p) -> n p", p=P)))
    return out


def build(nc, a, out):
    ctx = ExitStack()
    with ctx:
        sems = {}

        def sem(name):
            if name not in sems:
                sems[name] = ctx.enter_context(nc.semaphore(name))
            return sems[name]

        def sb(name, shape, dt=F32):
            return ctx.enter_context(nc.sbuf_tensor(name, shape, dt))

        raw = [sb(f"raw{i}", [P, KC, UNIT_COLS]) for i in range(2)]
        w_hi = [sb(f"w_hi{i}", [P, KC, P], F32R) for i in range(M_PER_UNIT)]
        w_lo = [sb(f"w_lo{i}", [P, KC, P], F32R) for i in range(M_PER_UNIT)]
        x_res = sb("x_res", [P, KC, T])
        x_hi = sb("x_hi", [P, KC, T], F32R)
        x_lo = sb("x_lo", [P, KC, T], F32R)
        sub_base = nc.sbuf_base
        sub = sb("sub", [P, 12, T])
        arena_base = nc.sbuf_base
        pj = sb("pj", [P, 96, T])
        ident = sb("ident", [P, P])
        ones = sb("ones", [P, P])
        blk = sb("blk", [P, P])
        tri = sb("tri", [P, P])
        scan_mask = sb("scan_mask", [P, T])
        g_mask = sb("g_mask", [P, 2 * CHUNK])
        head_sel = sb("head_sel", [P, KC, RWKV_HEADS])
        eps = sb("eps", [P, 3])
        rs = sb("rs", [P, T])
        rstd = sb("rstd", [P, T])
        small = sb("small", [SSD_HEADS, T])
        bonus = small[0:RWKV_HEADS, :]
        chunk_decay = sb("chunk_decay", [P, KC, NCHUNK])
        heads_col = sb("heads_col", [SSD_HEADS, 4])
        fox_g = sb("fox_g", [P, 4])
        d_skip = sb("d_skip", [P, SSD_Z])

        par_rows = params_of(a)
        col, n_rows = {}, 0
        for name, n, _ in par_rows:
            col[name] = n_rows
            n_rows += n
        par_tiles = -(-n_rows // P)
        par = sb("par", [P, n_rows])

        def slot(i):
            return pj[:, 8 * i:8 * i + 8, :]

        R, K, V, U, GATE, BK, KK, A, TMP, W, G = 0, 1, 2, 3, 4, 5, 7, 8, 9, 10, 11
        ZR, ZC, OUT1 = K, A, R
        x_tok = pj[:, 40:48, :].rearrange("p a b -> p (a b)").rearrange("p (c d) -> p c d", c=2)
        par_tok = pj[:, 48:52, :].rearrange("p a b -> p (a b)")[:, 0:par_tiles * P].rearrange("p (t c) -> p t c", c=P)
        tmp2 = sub[:, 0:8, :]
        lora_w, lora_a, lora_g = sub[0:64, 8, :], sub[0:64, 9, :], sub[:, 10, :]
        bk = pj[:, 40:56, :].rearrange("p a b -> p (a b)").rearrange("p (k c j s) -> p k c j s", k=KC, c=NCHUNK, j=2)
        region = pj[:, 72:88, :].rearrange("p a b -> p (a b)")
        lab_t = region[0:CHUNK, :].rearrange("s (y t) -> s y t", t=CHUNK)
        g_buf = [region[64:128, 1024 * q:1024 * q + 1024].rearrange("p (h n) -> p h n", h=RWKV_HEADS) for q in range(2)]
        uv = [region[64:128, 2048 + 1024 * q:3072 + 1024 * q] for q in range(2)]
        flat_sub = sub[:, :, :].rearrange("p a b -> p (a b)")
        lt = flat_sub[:, 0:1024].rearrange("p (s t) -> p s t", t=CHUNK)
        mt = flat_sub[:, 1024:2048].rearrange("p (s t) -> p s t", t=CHUNK)
        prod = flat_sub[:, 2048:3072].rearrange("p (s t) -> p s t", t=CHUNK)
        bk_t = [flat_sub[64:128, 1024 * q:1024 * q + 1024] for q in range(2)]
        x_buf = flat_sub[0:CHUNK, 0:1024]
        state = flat_sub[:, 2048:3072].rearrange("p (m v) -> p m v", m=KC)
        act_hi = nc.alloc_sbuf_tensor_at("act_hi", [P, FC, T], F32R, offset=arena_base)
        act_lo = nc.alloc_sbuf_tensor_at("act_lo", [P, FC, T], F32R, offset=arena_base + FC * T * 4)
        OUT_FFN = 8
        g_tile = [sub[:, i, :] for i in (0, 1)]
        s_tile = [sub[:, i, :] for i in (2, 3)]
        u_tile = [sub[:, i, :] for i in (4, 5)]
        a_tile = [sub[:, i, :] for i in (6, 7)]
        c_tile = [sub[:, i, :] for i in (8, 9)]
        z_t, xbc, y_ssd = pj[:, 0:16, :], pj[:, 16:40, :], pj[:, 40:56, :]
        x_gain = pj[:, 40:48, :]
        xdt = pj[:, 56:72, :].rearrange("p a b -> p (a b)").rearrange("p (c f) -> p c f", c=2)
        xdt_end = pj[:, 72:80, :].rearrange("p a b -> p (a b)")
        att = [pj[:, 80 + 2 * q:82 + 2 * q, :].rearrange("p a b -> p (a b)").rearrange("p (h l) -> p h l", l=P) for q in range(2)]
        cbm = pj[:, 84:88, :].rearrange("p a b -> p (a b)").rearrange("p (c g l) -> p c g l", c=2, g=SSD_GROUPS)
        st_ssd = pj[:, 88:96, :].rearrange("p a b -> p (a b)")
        conv_in = [sub[:, i, :] for i in range(4)]
        conv_sig = [sub[:, 4 + i, :] for i in range(4)]
        dt_z, dt_e, dt, acs = (sub[0:SSD_HEADS, i, :] for i in (8, 9, 10, 11))
        tok_heads = sb("tok_heads", [P, 5, SSD_HEADS])
        da_end, da_exp = small[:, 0:P], small[:, P:T]
        eab = sub[:, 0:8, :].rearrange("p a b -> p (a b)").rearrange("p (m l) -> p m l", l=P)
        b_tok = x_gain[:, 0:2, :].rearrange("p a b -> p (a b)").rearrange("p (g n) -> p g n", g=SSD_GROUPS)
        yz_hi = nc.alloc_sbuf_tensor_at("yz_hi", [P, SSD_Z, T], F32R, offset=arena_base + 56 * T * 4)
        yz_lo = nc.alloc_sbuf_tensor_at("yz_lo", [P, SSD_Z, T], F32R, offset=arena_base + 16 * T * 4)
        q_t, k_t, v_t, gate_t = (pj[:, 8 * i:8 * i + 8, :] for i in range(4))
        fox_tmp = pj[:, 32:40, :]
        v_tok = pj[:, 48:56, :].rearrange("p a b -> p (a b)").rearrange("p (c f) -> p c f", c=2)
        NS = 3
        sc = [pj[:, 56 + 2 * i:58 + 2 * i, :] for i in range(NS)]
        pt = [pj[:, 64 + 2 * i:66 + 2 * i, :].rearrange("p a b -> p (a b)") for i in range(NS)]
        o_fox = pj[:, 72:80, :]
        fox_stat = pj[:, 80, :].rearrange("p (s h) -> p s h", h=FOX_HEADS)
        fox_mask = pj[:, 81, :]
        pj4 = pj[:, :, :].rearrange("p (s k) t -> p s k t", k=KC)
        y_tok = pj[:, 0:8, :].rearrange("p a b -> p (a b)").rearrange("p (c d) -> p c d", c=2)
        cum_neg = dt_z

        pb = [ctx.enter_context(nc.psum_tensor(f"pb{i}", [P, 512], F32)) for i in range(8)]
        sub_in = nc.dram_tensor("sub_in", [CHUNK, P, CHUNK], F32, kind="Internal").ap()
        sub_out = nc.dram_tensor("sub_out", [P, CHUNK, CHUNK], F32, kind="Internal").ap()

        def cols(ap, first, n=UNIT_COLS):
            v = ap.rearrange("(k p) n -> p k n", p=P)
            return lambda u: [(slice(0, n), v[:, :, bass.ds(first + n * u, n)])]

        def gate_up(g, up):
            h = UNIT_COLS // 2
            gv, uv_ = g.rearrange("(k p) n -> p k n", p=P), up.rearrange("(k p) n -> p k n", p=P)
            return lambda u: [(slice(0, h), gv[:, :, bass.ds(h * u, h)]), (slice(h, 2 * h), uv_[:, :, bass.ds(h * u, h)])]

        def k_split(ap, nkc, parts):
            v = ap.rearrange("(k p) n -> p k n", p=P)

            def source(u):
                k0 = sum(nkc[:u % parts])
                n0 = UNIT_COLS * (u // parts)
                return [(slice(0, UNIT_COLS), v[:, k0:k0 + nkc[u % parts], n0:n0 + UNIT_COLS])]
            return source

        w_in = a["w_in"][0]
        down_kc = [8, 7, 7]
        up2, down2 = a["ffn_w_up_2"], a["ffn_w_down_2"]
        L = {}
        order = []

        def layer(name, sources, nkc, **kw):
            L[name] = Layer(name, sources, nkc, **kw)
            order.append(L[name])

        def lora_in(u):
            return [(slice(0, 64), a["decay_w1"][0].rearrange("(k p) n -> p k n", p=P)),
                    (slice(64, 128), a["a_1"][0].rearrange("(k p) n -> p k n", p=P)),
                    (slice(128, 256), a["g_1"][0].rearrange("(k p) n -> p k n", p=P))]

        def narrow(ap, first, n):
            return lambda u: [(slice(0, n), ap.rearrange("(k p) n -> p k n", p=P)[:, :, first:first + n])]

        layer("rkv", cols(w_in, 0), [KC] * 6)
        layer("lora_in", lora_in, [KC], dmas=3)
        layer("lora_out", None, [KC], dmas=3)
        layer("ug", cols(w_in, 3 * D), [KC] * 4)
        layer("z", cols(w_in, 5 * D), [KC] * 4)
        layer("conv_out", cols(a["w_conv_out"][0], 0), [KC] * 2)
        layer("rwkv_out", cols(a["w_rwkv_out"][0], 0), [KC] * 2)
        layer("w_out", cols(a["w_out"][0], 0), [KC] * 2)
        layer("up0", gate_up(a["ffn_w_gate"][0], a["ffn_w_up"][0]), [KC] * 11, dmas=2)
        layer("down0", k_split(a["ffn_w_down"][0], down_kc, 3), down_kc * 2, k_split=3)
        layer("ssd_z", cols(a["ssd_w_in_2"][0], 0), [KC] * 4)
        layer("ssd_xbc", cols(a["ssd_w_in_2"][0], SSD_INNER), [KC] * 6)
        layer("ssd_dt", narrow(a["ssd_w_in_2"][0], 5120, SSD_HEADS), [KC])
        layer("ssd_out", k_split(a["ssd_w_out_2"][0], [8, 8], 2), [8, 8] * 2, k_split=2)
        layer("up1", gate_up(up2[0][:, 0:FF], up2[0][:, FF:2 * FF]), [KC] * 11, dmas=2)
        layer("down1", k_split(down2[0], down_kc, 3), down_kc * 2, k_split=3)
        layer("fox_in", cols(a["fox_w_in_2"][0], 0), [KC] * 8)
        layer("fox_f", narrow(a["fox_w_in_2"][0], 4 * D, FOX_HEADS), [KC])
        layer("fox_out", cols(a["fox_w_out_2"][0], 0), [KC] * 2)
        layer("up2", gate_up(up2[1][:, 0:FF], up2[1][:, FF:2 * FF]), [KC] * 11, dmas=2)
        layer("down2", k_split(down2[1], down_kc, 3), down_kc * 2, k_split=3)
        special = {"lora_in": ("lora1_done", 3), "lora_out": ("lora2_done", 12), "ssd_dt": ("dt_done", 1), "fox_f": ("f_done", 1)}
        landed = [0, 0]
        unit, item, evac = 0, 0, 0
        occupant = [None, None]
        for ly in order:
            ly.u0, ly.item0, ly.evac0 = unit, item, evac
            ly.landed, ly.free = [], []
            for u in range(len(ly)):
                s = unit % 2
                landed[s] += 16 * ly.dmas
                ly.landed.append(landed[s])
                ly.free.append(occupant[s])
                unit += 1
                if ly.name in special:
                    occupant[s] = special[ly.name]
                else:
                    item += M_PER_UNIT
                    occupant[s] = ("w_lo_ready", item)
                    if u % ly.k_split == ly.k_split - 1:
                        evac += M_PER_UNIT
            ly.item1, ly.evac1 = item, evac

        def units(eng, ly, body):
            n = len(ly)
            pairs = (n - 2) // 2 if n >= 6 and ly.k_split == 1 else 0
            if pairs:
                with eng.Fori(0, pairs) as i:
                    for p in range(2):
                        body(2 * i + p, p, False)
            for u in range(2 * pairs, n):
                body(u, u % 2, u == n - 1)

        def nth(ly, u, p, table):
            return table[u] if isinstance(u, int) else table[p] + (u - p) * ((table[p + 2] - table[p]) // 2)

        BANKS = M_PER_UNIT

        def pe_layer(pe, ly, hi, lo, in_ready, in_base):
            def body(u, p, last):
                part = u % ly.k_split if isinstance(u, int) else 0
                k0, nk = (ly.first_k(u), ly.nkc[u]) if isinstance(u, int) else (0, KC)
                first, final = part == 0, part == ly.k_split - 1
                group = u // ly.k_split if isinstance(u, int) else u
                for m in range(M_PER_UNIT):
                    pe.wait_ge(sem("w_lo_ready"), ly.item0 + M_PER_UNIT * u + m + 1)
                    if first:
                        pe.wait_ge(sem("evac_done"), ly.evac0 + M_PER_UNIT * group + m + 1)
                    if isinstance(u, int) and u < ly.k_split and m == 0:
                        pe.wait_ge(sem(in_ready), in_base + k0 + nk)
                    for k in range(nk):
                        o = pb[m][:, 0:T]
                        pe.matmul(o, w_hi[m][:, k, :], hi[:, k0 + k, :], start=first and k == 0, stop=False)
                        pe.matmul(o, w_hi[m][:, k, :], lo[:, k0 + k, :], start=False, stop=False)
                        mm = pe.matmul(o, w_lo[m][:, k, :], hi[:, k0 + k, :], start=False, stop=final and k == nk - 1)
                    mm.then_inc(sem("block_done"), 1)
            pe.wait_ge(sem(in_ready), in_base + ly.nkc[0])
            units(pe, ly, body)

        def act_head(act, ly, u, p, m):
            s = (ly.u0 + p) % 2
            nk = ly.nkc[u] if isinstance(u, int) else KC
            if m == 0:
                act.wait_ge(sem(f"landed{s}"), nth(ly, u, p, ly.landed))
            act.wait_ge(sem("block_done"), ly.item0 + M_PER_UNIT * u + m + 1)
            act.activation(w_hi[m][:, 0:nk, :], raw[s][:, 0:nk, m * P:(m + 1) * P], ACT.Copy).then_inc(sem("w_hi_ready"), 1)

        def dve_rest(dve, ly, u, p, m):
            s = (ly.u0 + p) % 2
            nk = ly.nkc[u] if isinstance(u, int) else KC
            dve.wait_ge(sem("w_hi_ready"), ly.item0 + M_PER_UNIT * u + m + 1)
            dve.tensor_tensor(w_lo[m][:, 0:nk, :], raw[s][:, 0:nk, m * P:(m + 1) * P], w_hi[m][:, 0:nk, :].bitcast(F32),
                              ALU.subtract).then_inc(sem("w_lo_ready"), 1)

        def ahead(split, eng, ly):
            for m in range(LOOKAHEAD):
                split(eng, ly, 0, 0, m)

        def split_next(split, eng, ly, u, p, m, last):
            if m + LOOKAHEAD < M_PER_UNIT:
                split(eng, ly, u, p, m + LOOKAHEAD)
            elif not last:
                split(eng, ly, u + 1, (p + 1) % 2, m + LOOKAHEAD - M_PER_UNIT)

        def act_layer(act, ly, hook=None):
            def body(u, p, last):
                for m in range(M_PER_UNIT):
                    split_next(act_head, act, ly, u, p, m, last)
                    if hook:
                        hook(u, m)
            units(act, ly, body)

        def dve_layer(dve, ly, out_block):
            def body(u, p, last):
                for m in range(M_PER_UNIT):
                    split_next(dve_rest, dve, ly, u, p, m, last)
                    if not isinstance(u, int) or u % ly.k_split == ly.k_split - 1:
                        dve.wait_ge(sem("block_done"), ly.item0 + M_PER_UNIT * u + m + 1 + BANKS)
                        out_block(u // ly.k_split if isinstance(u, int) else u, m)
            units(dve, ly, body)

        def par_col(name, i):
            c = col[name]
            return par[:, c + i:c + i + 1] if isinstance(i, int) else par[:, bass.ds(c + i, 1)]

        def tile(base, i):
            return pj[:, base + i, :]

        class Chain:

            def __init__(self, eng, name):
                self.eng, self.sem, self.n = eng, sem(name), 0

            def go(self, ins):
                ins.then_inc(self.sem, 1)
                self.n += 1

            def sync(self):
                self.eng.wait_ge(self.sem, self.n)

            def link(self, ins):
                self.go(ins)
                self.sync()

        X_BASE = {0: 0, 1: 4 * KC, 2: 5 * KC, 3: 6 * KC, 4: 7 * KC, "fox": 8 * KC, 5: 9 * KC}
        par_dmas = sum(1 + (col[n] + r - 1) // P - col[n] // P for n, r, _ in par_rows)
        NORMS = [("pre_mix_norm", 0), ("pre_ffn_norm", 0), ("mix_norm_g_2", 0), ("ffn_norm_g_2", 0),
                 ("mix_norm_g_2", KC), ("ffn_norm_g_2", KC)]
        block = ctx.enter_context(nc.Block())


        @block.sync
        def _(sp):
            sp.dma_start(x_tok, a["x"][0].rearrange("(c p) d -> p c d", p=P)).then_inc(sem("x_loaded"), 16)
            for ly in order:
                s0 = ly.u0 % 2
                if ly.name == "lora_out":
                    sp.wait_ge(sem(ly.free[0][0]), ly.free[0][1])
                    flat = raw[s0][:, :, :].rearrange("p k n -> p (k n)")
                    for i, (n, rows) in enumerate((("decay_w2", 64), ("a_2", 64), ("g_2", 128))):
                        sp.dma_start(flat[0:rows, D * i:D * i + D], a[n][0]).then_inc(sem(f"landed{s0}"), 16)
                    continue

                def body(u, p, last):
                    s = (ly.u0 + p) % 2
                    nk = KC
                    if isinstance(u, int):
                        nk = ly.nkc[u]
                        if ly.free[u]:
                            sp.wait_ge(sem(ly.free[u][0]), ly.free[u][1])
                    else:
                        sp.wait_ge(sem("w_lo_ready"), ly.item0 + M_PER_UNIT * (u - 1))
                    for c, src in ly.sources(u):
                        sp.dma_start(raw[s][:, 0:nk, c], src).then_inc(sem(f"landed{s}"), 16)
                if ly is order[0]:
                    for u in range(len(ly)):
                        body(u, u % 2, False)
                else:
                    units(sp, ly, body)
            for c in range(2):
                sp.wait_ge(sem("y_tok_ready"), 2 * (c + 1))
                sp.dma_start(out[0, c * P:(c + 1) * P, :], y_tok[:, c, :]).then_inc(sem("out_done"), 16)
            sp.wait_ge(sem("out_done"), 32)

        @block.gpsimd
        def _(pool):
            ch = Chain(pool, "pool_chain")
            go, sync, link = ch.go, ch.sync, ch.link

            go(pool.memset(ident[:, :], 0.0))
            go(pool.memset(tri[:, :], 1.0))
            go(pool.memset(blk[:, :], 0.0))
            go(pool.memset(scan_mask[:, :], 1.0))
            go(pool.memset(head_sel[:, :, :], 0.0))
            go(pool.memset(ones[:, :], 1.0))
            for i, e in enumerate((RMS_EPS, LN_EPS, GN_EPS)):
                go(pool.memset(eps[:, i:i + 1], e))
            sync()
            link(pool.affine_select(out=ident[:, :], in_=ident[:, :], compare_op=ALU.not_equal, fill=1.0, base=0,
                                  pattern=[[-1, P]], channel_multiplier=1))
            link(pool.affine_select(out=tri[:, :], in_=tri[:, :], compare_op=ALU.is_ge, fill=0.0, base=0,
                                  pattern=[[1, P]], channel_multiplier=-1))
            for h in range(2):
                link(pool.memset(blk[64 * h:64 * h + 64, 64 * h:64 * h + 64], 1.0))
                link(pool.affine_select(out=head_sel[64 * h:64 * h + 64, :, :], in_=head_sel[64 * h:64 * h + 64, :, :],
                                      compare_op=ALU.not_equal, fill=1.0, base=-h,
                                      pattern=[[-2, KC], [1, RWKV_HEADS]], channel_multiplier=0))
            link(pool.memset(scan_mask[:, :].rearrange("p (c s) -> p c s", s=CHUNK)[:, :, 0:1], 0.0))
            sync()
            for b in range(4):
                rows = slice(32 * b, 32 * b + 32)
                link(pool.tensor_copy(g_mask[rows, 0:CHUNK], tri[rows, rows]))
                link(pool.tensor_tensor(g_mask[rows, CHUNK:2 * CHUNK], tri[rows, rows], ident[rows, rows], ALU.subtract))
            sync()
            pool.nop().then_inc(sem("const_ready"), 1)

            pool.wait_ge(sem("lab_ready"), NCHUNK)
            pool.wait_ge(sem("bonus_ready"), 1)
            pool.dma_start(sub_in, lab_t).then_inc(sem("sub_dma"), 16)
            pool.wait_ge(sem("sub_dma"), 16)
            pool.dma_start(lt, sub_in.rearrange("s y t -> y s t")).then_inc(sem("sub_dma"), 16)
            pool.wait_ge(sem("inverse_ready"), 1)
            pool.dma_start(sub_out, mt).then_inc(sem("sub_dma"), 16)
            pool.wait_ge(sem("sub_dma"), 48)
            pool.dma_start(lab_t, sub_out.rearrange("y j t -> j y t")).then_inc(sem("sub_dma"), 16)
            link(pool.memset(state, 0.0))
            pool.nop().then_inc(sem("state_ready"), 1)
            for c in range(NCHUNK - 1):
                pool.wait_ge(sem("y1_done"), c + 1)
                pool.wait_ge(sem("state_ready"), c + 1)
                pool.tensor_tensor(state, state, chunk_decay[:, :, c:c + 1].broadcast_to([P, KC, P]),
                                   ALU.mult).then_inc(sem("state_decayed"), 1)

            def silu_tiles(ly, n):
                src = g_tile if n == 0 else c_tile

                def body(u, p, last):
                    for m in range(2):
                        pool.wait_ge(sem("glu_sig"), FC * n + 2 * u + m + 1)
                        pool.tensor_tensor(s_tile[m], s_tile[m], src[m], ALU.mult).then_inc(sem("glu_silu"), 1)
                units(pool, ly, body)
            silu_tiles(L["up0"], 0)
            ly = L["ssd_xbc"]
            for m in range(M_PER_UNIT):
                pool.nop().then_inc(sem("xbc_ready"), 1)

            def xbc_silu(u, p, last):
                for m in range(M_PER_UNIT):
                    j = 4 * u + m
                    t = xbc[:, j, :] if isinstance(u, int) else pj[:, bass.ds(SSD_Z + j, 1), :].rearrange("p a b -> p (a b)")
                    pool.wait_ge(sem("xbc_sig"), j + 1)
                    pool.tensor_tensor(t, t, conv_sig[m], ALU.mult).then_inc(sem("xbc_ready"), 1)
            units(pool, ly, xbc_silu)
            pool.wait_ge(sem("xdt_ready"), 4)
            pool.tensor_tensor(xdt_end.rearrange("p (h d) -> p h d", d=HEAD),
                               xdt[:, 0, :].rearrange("p (h d) -> p h d", d=HEAD),
                               tok_heads[:, 4, :].unsqueeze(2).broadcast_to([P, SSD_HEADS, HEAD]), ALU.mult).then_inc(sem("xdt_end_ready"), 1)
            silu_tiles(L["up1"], 1)
            pool.wait_ge(sem("fox_arena_free"), 1)
            link(pool.memset(fox_mask, 0.0))
            link(pool.affine_select(out=fox_mask[:, P:T], in_=fox_mask[:, P:T], compare_op=ALU.is_ge, fill=MASKED,
                                    base=0, pattern=[[-1, P]], channel_multiplier=1))
            pool.nop().then_inc(sem("fox_mask_ready"), 1)
            silu_tiles(L["up2"], 2)

        @block.scalar
        def _(act):
            ch = Chain(act, "act_chain")
            go, sync, link = ch.go, ch.sync, ch.link
            n = 0
            for name, rows, src in par_rows:
                c0, r0 = col[name], 0
                while r0 < rows:
                    t, p0 = divmod(c0 + r0, P)
                    m = min(rows - r0, P - p0)
                    act.dma_start(par_tok[p0:p0 + m, t, :], src[r0:r0 + m, :]).then_inc(sem("par_loaded"), 16)
                    n += 1
                    r0 += m
            assert n == par_dmas
            for i, name in enumerate(("ssd_dt_bias_2", "ssd_a_log_2")):
                act.dma_start(heads_col[:, i:i + 1], a[name][0].rearrange("(h a) -> h a", a=1)).then_inc(sem("small_loaded"), 16)
            act.dma_start(heads_col[0:FOX_HEADS, 2:3], a["fox_b_f_2"][0].rearrange("(h a) -> h a", a=1)).then_inc(sem("small_loaded"), 16)
            for h in range(2):
                for i, name in enumerate(("fox_q_norm_g_2", "fox_k_norm_g_2")):
                    act.dma_start(fox_g[64 * h:64 * h + 64, i:i + 1], a[name][0].rearrange("(d a) -> d a", a=1)).then_inc(sem("small_loaded"), 16)
                act.dma_start(d_skip[64 * h:64 * h + 64, :],
                              a["ssd_d_2"][0].rearrange("(m t a) -> t a m", t=2, a=1)[h].broadcast_to([64, SSD_Z]), allow_slow_non_contiguous=True).then_inc(sem("small_loaded"), 16)

            def norm_in(n):
                name, o = NORMS[n]
                for k in range(KC):
                    act.wait_ge(sem("x_ready"), KC * n + k + 1)
                    act.activation(sub[:, k, :], x_res[:, k, :], ACT.Square).then_inc(sem("sq_ready"), 1)
                    act.activation(x_hi[:, k, :], x_res[:, k, :], ACT.Copy, scale=par_col(name, o + k)).then_inc(sem("x_hi_ready"), 1)

            def norm_root(n, bank=7):
                act.wait_ge(sem("ssq_done"), n + 1)
                act.activation(rs[:, :], pb[bank][:, 0:T], ACT.Sqrt, bias=eps[:, 0:1], scale=1.0 / D).then_inc(sem("rs_ready"), 1)

            act.wait_ge(sem("const_ready"), 1)
            norm_in(0)
            ahead(act_head, act, L["rkv"])
            norm_root(0)
            act_layer(act, L["rkv"])
            act.wait_ge(sem("lora1_done"), 1)
            act.activation(lora_w, pb[4][0:64, 0:T], ACT.Tanh).then_inc(sem("lora_mid"), 1)
            act.wait_ge(sem("lora1_done"), 2)
            act.activation(lora_a, pb[5][0:64, 0:T], ACT.Copy).then_inc(sem("lora_mid"), 1)
            act.wait_ge(sem("lora1_done"), 3)
            act.activation(lora_g, pb[6][:, 0:T], ACT.Sigmoid).then_inc(sem("lora_mid"), 1)
            for f, (dst, bias) in enumerate(((W, "decay_w0"), (A, "a_0"), (G, None))):
                for j in range(4):
                    i = 4 * f + j
                    act.wait_ge(sem("lora2_done"), i + 1)
                    bank = pb[4 + i % 3]
                    if bias:
                        go(act.activation(slot(dst)[:, 2 * j, :], bank[:, 0:T], ACT.Sigmoid, bias=par_col(bias, 2 * j)))
                        act.activation(slot(dst)[:, 2 * j + 1, :], bank[:, T:2 * T], ACT.Sigmoid,
                                       bias=par_col(bias, 2 * j + 1)).then_inc(sem("lora_ready"), 1)
                    else:
                        act.activation(slot(dst)[:, 2 * j:2 * j + 2, :], bank[:, :], ACT.Copy).then_inc(sem("lora_ready"), 1)
            act.wait_ge(sem("kk_ready"), 1)
            act.activation(slot(TMP), slot(KK), ACT.Square).then_inc(sem("kk_sq"), 1)
            act.wait_ge(sem("bonus_done"), 1)
            act.activation(bonus, pb[3][0:RWKV_HEADS, 0:T], ACT.Copy).then_inc(sem("bonus_ready"), 1)
            act.wait_ge(sem("kk_max"), 4)
            act.activation(slot(TMP), slot(TMP), ACT.Sqrt).then_inc(sem("kk_root"), 1)
            act.wait_ge(sem("cum_ready"), KC)
            act.activation(slot(W), slot(TMP), ACT.Exp, scale=-EXP_MINUS_HALF).then_inc(sem("decay_ready"), 1)
            act.wait_ge(sem("decay_ready"), 1)
            act.activation(slot(TMP), slot(TMP), ACT.Exp, scale=EXP_MINUS_HALF).then_inc(sem("decay_ready"), 1)
            ahead(act_head, act, L["ug"])
            act_layer(act, L["ug"])
            ahead(act_head, act, L["z"])
            act_layer(act, L["z"])
            act.wait_ge(sem("evac_done"), L["ug"].evac1 + BANKS)
            act.activation(slot(GATE), slot(GATE), ACT.Sigmoid).then_inc(sem("gate_ready"), 1)
            act.wait_ge(sem("evac_done"), L["z"].evac1 + BANKS)
            act.activation(slot(ZR), slot(ZR), ACT.Sigmoid).then_inc(sem("z_ready"), 1)
            act.activation(slot(ZC), slot(ZC), ACT.Sigmoid).then_inc(sem("z_ready"), 1)

            def v_rows(c):
                act.wait_ge(sem("v_turned"), c + 1)
                if c >= 2:
                    act.wait_ge(sem("y2_done"), c - 1)
                go(act.activation(uv[c % 2][0:CHUNK, 0:512], pb[2][0:CHUNK, :], ACT.Copy))
                act.activation(uv[c % 2][0:CHUNK, 512:1024], pb[3][0:CHUNK, :], ACT.Copy).then_inc(sem("v_rows"), 1)

            def bk_rows(c):
                act.wait_ge(sem("bk_turned"), c + 1)
                if c >= 2:
                    act.wait_ge(sem("y2_done"), c - 1)
                go(act.activation(bk_t[c % 2][:, 0:512], pb[0][0:64, :], ACT.Copy))
                act.activation(bk_t[c % 2][:, 512:1024], pb[1][0:64, :], ACT.Copy).then_inc(sem("bk_rows"), 1)

            act.wait_ge(sem("sub_dma"), 64)
            v_rows(0)
            bk_rows(0)
            for c in range(NCHUNK):
                act.wait_ge(sem("x_done"), c + 1)
                act.activation(x_buf[:, 512:1024], pb[5][0:CHUNK, :], ACT.Copy).then_inc(sem("x_rows_a"), 1)
                if c + 1 < NCHUNK:
                    v_rows(c + 1)
                act.wait_ge(sem("u_done"), c + 1)
                act.activation(uv[c % 2][CHUNK:2 * CHUNK, 512:1024], pb[5][0:CHUNK, :], ACT.Copy).then_inc(sem("u_rows_a"), 1)
                if c + 1 < NCHUNK:
                    bk_rows(c + 1)
            act.wait_ge(sem("gn_centred"), 4)
            act.activation(tmp2, slot(R), ACT.Square).then_inc(sem("gn_sq"), 1)
            act.wait_ge(sem("gn_var"), 1)
            for b in range(4):
                act.activation(slot(TMP)[:, 2 * b:2 * b + 2, :], pb[4 + b][:, :], ACT.Sqrt, bias=eps[:, 2:3],
                               scale=1.0 / HEAD).then_inc(sem("gn_root"), 1)
            act.wait_ge(sem("ln_centred"), 1)
            act.activation(tmp2, slot(GATE), ACT.Square).then_inc(sem("ln_sq"), 1)
            act.wait_ge(sem("ln_var"), 1)
            act.activation(rs[:, :], pb[5][:, 0:T], ACT.Sqrt, bias=eps[:, 1:2], scale=1.0 / D).then_inc(sem("ln_root"), 1)
            ahead(act_head, act, L["conv_out"])
            act.wait_ge(sem("ln_ready"), 1)
            act.activation(slot(TMP), slot(GATE), ACT.Sigmoid).then_inc(sem("ln_sig"), 1)
            for i, (src, ly) in enumerate(((GATE, "conv_out"), (R, "rwkv_out"), (ZC, "w_out"))):
                act.wait_ge(sem("mix_in"), i + 1)
                for k in range(KC):
                    act.activation(x_hi[:, k, :], slot(src)[:, k, :], ACT.Copy).then_inc(sem("x_hi_ready"), 1)
                act_layer(act, L[ly])
                if i < 2:
                    ahead(act_head, act, L[("rwkv_out", "w_out")[i]])

            def post_norm(i, first, bank):
                for k in range(KC):
                    act.wait_ge(sem("evac_done"), first + k + 1 + BANKS)
                    act.activation(sub[:, k, :], tile(64 if i else 0, k), ACT.Square).then_inc(sem("osq_ready"), 1)
                act.wait_ge(sem("osum_done"), i + 1)
                act.activation(rs[:, :], pb[bank][:, 0:T], ACT.Sqrt, bias=eps[:, 0:1], scale=1.0 / D).then_inc(sem("ors_ready"), 1)

            ahead(act_head, act, L["up0"])
            post_norm(0, L["w_out"].evac0, 7)
            norm_in(1)
            norm_root(1)

            def ffn(n, up, down):
                src = g_tile if n == 0 else c_tile

                def sig(u, m):
                    act.wait_ge(sem("glu_gate"), FC * n + 2 * u + m + 1)
                    act.activation(s_tile[m], src[m], ACT.Sigmoid).then_inc(sem("glu_sig"), 1)

                def head(u, m):
                    act.wait_ge(sem("act_ready"), FC * n + 2 * u + m + 1)
                    j = 2 * u + m
                    o = act_hi[:, j, :] if isinstance(u, int) else act_hi[:, bass.ds(j, 1), :].rearrange("p a b -> p (a b)")
                    act.activation(o, a_tile[m], ACT.Copy).then_inc(sem("act_hi_ready"), 1)

                def hook(u, m):
                    if m in (1, 2):
                        sig(u, m - 1)
                    if m == 3:
                        head(u, 0)
                        head(u, 1)
                act_layer(act, up, hook)
                ahead(act_head, act, down)
                act_layer(act, down)

            ffn(0, L["up0"], L["down0"])
            ahead(act_head, act, L["ssd_z"])
            post_norm(1, L["down0"].evac0, 7)
            norm_in(2)
            norm_root(2)
            act_layer(act, L["ssd_z"])
            ahead(act_head, act, L["ssd_xbc"])

            def xbc_sig(u, m):
                j = 4 * u + m
                t = xbc[:, j, :] if isinstance(u, int) else pj[:, bass.ds(SSD_Z + j, 1), :].rearrange("p a b -> p (a b)")
                act.wait_ge(sem("xbc_conv"), j + 1)
                act.wait_ge(sem("xbc_ready"), j + 1)
                act.activation(conv_sig[m], t, ACT.Sigmoid).then_inc(sem("xbc_sig"), 1)
            act_layer(act, L["ssd_xbc"], xbc_sig)
            act.wait_ge(sem("dt_abs"), 1)
            link(act.activation(dt_e, dt_e, ACT.Exp, scale=-1.0))
            act.wait_ge(sem("small_loaded"), 16 * 9)
            go(act.activation(heads_col[:, 3:4], heads_col[:, 1:2], ACT.Exp))
            act.activation(dt_e, dt_e, ACT.Ln, bias=1.0).then_inc(sem("dt_log"), 1)
            act.wait_ge(sem("acs_ready"), 2)
            go(act.activation(da_end, acs[:, 0:P], ACT.Exp, scale=-1.0, bias=acs[:, P - 1:P]))
            act.activation(da_exp, acs[:, P:T], ACT.Exp).then_inc(sem("da_ready"), 1)
            act.wait_ge(sem("xbc_ready"), M_PER_UNIT + SSD_XBC)
            for b in range(4):
                act.wait_ge(sem("eab_done"), b + 1)
                act.activation(eab[:, 4 * b:4 * b + 4, :].rearrange("p m l -> p (m l)"), pb[4 + b % 2][:, :], ACT.Copy).then_inc(sem("eab_ready"), 1)
            ahead(act_head, act, L["ssd_out"])
            for i in range(16):
                act.wait_ge(sem("diff_ready"), i + 1)
                a2 = att[i % 2].rearrange("p h l -> p (h l)")
                act.activation(a2, a2, ACT.Exp).then_inc(sem("att_exp"), 1)
            act.wait_ge(sem("evac_done"), L["ssd_z"].evac1 + BANKS)
            act.wait_ge(sem("eab_used"), 4)
            for h in range(2):
                act.activation(sub[:, 0:8, :], z_t[:, 8 * h:8 * h + 8, :], ACT.Sigmoid).then_inc(sem("z_sig"), 1)
                act.wait_ge(sem("yz_ready"), h + 1)
            for g in range(SSD_GROUPS):
                act.wait_ge(sem("yz_ready"), 2)
                if g >= 2:
                    act.wait_ge(sem("yz_sum"), g - 1)
                act.activation(sub[:, 4 * (g % 2):4 * (g % 2) + 4, :], y_ssd[:, 4 * g:4 * g + 4, :], ACT.Square).then_inc(sem("yz_sq"), 1)
            for g in range(SSD_GROUPS):
                act.wait_ge(sem("yz_sum"), g + 1)
                act.activation(sub[:, 8 + g, :], pb[4 + g][:, 0:T], ACT.Sqrt, bias=eps[:, 0:1], scale=1.0 / (4 * P)).then_inc(sem("yz_root"), 1)
            for m in range(SSD_Z):
                act.wait_ge(sem("yn_ready"), m + 1)
                act.activation(yz_hi[:, m, :], y_ssd[:, m, :], ACT.Copy).then_inc(sem("yz_hi_ready"), 1)
            act_layer(act, L["ssd_out"])
            ahead(act_head, act, L["up1"])
            norm_in(3)
            norm_root(3)
            ffn(1, L["up1"], L["down1"])
            ahead(act_head, act, L["fox_in"])
            norm_in(4)
            norm_root(4)
            act_layer(act, L["fox_in"])
            act.wait_ge(sem("f_abs"), 1)
            link(act.activation(dt_e[0:FOX_HEADS, :], dt_e[0:FOX_HEADS, :], ACT.Exp, scale=-1.0))
            act.activation(dt_e[0:FOX_HEADS, :], dt_e[0:FOX_HEADS, :], ACT.Ln, bias=1.0).then_inc(sem("f_log"), 1)
            act.wait_ge(sem("evac_done"), L["fox_in"].evac1 + BANKS)
            act.activation(gate_t, gate_t, ACT.Sigmoid).then_inc(sem("fox_gate"), 1)
            for i, t in enumerate((q_t, k_t)):
                if i:
                    act.wait_ge(sem("fox_sum"), 1)
                act.activation(fox_tmp, t, ACT.Square).then_inc(sem("fox_sq"), 1)
                act.wait_ge(sem("fox_sum"), i + 1)
                for b in range(4):
                    act.activation(tmp2[:, 2 * b:2 * b + 2, :], pb[4 + b][:, :], ACT.Sqrt, bias=eps[:, 0:1], scale=1.0 / HEAD).then_inc(sem("fox_root"), 1)
                act.wait_ge(sem("qk_ready"), i + 1)
            ahead(act_head, act, L["fox_out"])
            for i in range(2 * FOX_HEADS):
                n, s = (i % 2 + 1) * P, i % NS
                act.wait_ge(sem("max_ready"), i + 1)
                act.activation(sc[s][:, 0, 0:n], sc[s][:, 1, 0:n], ACT.Exp, bias=fox_stat[:, 2 * (i % 2), i // 2:i // 2 + 1],
                               accum_out=fox_stat[:, 2 * (i % 2) + 1, i // 2:i // 2 + 1]).then_inc(sem("exp_ready"), 1)
                act.wait_ge(sem("share_ready"), i + 1)
                act.activation(sc[s][:, 0, 0:n], sc[s][:, 0, 0:n], ACT.Copy,
                               scale=fox_stat[:, 4 + i % 2, i // 2:i // 2 + 1]).then_inc(sem("p_ready"), 1)
            for k in range(KC):
                act.wait_ge(sem("o_ready"), k + 1)
                act.activation(x_hi[:, k, :], o_fox[:, k, :], ACT.Copy).then_inc(sem("x_hi_ready"), 1)
            act_layer(act, L["fox_out"])
            ahead(act_head, act, L["up2"])
            act.wait_ge(sem("block_done"), L["fox_out"].item1 + BANKS)
            norm_in(5)
            norm_root(5)
            ffn(2, L["up2"], L["down2"])
            for k in range(KC):
                act.wait_ge(sem("x_ready"), KC * 6 + k + 1)
                act.activation(sub[:, k, :], x_res[:, k, :], ACT.Square).then_inc(sem("sq_ready"), 1)
            norm_root(6)

        @block.vector
        def _(dve):
            ch = Chain(dve, "dve_chain")
            go, sync, link = ch.go, ch.sync, ch.link
            stt, tt, ts = dve.scalar_tensor_tensor, dve.tensor_tensor, dve.tensor_scalar

            def norm_rest(n):
                name, o = NORMS[n]
                for k in range(KC):
                    dve.wait_ge(sem("x_hi_ready"), X_BASE[n] + k + 1)
                    stt(x_lo[:, k, :], x_res[:, k, :], par_col(name, o + k), x_hi[:, k, :].bitcast(F32),
                        ALU.mult, ALU.subtract).then_inc(sem("x_lo_ready"), 1)

            def norm_scale(n):
                dve.wait_ge(sem("rs_ready"), n + 1)
                link(dve.reciprocal(rstd[:, :], rs[:, :]))

            def scaled(dst):
                def out_block(u, m):
                    j = M_PER_UNIT * u + m
                    o = dst(j) if isinstance(u, int) else pj[:, bass.ds(j + dst(None), 1), :].rearrange("p a b -> p (a b)")
                    tt(o, pb[m][:, 0:T], rstd[:, :], ALU.mult).then_inc(sem("evac_done"), 1)
                return out_block

            for i in range(BANKS):
                dve.nop().then_inc(sem("evac_done"), 1)
            for b in range(2):
                dve.wait_ge(sem("par_turned"), b + 1)
                n = min(n_rows - 512 * b, 512)
                go(dve.tensor_copy(par[:, 512 * b:512 * b + n], pb[1 + b][:, 0:n]))
            sync()
            for k in range(KC):
                dve.wait_ge(sem("x_turned"), k // 2 + 1)
                dve.tensor_copy(x_res[:, k, :], pb[3 + k // 2][:, T * (k % 2):T * (k % 2) + T]).then_inc(sem("x_ready"), 1)
            dve.wait_ge(sem("x_ready"), KC)
            norm_rest(0)
            ahead(dve_rest, dve, L["rkv"])
            norm_scale(0)
            h, xx = slot(TMP), slot(W)
            for k in range(KC):
                go(stt(h[:, k, :], x_res[:, k, :], par_col("pre_mix_norm", k), rstd[:, :], ALU.mult, ALU.mult))
            sync()

            def shift_less(o, s):
                go(tt(o[:, :, 1:T], s[:, :, 0:T - 1], s[:, :, 1:T], ALU.subtract))
                link(ts(o[:, :, 0:1], s[:, :, 0:1], -1.0, None, ALU.mult))

            shift_less(xx, h)
            for i, s in enumerate((KK, A, G)):
                for k in range(KC):
                    ins = stt(slot(s)[:, k, :], xx[:, k, :], par_col("mu_wag", KC * i + k), h[:, k, :], ALU.mult, ALU.add)
                    ins.then_inc(sem("lora_x"), 1)
            dve_layer(dve, L["rkv"], scaled(lambda j: tile(0, j) if j is not None else 0))
            dve.wait_ge(sem("evac_done"), L["rkv"].evac1 + BANKS)

            def lerp(s, i):
                shift_less(tmp2, slot(s))
                for k in range(KC):
                    go(stt(slot(s)[:, k, :], tmp2[:, k, :], par_col("mu_rkv", KC * i + k), slot(s)[:, k, :], ALU.mult, ALU.add))
                sync()
            lerp(K, 1)
            dve.wait_ge(sem("lora1_done"), 1)
            for k in range(KC):
                go(ts(slot(KK)[:, k, :], slot(K)[:, k, :], par_col("k_k", k), None, ALU.mult))
            sync()
            dve.nop().then_inc(sem("kk_ready"), 1)
            lerp(R, 0)
            lerp(V, 2)
            dve.wait_ge(sem("lora_ready"), 8)
            for k in range(KC):
                go(ts(tmp2[:, k, :], slot(A)[:, k, :], 1.0, par_col("k_a", k), ALU.subtract, ALU.mult))
            sync()
            link(stt(slot(K), tmp2, 1.0, slot(K), ALU.add, ALU.mult))
            for k in range(KC):
                go(stt(tmp2[:, k, :], slot(R)[:, k, :], par_col("r_k", k), slot(K)[:, k, :], ALU.mult, ALU.mult))
            sync()
            dve.nop().then_inc(sem("bonus_in"), 1)
            dve.wait_ge(sem("kk_sum"), 1)
            for b in range(4):
                ts(slot(TMP)[:, 2 * b:2 * b + 2, :], pb[4 + b][:, :], 1e-24, None, ALU.max).then_inc(sem("kk_max"), 1)
            dve.wait_ge(sem("kk_root"), 1)
            link(dve.reciprocal(slot(TMP), slot(TMP)))
            link(tt(slot(KK), slot(KK), slot(TMP), ALU.mult))
            link(tt(slot(A), slot(KK), slot(A), ALU.mult))
            dve.wait_ge(sem("lora_ready"), 12)
            for k in range(KC):
                dve.tensor_tensor_scan(slot(TMP)[:, k, :], scan_mask[:, :], slot(W)[:, k, :], 0.0, ALU.mult,
                                       ALU.add).then_inc(sem("cum_ready"), 1)
            dve.wait_ge(sem("decay_ready"), 2)

            def chunks(i):
                return slot(i).rearrange("p k (c s) -> p (k c) s", s=CHUNK)

            bk_v = bk.rearrange("p k c j s -> p (k c) j s")
            go(tt(slot(R), slot(R), slot(W), ALU.mult))
            go(stt(chunks(KK)[:, :, 1:CHUNK], chunks(KK)[:, :, 1:CHUNK], -1.0, chunks(W)[:, :, 0:CHUNK - 1], ALU.mult, ALU.mult))
            go(ts(chunks(KK)[:, :, 0:1], chunks(KK)[:, :, 0:1], -1.0, None, ALU.mult))
            go(tt(bk_v[:, :, 0, :], chunks(K), chunks(TMP), ALU.mult))
            go(tt(bk_v[:, :, 1, :], chunks(A), chunks(TMP), ALU.mult))
            go(dve.tensor_copy(chunk_decay[:, :, :].rearrange("p k c -> p (k c)"), chunks(W)[:, :, CHUNK - 1]))
            sync()
            dve.nop().then_inc(sem("scan_in"), 1)
            for c in range(NCHUNK):
                dve.wait_ge(sem("lab_done"), c + 1)
                dst = lab_t[:, 16 * c:16 * c + 16, :].rearrange("s (m h) t -> s h m t", h=2)
                for h in range(2):
                    ins = tt(dst[:, h], pb[4 + 2 * h + c % 2][0:CHUNK, 0:T].rearrange("s (m t) -> s m t", t=CHUNK),
                             g_mask[0:CHUNK, CHUNK:2 * CHUNK].unsqueeze(1).broadcast_to([CHUNK, 8, CHUNK]), ALU.mult)
                    if h:
                        ins.then_inc(sem("lab_ready"), 1)
                    else:
                        go(ins)
            dve.wait_ge(sem("lab_ready"), NCHUNK)
            ahead(dve_rest, dve, L["ug"])
            dve_layer(dve, L["ug"], scaled(lambda j: tile(24, j)))
            dve.wait_ge(sem("sub_dma"), 32)
            link(dve.memset(mt, 0.0))
            link(dve.memset(mt.rearrange("p s t -> p (s t)")[:, 0:CHUNK * CHUNK:CHUNK + 1], 1.0))
            for t in range(1, CHUNK):
                link(tt(prod[:, 0:t, 0:t], mt[:, 0:t, 0:t], lt[:, 0:t, t].unsqueeze(1).broadcast_to([P, t, t]), ALU.mult))
                link(dve.tensor_reduce(mt[:, 0:t, t], prod[:, 0:t, 0:t], AX_X, ALU.add))
            dve.nop().then_inc(sem("inverse_ready"), 1)
            ahead(dve_rest, dve, L["z"])
            dve_layer(dve, L["z"], scaled(lambda j: slot(ZR)[:, j, :] if j < KC else slot(ZC)[:, j - KC, :]))
            dve.wait_ge(sem("gate_ready"), 1)
            link(tt(slot(U), slot(U), slot(GATE), ALU.mult))
            for tap in range(CONV_TAPS - 1, -1, -1):
                s = CONV_TAPS - 1 - tap
                for k in range(KC):
                    w = par_col("conv_dw", KC * tap + k)
                    o, c = slot(GATE)[:, k, :], slot(U)[:, k, :]
                    if s == 0:
                        go(ts(o, c, w, par_col("conv_b", k), ALU.mult, ALU.add))
                    else:
                        go(stt(o[:, s:T], c[:, 0:T - s], w, o[:, s:T], ALU.mult, ALU.add))
                sync()
            dve.nop().then_inc(sem("conv_ready"), 1)
            dve.wait_ge(sem("z_ready"), 2)

            def mask_products(c):
                dve.wait_ge(sem("g_done"), c + 1)
                if c >= 2:
                    dve.wait_ge(sem("y2_done"), c - 1)
                for h in range(2):
                    go(tt(g_buf[c % 2][:, h::2, :], pb[h][64:128, :].rearrange("s (m n) -> s m n", n=64),
                          g_mask[64:128, :].unsqueeze(1).broadcast_to([64, 8, 64]), ALU.mult))
                sync()
                dve.nop().then_inc(sem("g_masked"), 1)
                v = bk[:, :, c, :, :].rearrange("p k j s -> p k (j s)")
                tt(v, v, chunk_decay[:, :, c:c + 1].broadcast_to([P, KC, 2 * CHUNK]), ALU.mult).then_inc(sem("bk_scaled"), 1)

            dve.wait_ge(sem("sub_dma"), 64)
            mask_products(0)
            for c in range(NCHUNK):
                dve.wait_ge(sem("x_done"), c + 1)
                dve.tensor_copy(x_buf[:, 0:512], pb[4][0:CHUNK, :]).then_inc(sem("x_rows_v"), 1)
                if c + 1 < NCHUNK:
                    mask_products(c + 1)
                dve.wait_ge(sem("u_done"), c + 1)
                dve.tensor_copy(uv[c % 2][CHUNK:2 * CHUNK, 0:512], pb[4][0:CHUNK, :]).then_inc(sem("u_rows_v"), 1)
                if c + 1 < NCHUNK:
                    dve.wait_ge(sem("s_done"), c + 1)
                    dve.wait_ge(sem("state_decayed"), c + 1)
                    for h in range(2):
                        rows = slice(64 * h, 64 * h + 64)
                        go(tt(state[rows, :, rows], state[rows, :, rows],
                              pb[6][rows, :].rearrange("k (m v) -> k m v", v=64), ALU.add))
                    sync()
                    dve.nop().then_inc(sem("state_ready"), 1)
                dve.wait_ge(sem("y2_done"), c + 1)
                dve.tensor_copy(slot(R)[:, :, CHUNK * c:CHUNK * c + CHUNK],
                                pb[7][:, 0:T].rearrange("p (m t) -> p m t", t=CHUNK)).then_inc(sem("y_out"), 1)
            dve.wait_ge(sem("y_out"), NCHUNK)

            y = slot(R)
            dve.wait_ge(sem("gn_mean"), 1)
            for b in range(4):
                yb = y[:, 2 * b:2 * b + 2, :].rearrange("p k t -> p (k t)")
                stt(yb, pb[4 + b][:, :], -1.0 / HEAD, yb, ALU.mult, ALU.add).then_inc(sem("gn_centred"), 1)
            dve.wait_ge(sem("gn_root"), 4)
            link(dve.reciprocal(slot(TMP), slot(TMP)))
            link(tt(y, y, slot(TMP), ALU.mult))
            for k in range(KC):
                go(ts(y[:, k, :], y[:, k, :], par_col("gn_w", k), par_col("gn_b", k), ALU.mult, ALU.add))
            dve.wait_ge(sem("bonus_out"), 1)
            for b in range(4):
                go(tt(slot(TMP)[:, 2 * b:2 * b + 2, :].rearrange("p k t -> p (k t)"),
                      slot(V)[:, 2 * b:2 * b + 2, :].rearrange("p k t -> p (k t)"), pb[4 + b][:, :], ALU.mult))
            sync()
            link(tt(y, y, slot(TMP), ALU.add))
            link(tt(y, y, slot(G), ALU.mult))
            dve.nop().then_inc(sem("gn_out"), 1)

            cv = slot(GATE)
            dve.wait_ge(sem("ln_mean"), 1)
            link(ts(sub[:, 8, :], pb[4][:, 0:T], 1.0 / D, None, ALU.mult))
            link(tt(cv, cv, sub[:, 8:9, :].broadcast_to([P, KC, T]), ALU.subtract))
            dve.nop().then_inc(sem("ln_centred"), 1)
            dve.wait_ge(sem("ln_root"), 1)
            link(dve.reciprocal(sub[:, 9, :], rs[:, :]))
            link(tt(cv, cv, sub[:, 9:10, :].broadcast_to([P, KC, T]), ALU.mult))
            for k in range(KC):
                go(ts(cv[:, k, :], cv[:, k, :], par_col("conv_ln_w", k), par_col("conv_ln_b", k), ALU.mult, ALU.add))
            sync()
            dve.nop().then_inc(sem("ln_ready"), 1)
            ahead(dve_rest, dve, L["conv_out"])
            dve.wait_ge(sem("ln_sig"), 1)
            link(tt(cv, cv, slot(TMP), ALU.mult))

            def mix_rest(i, src):
                dve.nop().then_inc(sem("mix_in"), 1)
                for k in range(KC):
                    dve.wait_ge(sem("x_hi_ready"), KC * (i + 1) + k + 1)
                    tt(x_lo[:, k, :], slot(src)[:, k, :], x_hi[:, k, :].bitcast(F32), ALU.subtract).then_inc(sem("x_lo_ready"), 1)

            mix_rest(0, GATE)

            def gate_conv(u, m):
                o = slot(ZC)[:, M_PER_UNIT * u + m, :]
                tt(o, o, pb[m][:, 0:T], ALU.mult).then_inc(sem("evac_done"), 1)
            dve_layer(dve, L["conv_out"], gate_conv)
            ahead(dve_rest, dve, L["rwkv_out"])
            dve.wait_ge(sem("evac_done"), L["conv_out"].evac1 + BANKS)
            mix_rest(1, R)

            def gate_rwkv(u, m):
                o, z = slot(ZC)[:, M_PER_UNIT * u + m, :], slot(ZR)[:, M_PER_UNIT * u + m, :]
                tt(z, z, pb[m][:, 0:T], ALU.mult).then_inc(sem("evac_done"), 1)
                dve.wait_ge(sem("evac_done"), L["rwkv_out"].evac0 + M_PER_UNIT * u + m + 1 + BANKS)
                go(tt(o, o, z, ALU.add))
            dve_layer(dve, L["rwkv_out"], gate_rwkv)
            sync()
            ahead(dve_rest, dve, L["w_out"])
            mix_rest(2, ZC)

            def plain(dst):
                def out_block(u, m):
                    dve.tensor_copy(tile(dst, M_PER_UNIT * u + m), pb[m][:, 0:T]).then_inc(sem("evac_done"), 1)
                return out_block

            def post_norm(i, src, name):
                dve.wait_ge(sem("ors_ready"), i + 1)
                link(dve.reciprocal(rstd[:, :], rs[:, :]))
                for k in range(KC):
                    go(stt(tile(src, k), tile(src, k), par_col(name, k), rstd[:, :], ALU.mult, ALU.mult))
                sync()
                for k in range(KC):
                    tt(x_res[:, k, :], x_res[:, k, :], tile(src, k), ALU.add).then_inc(sem("x_ready"), 1)

            def norm_begin(n):
                dve.wait_ge(sem("x_ready"), KC * (n + 1))
                norm_rest(n)
                norm_scale(n)

            dve_layer(dve, L["w_out"], plain(0))
            ahead(dve_rest, dve, L["up0"])
            post_norm(0, 0, "post_mix_norm")
            norm_begin(1)

            def ffn(n, up, down, out_block):
                w = lambda tap, j: par_col("ffn_conv_w_2", (n - 1) * GLU_TAPS * FC + tap * FC + j)

                def hidden(u, m):
                    e = up.evac0 + M_PER_UNIT * u + m + 1 + BANKS
                    if m < 2:
                        tt(g_tile[m], pb[m][:, 0:T], rstd[:, :], ALU.mult).then_inc(sem("evac_done"), 1)
                        dve.wait_ge(sem("evac_done"), e)
                        if n:
                            j = 2 * u + m
                            conv_step(u, ts(c_tile[m], g_tile[m], w(2, j), par_col("ffn_conv_b_2", (n - 1) * FC + j), ALU.mult, ALU.add),
                                      n, 3 * m)
                            for s in (1, 2):
                                conv_step(u, stt(c_tile[m][:, s:T], g_tile[m][:, 0:T - s], w(2 - s, j), c_tile[m][:, s:T],
                                                 ALU.mult, ALU.add), n, 3 * m + s)
                        dve.nop().then_inc(sem("glu_gate"), 1)
                    else:
                        tt(u_tile[m - 2], pb[m][:, 0:T], rstd[:, :], ALU.mult).then_inc(sem("evac_done"), 1)
                        dve.wait_ge(sem("evac_done"), e)
                        dve.wait_ge(sem("glu_silu"), FC * n + 2 * u + m - 1)
                        tt(a_tile[m - 2], u_tile[m - 2], s_tile[m - 2], ALU.mult).then_inc(sem("act_ready"), 1)
                    if m == 3:
                        for i in range(2):
                            j = 2 * u + i
                            if isinstance(u, int):
                                hi_, lo_ = act_hi[:, j, :], act_lo[:, j, :]
                            else:
                                hi_, lo_ = (t[:, bass.ds(j, 1), :].rearrange("p a b -> p (a b)") for t in (act_hi, act_lo))
                            dve.wait_ge(sem("act_hi_ready"), FC * n + j + 1)
                            tt(lo_, a_tile[i], hi_.bitcast(F32), ALU.subtract).then_inc(sem("act_lo_ready"), 1)
                dve_layer(dve, up, hidden)
                ahead(dve_rest, dve, down)
                dve_layer(dve, down, out_block)

            def conv_step(u, ins, n, s):
                ins.then_inc(sem("glu_step"), 1)
                dve.wait_ge(sem("glu_step"), GLU_TAPS * (FC * (n - 1) + 2 * u) + s + 1)

            def residual(u, m):
                x = x_res[:, M_PER_UNIT * u + m, :]
                ins = tt(x, x, pb[m][:, 0:T], ALU.add)
                ins.then_inc(sem("x_ready"), 1)
                dve.nop().then_inc(sem("evac_done"), 1)

            ffn(0, L["up0"], L["down0"], plain(64))
            ahead(dve_rest, dve, L["ssd_z"])
            post_norm(1, 64, "post_ffn_norm")
            norm_begin(2)

            def gain_in(n, which):
                name, o = NORMS[n]
                for k in range(KC):
                    ts(x_gain[:, k, :], x_res[:, k, :], par_col(name, o + k), None, ALU.mult).then_inc(sem(which), 1)

            gain_in(2, "dt_in")
            dve_layer(dve, L["ssd_z"], scaled(lambda j: z_t[:, j, :]))
            ahead(dve_rest, dve, L["ssd_xbc"])
            ly = L["ssd_xbc"]
            n_xbc = SSD_XBC

            def xbc_block(u, m):
                j = M_PER_UNIT * u + m
                t = xbc[:, j, :] if isinstance(u, int) else pj[:, bass.ds(SSD_Z + j, 1), :].rearrange("p a b -> p (a b)")
                tt(conv_in[m], pb[m][:, 0:T], rstd[:, :], ALU.mult).then_inc(sem("evac_done"), 1)
                dve.wait_ge(sem("evac_done"), ly.evac0 + j + 1 + BANKS)
                w = lambda tap: par_col("ssd_conv_w_2", tap * n_xbc + j)
                for s in range(SSD_TAPS):
                    if s == 0:
                        ins = ts(t, conv_in[m], w(3), par_col("ssd_conv_b_2", j), ALU.mult, ALU.add)
                    else:
                        ins = stt(t[:, s:T], conv_in[m][:, 0:T - s], w(3 - s), t[:, s:T], ALU.mult, ALU.add)
                    if s < SSD_TAPS - 1:
                        ins.then_inc(sem("xbc_step"), 1)
                        dve.wait_ge(sem("xbc_step"), (SSD_TAPS - 1) * j + s + 1)
                    else:
                        ins.then_inc(sem("xbc_conv"), 1)
            dve_layer(dve, ly, xbc_block)
            dve.wait_ge(sem("dt_done"), 1)
            dve.wait_ge(sem("small_loaded"), 16 * 9)
            link(tt(dt_z, pb[4][0:SSD_HEADS, 0:T], rstd[0:SSD_HEADS, :], ALU.mult))
            link(ts(dt_z, dt_z, heads_col[:, 0:1], None, ALU.add))
            stt(dt_e, dt_z, -1.0, dt_z, ALU.mult, ALU.max).then_inc(sem("dt_abs"), 1)
            dve.wait_ge(sem("dt_log"), 1)
            link(stt(dt, dt_z, 0.0, dt_e, ALU.max, ALU.add))
            link(ts(dt_z, dt, heads_col[:, 3:4], -1.0, ALU.mult, ALU.mult))
            for c in range(2):
                s = slice(c * P, c * P + P)
                dve.tensor_tensor_scan(acs[:, s], ones[0:SSD_HEADS, :], dt_z[:, s], 0.0, ALU.mult, ALU.add).then_inc(sem("acs_ready"), 1)
            for c in range(2):
                dve.wait_ge(sem("cb_done"), c + 1)
                tt(cbm[:, c], pb[6 + c][:, :].rearrange("p (g l) -> p g l", l=P),
                   tri[:, :].unsqueeze(1).broadcast_to([P, SSD_GROUPS, P]), ALU.mult).then_inc(sem("cbm_ready"), 1)
            dve.wait_ge(sem("b_turned"), 1)
            dve.tensor_copy(b_tok.rearrange("p g n -> p (g n)"), pb[5][:, :]).then_inc(sem("b_tok_ready"), 1)
            dve.wait_ge(sem("heads_turned"), 1)
            link(dve.tensor_copy(tok_heads[:, :, :].rearrange("p a h -> p (a h)"), pb[4][:, 0:5 * SSD_HEADS]))
            dve.nop().then_inc(sem("heads_ready"), 1)
            for i in range(8):
                c, b = divmod(i, 4)
                dve.wait_ge(sem("xs_turned"), i + 1)
                tt(xdt[:, c, 512 * b:512 * b + 512].rearrange("p (h d) -> p h d", d=HEAD),
                   pb[6 + i % 2][:, :].rearrange("p (h d) -> p h d", d=HEAD),
                   tok_heads[:, 2 + c, 8 * b:8 * b + 8].unsqueeze(2).broadcast_to([P, 8, HEAD]), ALU.mult).then_inc(sem("xdt_ready"), 1)
            for g in range(SSD_GROUPS):
                dve.wait_ge(sem("st_done"), g + 1)
                dve.tensor_copy(st_ssd[:, 512 * g:512 * g + 512], pb[6 + g % 2][:, :]).then_inc(sem("st_ready"), 1)
            for b in range(4):
                dve.wait_ge(sem("yoff_done"), b + 1)
                dve.wait_ge(sem("eab_ready"), b + 1)
                tt(y_ssd[:, 4 * b:4 * b + 4, P:T], pb[4 + b % 2][:, :].rearrange("p (m l) -> p m l", l=P),
                   eab[:, 4 * b:4 * b + 4, :], ALU.mult).then_inc(sem("eab_used"), 1)
            dve.wait_ge(sem("eab_used"), 4)
            for m in range(SSD_Z):
                go(stt(y_ssd[:, m, P:T], xbc[:, m, P:T], d_skip[:, m:m + 1], y_ssd[:, m, P:T], ALU.mult, ALU.add))
            sync()
            for i in range(18):
                if i < 16:
                    c, hq = divmod(i, 8)
                    dve.wait_ge(sem("bc_done"), i + 1)
                    if i >= 2:
                        dve.wait_ge(sem("y_done"), i - 1)
                    for r in range(4):
                        go(ts(att[i % 2][:, r, :], pb[i % 2][:, P * r:P * r + P], tok_heads[:, c, 4 * hq + r:4 * hq + r + 1],
                              0.0, ALU.subtract, ALU.min))
                    sync()
                    dve.nop().then_inc(sem("diff_ready"), 1)
                if 1 <= i < 17:
                    c, hq = divmod(i - 1, 8)
                    dve.wait_ge(sem("att_exp"), i)
                    t = att[(i - 1) % 2]
                    tt(t, t, cbm[:, c, hq // 2, :].unsqueeze(1).broadcast_to([P, 4, P]), ALU.mult).then_inc(sem("att_ready"), 1)
                if i >= 2:
                    c, hq = divmod(i - 2, 8)
                    dve.wait_ge(sem("y_done"), i - 1)
                    src = pb[2 + i % 2][:, 0:T].rearrange("p (m l) -> p m l", l=P)
                    if c == 0:
                        for r in range(2):
                            m = 2 * hq + r
                            ins = stt(y_ssd[:, m, 0:P], xbc[:, m, 0:P], d_skip[:, m:m + 1], src[:, r, :], ALU.mult, ALU.add)
                            if r == 0:
                                go(ins)
                    else:
                        yy = y_ssd[:, 2 * hq:2 * hq + 2, P:T]
                        ins = tt(yy, yy, src, ALU.add)
                    ins.then_inc(sem("y_out_ssd"), 1)
            dve.wait_ge(sem("y_out_ssd"), 16)
            for h in range(2):
                yy, zz = y_ssd[:, 8 * h:8 * h + 8, :], z_t[:, 8 * h:8 * h + 8, :]
                link(tt(yy, yy, zz, ALU.mult))
                dve.wait_ge(sem("z_sig"), h + 1)
                link(tt(yy, yy, sub[:, 0:8, :], ALU.mult))
                dve.nop().then_inc(sem("yz_ready"), 1)
            for g in range(SSD_GROUPS):
                dve.wait_ge(sem("yz_root"), g + 1)
                link(dve.reciprocal(sub[:, 8 + g, :], sub[:, 8 + g, :]))
                for m in range(4 * g, 4 * g + 4):
                    stt(y_ssd[:, m, :], y_ssd[:, m, :], par_col("ssd_norm_g_2", m), sub[:, 8 + g, :], ALU.mult, ALU.mult).then_inc(sem("yn_ready"), 1)
            ahead(dve_rest, dve, L["ssd_out"])
            dve.wait_ge(sem("yn_ready"), SSD_Z)
            for m in range(SSD_Z):
                dve.wait_ge(sem("yz_hi_ready"), m + 1)
                tt(yz_lo[:, m, :], y_ssd[:, m, :], yz_hi[:, m, :].bitcast(F32), ALU.subtract).then_inc(sem("yz_lo_ready"), 1)
            dve_layer(dve, L["ssd_out"], residual)
            ahead(dve_rest, dve, L["up1"])
            norm_begin(3)
            ffn(1, L["up1"], L["down1"], residual)
            ahead(dve_rest, dve, L["fox_in"])
            norm_begin(4)

            dve.nop().then_inc(sem("fox_arena_free"), 1)
            gain_in(4, "f_in")
            dve_layer(dve, L["fox_in"], scaled(lambda j: tile(0, j) if j is not None else 0))
            nh = FOX_HEADS
            dve.wait_ge(sem("f_done"), 1)
            link(tt(dt_z[0:nh, :], pb[4][0:nh, 0:T], rstd[0:nh, :], ALU.mult))
            link(ts(dt_z[0:nh, :], dt_z[0:nh, :], heads_col[0:nh, 2:3], None, ALU.add))
            stt(dt_e[0:nh, :], dt_z[0:nh, :], -1.0, dt_z[0:nh, :], ALU.mult, ALU.max).then_inc(sem("f_abs"), 1)
            dve.wait_ge(sem("f_log"), 1)
            link(stt(dt[0:nh, :], dt_z[0:nh, :], 0.0, dt_e[0:nh, :], ALU.min, ALU.subtract))
            link(dve.tensor_tensor_scan(acs[0:nh, 0:P], ones[0:nh, :], dt[0:nh, 0:P], 0.0, ALU.mult, ALU.add))
            link(dve.tensor_tensor_scan(acs[0:nh, P:T], ones[0:nh, :], dt[0:nh, P:T], acs[0:nh, P - 1:P], ALU.mult, ALU.add))
            link(ts(cum_neg[0:nh, :], acs[0:nh, :], -1.0, None, ALU.mult))
            go(ts(fox_g[:, 2:3], fox_g[:, 0:1], HEAD ** -0.5, None, ALU.mult))
            sync()
            dve.nop().then_inc(sem("cum_fox"), 1)
            for i, (t, g) in enumerate(((q_t, fox_g[:, 2:3]), (k_t, fox_g[:, 1:2]))):
                dve.wait_ge(sem("fox_root"), 4 * (i + 1))
                link(dve.reciprocal(tmp2, tmp2))
                link(stt(t, t, g, tmp2, ALU.mult, ALU.mult))
                dve.nop().then_inc(sem("qk_ready"), 1)
            dve.wait_ge(sem("cq_turned"), 1)
            link(dve.tensor_copy(tok_heads[:, 0:2, 0:nh], pb[3][:, 0:2 * nh].rearrange("p (c h) -> p c h", c=2)))
            for i in range(4):
                dve.wait_ge(sem("v_fox_turned"), i + 1)
                dve.tensor_copy(v_tok[:, i // 2, 512 * (i % 2):512 * (i % 2) + 512], pb[4 + i][:, :]).then_inc(sem("v_fox_ready"), 1)
            dve.wait_ge(sem("fox_mask_ready"), 1)
            steps = 2 * nh
            for i in range(steps + 3):
                if i < steps:
                    h, qc = divmod(i, 2)
                    n, s = (qc + 1) * P, i % NS
                    dve.wait_ge(sem("score_done"), i + 1)
                    if i >= NS:
                        dve.wait_ge(sem("turned"), i - NS + 1)
                    stt(sc[s][:, 1, 0:n], pb[i % 2][:, 0:n], tok_heads[:, qc, h:h + 1], fox_mask[:, T - n:T],
                        ALU.add, ALU.add).then_inc(sem("masked"), 1)
                    dve.wait_ge(sem("masked"), i + 1)
                    link(dve.tensor_reduce(fox_stat[:, 6, h:h + 1], sc[s][:, 1, 0:n], AX_X, ALU.max))
                    ts(fox_stat[:, 2 * qc, h:h + 1], fox_stat[:, 6, h:h + 1], -1.0, None, ALU.mult).then_inc(sem("max_ready"), 1)
                if 1 <= i <= steps:
                    h, qc = divmod(i - 1, 2)
                    dve.wait_ge(sem("exp_ready"), i)
                    dve.reciprocal(fox_stat[:, 4 + qc, h:h + 1], fox_stat[:, 2 * qc + 1, h:h + 1]).then_inc(sem("share_ready"), 1)
                if 2 <= i < steps + 2:
                    j = i - 2
                    n, s = (j % 2 + 1) * P, j % NS
                    dve.wait_ge(sem("turned"), j + 1)
                    if j >= NS:
                        dve.wait_ge(sem("pv_done"), j - NS + 1)
                    dve.tensor_copy(pt[s][:, 0:n], pb[2 + j % 2][:, 0:n]).then_inc(sem("pt_ready"), 1)
                if i >= 3 and (i - 3) % 4 == 3:
                    m = (i - 3) // 4
                    dve.wait_ge(sem("pv_done"), 4 * (m + 1))
                    dve.wait_ge(sem("fox_gate"), 1)
                    tt(o_fox[:, m, :], pb[4 + m % 2][:, 0:T], gate_t[:, m, :], ALU.mult).then_inc(sem("o_ready"), 1)
            ahead(dve_rest, dve, L["fox_out"])
            for k in range(KC):
                dve.wait_ge(sem("x_hi_ready"), X_BASE["fox"] + k + 1)
                tt(x_lo[:, k, :], o_fox[:, k, :], x_hi[:, k, :].bitcast(F32), ALU.subtract).then_inc(sem("x_lo_ready"), 1)
            dve_layer(dve, L["fox_out"], residual)
            ahead(dve_rest, dve, L["up2"])
            norm_begin(5)
            ffn(2, L["up2"], L["down2"], residual)
            dve.wait_ge(sem("x_ready"), KC * 7)
            norm_scale(6)
            for k in range(KC):
                stt(tile(16, k), x_res[:, k, :], par_col("final_norm_g_2", k), rstd[:, :], ALU.mult, ALU.mult).then_inc(sem("y_ready"), 1)
            for i in range(4):
                c, b = divmod(i, 2)
                dve.wait_ge(sem("y_turned"), i + 1)
                dve.tensor_copy(y_tok[:, c, 512 * b:512 * b + 512], pb[3 + i][:, :]).then_inc(sem("y_tok_ready"), 1)

        @block.tensor
        def _(pe):
            mm = pe.matmul

            def sum_squares(n, bank=7):
                for k in range(KC):
                    pe.wait_ge(sem("sq_ready"), KC * n + k + 1)
                    ins = mm(pb[bank][:, 0:T], ones[:, :], sub[:, k, :], start=k == 0, stop=k == KC - 1)
                ins.then_inc(sem("ssq_done"), 1)

            def head_sums(src, bank0=4):
                for k in range(KC):
                    ins = mm(pb[bank0 + k // 2][:, T * (k % 2):T * (k % 2) + T], blk[:, :], src[:, k, :], start=True, stop=True)
                return ins

            def turn(o, i):
                n = i.shape[0]
                return pe.transpose(o, i, ident[0:n, 0:n])

            for i in range(BANKS):
                pe.nop().then_inc(sem("block_done"), 1)
            pe.wait_ge(sem("const_ready"), 1)
            pe.wait_ge(sem("par_loaded"), 16 * par_dmas)
            for t in range(par_tiles):
                n = min(P, n_rows - P * t)
                ins = turn(pb[1 + t // 4][:, P * (t % 4):P * (t % 4) + n], par_tok[0:n, t, :])
                if t % 4 == 3 or t == par_tiles - 1:
                    ins.then_inc(sem("par_turned"), 1)
            pe.wait_ge(sem("x_loaded"), 16)
            for k in range(KC):
                for c in range(2):
                    ins = turn(pb[3 + k // 2][:, T * (k % 2) + P * c:T * (k % 2) + P * c + P], x_tok[:, c, P * k:P * k + P])
                if k % 2:
                    ins.then_inc(sem("x_turned"), 1)
            sum_squares(0)
            pe_layer(pe, L["rkv"], x_hi, x_lo, "x_lo_ready", X_BASE[0])

            s = L["lora_in"].u0 % 2
            pe.wait_ge(sem(f"landed{s}"), L["lora_in"].landed[0])
            for i, (c, n, src) in enumerate(((0, 64, KK), (64, 64, A), (128, 128, G))):
                pe.wait_ge(sem("lora_x"), KC * (i + 1))
                for k in range(KC):
                    ins = mm(pb[4 + i][0:n, 0:T], raw[s][:, k, c:c + n], slot(src)[:, k, :], start=k == 0, stop=k == KC - 1)
                ins.then_inc(sem("lora1_done"), 1)
            s = L["lora_out"].u0 % 2
            pe.wait_ge(sem(f"landed{s}"), L["lora_out"].landed[0])
            w2 = raw[s][:, :, :].rearrange("p k n -> p (k n)")
            for f, (rows, src) in enumerate(((64, lora_w), (64, lora_a), (128, lora_g))):
                pe.wait_ge(sem("lora_mid"), 3)
                for j in range(4):
                    i = 4 * f + j
                    if i >= 3:
                        pe.wait_ge(sem("lora_ready"), i - 2)
                    for m in (2 * j, 2 * j + 1):
                        ins = mm(pb[4 + i % 3][:, T * (m % 2):T * (m % 2) + T], w2[0:rows, D * f + P * m:D * f + P * m + P], src,
                                 start=True, stop=True)
                    ins.then_inc(sem("lora2_done"), 1)
            pe.wait_ge(sem("lora_ready"), 12)
            pe.wait_ge(sem("kk_sq"), 1)
            head_sums(slot(TMP)).then_inc(sem("kk_sum"), 1)
            pe.wait_ge(sem("bonus_in"), 1)
            pe.wait_ge(sem("evac_done"), L["rkv"].evac1 + BANKS)
            for k in range(KC):
                ins = mm(pb[3][0:RWKV_HEADS, 0:T], head_sel[:, k, :], tmp2[:, k, :], start=k == 0, stop=k == KC - 1)
            ins.then_inc(sem("bonus_done"), 1)
            pe.wait_ge(sem("scan_in"), 1)
            for c in range(NCHUNK):
                if c >= 2:
                    pe.wait_ge(sem("lab_ready"), c - 1)
                for h in range(RWKV_HEADS):
                    m, rows = h // 2, slice(64 * (h % 2), 64 * (h % 2) + 64)
                    ins = mm(pb[4 + 2 * (h % 2) + c % 2][0:CHUNK, CHUNK * m:CHUNK * m + CHUNK], bk[rows, m, c, 1, :],
                             slot(KK)[rows, m, CHUNK * c:CHUNK * c + CHUNK], start=True, stop=True)
                ins.then_inc(sem("lab_done"), 1)
            pe_layer(pe, L["ug"], x_hi, x_lo, "x_lo_ready", X_BASE[0])
            pe_layer(pe, L["z"], x_hi, x_lo, "x_lo_ready", X_BASE[0])

            def chunk_products(c):
                if c:
                    pe.wait_ge(sem("bk_rows"), c)
                    pe.wait_ge(sem("v_rows"), c)
                t = slice(CHUNK * c, CHUNK * c + CHUNK)
                for h in range(RWKV_HEADS):
                    m, rows = h // 2, slice(64 * (h % 2), 64 * (h % 2) + 64)
                    ins = mm(pb[h % 2][64:128, 64 * m:64 * m + 64], bk[rows, m, c, :, :].rearrange("p j s -> p (j s)"),
                             pj4[rows, 0:KK + 1:KK, m, t], start=True, stop=True)
                ins.then_inc(sem("g_done"), 1)
                for m in range(KC):
                    ins = turn(pb[2 + m // 4][0:CHUNK, P * (m % 4):P * (m % 4) + P], slot(V)[:, m, t])
                ins.then_inc(sem("v_turned"), 1)

            def chunk_keys(c):
                pe.wait_ge(sem("g_masked"), c + 1)
                pe.wait_ge(sem("bk_scaled"), c + 1)
                for m in range(KC):
                    ins = turn(pb[m // 4][0:64, P * (m % 4):P * (m % 4) + P], bk[:, m, c, :, :].rearrange("p j s -> p (j s)"))
                ins.then_inc(sem("bk_turned"), 1)

            pe.wait_ge(sem("evac_done"), L["z"].evac1 + BANKS)
            pe.wait_ge(sem("conv_ready"), 1)
            chunk_products(0)
            chunk_keys(0)
            pe.wait_ge(sem("sub_dma"), 64)
            for c in range(NCHUNK):
                t, q = slice(CHUNK * c, CHUNK * c + CHUNK), c % 2
                pe.wait_ge(sem("v_rows"), c + 1)
                pe.wait_ge(sem("g_masked"), c + 1)
                if c:
                    pe.wait_ge(sem("u_rows_v"), c)
                    pe.wait_ge(sem("u_rows_a"), c)
                for h in range(RWKV_HEADS):
                    mm(pb[4 + h // 8][0:CHUNK, 64 * (h % 8):64 * (h % 8) + 64], g_buf[q][0:CHUNK, h, CHUNK:2 * CHUNK],
                       uv[q][0:CHUNK, 64 * h:64 * h + 64], start=h % 8 == 0, stop=False, skip_group_check=True)
                pe.wait_ge(sem("state_ready"), c + 1)
                for m in range(KC):
                    ins = mm(pb[4 + m // 4][0:CHUNK, P * (m % 4):P * (m % 4) + P], slot(KK)[:, m, t], state[:, m, :],
                             start=False, stop=m % 4 == 3, skip_group_check=True)
                ins.then_inc(sem("x_done"), 1)
                if c:
                    pe.wait_ge(sem("y_out"), c)
                for m in range(KC):
                    ins = mm(pb[7][:, CHUNK * m:CHUNK * m + CHUNK], state[:, m, :], slot(R)[:, m, t],
                             start=m == 0, stop=False, skip_group_check=True)
                ins.then_inc(sem("y1_done"), 1)
                if c + 1 < NCHUNK:
                    chunk_products(c + 1)
                pe.wait_ge(sem("x_rows_v"), c + 1)
                pe.wait_ge(sem("x_rows_a"), c + 1)
                for h in range(RWKV_HEADS):
                    ins = mm(pb[4 + h // 8][0:CHUNK, 64 * (h % 8):64 * (h % 8) + 64], lab_t[:, 16 * c + h, :],
                             x_buf[:, 64 * h:64 * h + 64], start=True, stop=True)
                ins.then_inc(sem("u_done"), 1)
                if c + 1 < NCHUNK:
                    chunk_keys(c + 1)
                pe.wait_ge(sem("u_rows_v"), c + 1)
                pe.wait_ge(sem("u_rows_a"), c + 1)
                pe.wait_ge(sem("bk_rows"), c + 1)
                if c + 1 < NCHUNK:
                    for h in range(RWKV_HEADS):
                        ins = mm(pb[6][64 * (h % 2):64 * (h % 2) + 64, 64 * (h // 2):64 * (h // 2) + 64],
                                 bk_t[q][:, 64 * h:64 * h + 64], uv[q][:, 64 * h:64 * h + 64], start=True, stop=True)
                    ins.then_inc(sem("s_done"), 1)
                for h in range(RWKV_HEADS):
                    ins = mm(pb[7][64 * (h % 2):64 * (h % 2) + 64, CHUNK * (h // 2):CHUNK * (h // 2) + CHUNK],
                             uv[q][:, 64 * h:64 * h + 64], g_buf[q][:, h, 0:CHUNK], start=False, stop=h >= 14, skip_group_check=True)
                ins.then_inc(sem("y2_done"), 1)
            pe.wait_ge(sem("y_out"), NCHUNK)
            head_sums(slot(R)).then_inc(sem("gn_mean"), 1)
            pe.wait_ge(sem("gn_sq"), 1)
            head_sums(tmp2).then_inc(sem("gn_var"), 1)
            pe.wait_ge(sem("gn_root"), 4)
            pe.wait_ge(sem("bonus_ready"), 1)
            for h in range(RWKV_HEADS):
                m = h // 2
                ins = mm(pb[4 + m // 2][64 * (h % 2):64 * (h % 2) + 64, T * (m % 2):T * (m % 2) + T],
                         ident[0:RWKV_HEADS, h:h + 1].broadcast_to([RWKV_HEADS, 64]), bonus, start=True, stop=True)
            ins.then_inc(sem("bonus_out"), 1)
            pe.wait_ge(sem("gn_out"), 1)
            for i, (src, done) in enumerate(((slot(GATE), "ln_mean"), (tmp2, "ln_var"))):
                if i:
                    pe.wait_ge(sem("ln_sq"), 1)
                for k in range(KC):
                    ins = mm(pb[4 + i][:, 0:T], ones[:, :], src[:, k, :], start=k == 0, stop=k == KC - 1)
                ins.then_inc(sem(done), 1)
            for i, ly in enumerate(("conv_out", "rwkv_out", "w_out")):
                pe_layer(pe, L[ly], x_hi, x_lo, "x_lo_ready", KC * (i + 1))

            def post_squares(i):
                for k in range(KC):
                    pe.wait_ge(sem("osq_ready"), KC * i + k + 1)
                    ins = mm(pb[7][:, 0:T], ones[:, :], sub[:, k, :], start=k == 0, stop=k == KC - 1)
                ins.then_inc(sem("osum_done"), 1)

            post_squares(0)
            sum_squares(1)
            pe_layer(pe, L["up0"], x_hi, x_lo, "x_lo_ready", X_BASE[1])
            pe_layer(pe, L["down0"], act_hi, act_lo, "act_lo_ready", 0)
            post_squares(1)
            sum_squares(2)

            def narrow_product(ly, n, which, done):
                s = ly.u0 % 2
                pe.wait_ge(sem(f"landed{s}"), ly.landed[0])
                pe.wait_ge(sem(which), KC)
                for k in range(KC):
                    ins = mm(pb[4][0:n, 0:T], raw[s][:, k, 0:n], x_gain[:, k, :], start=k == 0, stop=k == KC - 1)
                ins.then_inc(sem(done), 1)

            pe_layer(pe, L["ssd_z"], x_hi, x_lo, "x_lo_ready", X_BASE[2])
            pe_layer(pe, L["ssd_xbc"], x_hi, x_lo, "x_lo_ready", X_BASE[2])
            narrow_product(L["ssd_dt"], SSD_HEADS, "dt_in", "dt_done")
            pe.wait_ge(sem("xbc_ready"), M_PER_UNIT + SSD_XBC)
            for c in range(2):
                t = slice(P * c, P * c + P)
                for g in range(SSD_GROUPS):
                    ins = mm(pb[6 + c][:, P * g:P * g + P], xbc[:, 16 + g, t], xbc[:, 20 + g, t], start=True, stop=True)
                ins.then_inc(sem("cb_done"), 1)
            for g in range(SSD_GROUPS):
                ins = turn(pb[5][:, P * g:P * g + P], xbc[:, 16 + g, 0:P])
            ins.then_inc(sem("b_turned"), 1)
            pe.wait_ge(sem("da_ready"), 1)
            for i, src in enumerate((acs[:, 0:P], acs[:, P:T], dt[:, 0:P], dt[:, P:T], da_end)):
                ins = turn(pb[4][:, SSD_HEADS * i:SSD_HEADS * i + SSD_HEADS], src)
            ins.then_inc(sem("heads_turned"), 1)
            pe.wait_ge(sem("cbm_ready"), 2)
            for i in range(8):
                c, b = divmod(i, 4)
                if i >= 2:
                    pe.wait_ge(sem("xdt_ready"), i - 1)
                for r in range(4):
                    ins = turn(pb[6 + i % 2][:, P * r:P * r + P], xbc[:, 4 * b + r, P * c:P * c + P])
                ins.then_inc(sem("xs_turned"), 1)
            pe.wait_ge(sem("heads_ready"), 1)
            pe.wait_ge(sem("b_tok_ready"), 1)

            def on_head(o, h, src):
                return mm(o, ident[0:SSD_HEADS, h:h + 1].broadcast_to([SSD_HEADS, o.shape[0]]), src, start=True, stop=True)

            for b in range(4):
                if b >= 2:
                    pe.wait_ge(sem("eab_ready"), b - 1)
                for h in range(8 * b, 8 * b + 8):
                    m = h // 2
                    ins = on_head(pb[4 + b % 2][64 * (h % 2):64 * (h % 2) + 64, P * (m % 4):P * (m % 4) + P], h, da_exp)
                ins.then_inc(sem("eab_done"), 1)
            pe.wait_ge(sem("xdt_end_ready"), 1)
            pe.wait_ge(sem("xdt_ready"), 8)
            for g in range(SSD_GROUPS):
                if g >= 2:
                    pe.wait_ge(sem("st_ready"), g - 1)
                mm(pb[6 + g % 2][:, :], b_tok[:, g, :], xdt_end[:, 512 * g:512 * g + 512], start=True, stop=True).then_inc(sem("st_done"), 1)
            pe.wait_ge(sem("eab_ready"), 4)
            for b in range(4):
                pe.wait_ge(sem("st_ready"), b + 1)
                if b >= 2:
                    pe.wait_ge(sem("eab_used"), b - 1)
                for m in range(4 * b, 4 * b + 4):
                    ins = mm(pb[4 + b % 2][:, P * (m % 4):P * (m % 4) + P], st_ssd[:, P * m:P * m + P], xbc[:, 20 + b, P:T], start=True, stop=True)
                ins.then_inc(sem("yoff_done"), 1)
            pe.wait_ge(sem("evac_done"), L["ssd_xbc"].evac1 + BANKS)
            for i in range(17):
                if i < 16:
                    c, hq = divmod(i, 8)
                    if i >= 2:
                        pe.wait_ge(sem("diff_ready"), i - 1)
                    for r in range(4):
                        ins = on_head(pb[i % 2][:, P * r:P * r + P], 4 * hq + r, acs[:, P * c:P * c + P])
                    ins.then_inc(sem("bc_done"), 1)
                if i >= 1:
                    j = i - 1
                    c, hq = divmod(j, 8)
                    pe.wait_ge(sem("att_ready"), j + 1)
                    if j >= 2:
                        pe.wait_ge(sem("y_out_ssd"), j - 1)
                    for r in range(4):
                        h = 4 * hq + r
                        ins = mm(pb[2 + j % 2][64 * (h % 2):64 * (h % 2) + 64, P * (r // 2):P * (r // 2) + P],
                                 xdt[:, c, 64 * h:64 * h + 64], att[j % 2][:, r, :], start=True, stop=True)
                    ins.then_inc(sem("y_done"), 1)
            for g in range(SSD_GROUPS):
                pe.wait_ge(sem("yz_sq"), g + 1)
                for m in range(4):
                    ins = mm(pb[4 + g][:, 0:T], ones[:, :], sub[:, 4 * (g % 2) + m, :], start=m == 0, stop=m == 3)
                ins.then_inc(sem("yz_sum"), 1)
            pe.wait_ge(sem("y_out_ssd"), 16)
            pe_layer(pe, L["ssd_out"], yz_hi, yz_lo, "yz_lo_ready", 0)
            sum_squares(3)
            pe_layer(pe, L["up1"], x_hi, x_lo, "x_lo_ready", X_BASE[3])
            pe_layer(pe, L["down1"], act_hi, act_lo, "act_lo_ready", FC * 1)
            sum_squares(4)

            pe_layer(pe, L["fox_in"], x_hi, x_lo, "x_lo_ready", X_BASE[4])
            narrow_product(L["fox_f"], FOX_HEADS, "f_in", "f_done")
            pe.wait_ge(sem("evac_done"), L["fox_in"].evac1 + BANKS)
            pe.wait_ge(sem("cum_fox"), 1)
            for c in range(2):
                ins = turn(pb[3][:, FOX_HEADS * c:FOX_HEADS * c + FOX_HEADS], acs[0:FOX_HEADS, P * c:P * c + P])
            ins.then_inc(sem("cq_turned"), 1)
            for i in range(2):
                pe.wait_ge(sem("fox_sq"), i + 1)
                if i:
                    pe.wait_ge(sem("fox_root"), 4)
                head_sums(fox_tmp).then_inc(sem("fox_sum"), 1)
            pe.wait_ge(sem("fox_root"), 8)
            for i in range(4):
                for r in range(4):
                    m = 4 * (i % 2) + r
                    ins = turn(pb[4 + i][:, P * r:P * r + P], v_t[:, m, P * (i // 2):P * (i // 2) + P])
                ins.then_inc(sem("v_fox_turned"), 1)
            pe.wait_ge(sem("qk_ready"), 2)
            pe.wait_ge(sem("v_fox_ready"), 4)
            steps = 2 * FOX_HEADS
            for i in range(steps + 3):
                if i < steps:
                    h, qc = divmod(i, 2)
                    m, rows, n = h // 2, slice(64 * (h % 2), 64 * (h % 2) + 64), (qc + 1) * P
                    if i >= 2:
                        pe.wait_ge(sem("masked"), i - 1)
                    mm(pb[i % 2][:, 0:n], q_t[rows, m, P * qc:P * qc + P], k_t[rows, m, 0:n], start=True, stop=False)
                    mm(pb[i % 2][:, 0:n], ident[0:FOX_HEADS, h:h + 1].broadcast_to([FOX_HEADS, P]), cum_neg[0:FOX_HEADS, 0:n],
                       start=False, stop=True).then_inc(sem("score_done"), 1)
                if 2 <= i < steps + 2:
                    j = i - 2
                    pe.wait_ge(sem("p_ready"), j + 1)
                    if j >= 2:
                        pe.wait_ge(sem("pt_ready"), j - 1)
                    for b in range(j % 2 + 1):
                        ins = turn(pb[2 + j % 2][:, P * b:P * b + P], sc[j % NS][:, 0, P * b:P * b + P])
                    ins.then_inc(sem("turned"), 1)
                if i >= 3:
                    j = i - 3
                    h, qc = divmod(j, 2)
                    m = h // 2
                    pe.wait_ge(sem("pt_ready"), j + 1)
                    if m >= 2:
                        pe.wait_ge(sem("o_ready"), m - 1)
                    for b in range(qc + 1):
                        ins = mm(pb[4 + m % 2][64 * (h % 2):64 * (h % 2) + 64, P * qc:P * qc + P],
                                 v_tok[:, b, 64 * h:64 * h + 64], pt[j % NS][:, P * b:P * b + P], start=b == 0, stop=b == qc)
                    ins.then_inc(sem("pv_done"), 1)
            pe_layer(pe, L["fox_out"], x_hi, x_lo, "x_lo_ready", X_BASE["fox"])
            sum_squares(5)
            pe_layer(pe, L["up2"], x_hi, x_lo, "x_lo_ready", X_BASE[5])
            pe_layer(pe, L["down2"], act_hi, act_lo, "act_lo_ready", FC * 2)
            sum_squares(6)
            for i in range(4):
                c, b = divmod(i, 2)
                pe.wait_ge(sem("y_ready"), 4 * b + 4)
                for r in range(4):
                    ins = turn(pb[3 + i][:, P * r:P * r + P], tile(16, 4 * b + r)[:, P * c:P * c + P])
                ins.then_inc(sem("y_turned"), 1)


def kernel(**inputs):
    import numpy as _np
    import concourse.bacc as _bacc
    from concourse import mybir as _mybir
    from concourse.bass_utils import run_bass_kernel_spmd as _run

    nc = _bacc.Bacc("TRN2", target_bir_lowering=False, num_devices=1)
    arrays, args = {}, {}
    for name, value in inputs.items():
        v = _np.ascontiguousarray(value)
        if v.size == 0:
            continue
        arrays[f"in_{name}_dram"] = v
        args[name] = nc.dram_tensor(f"in_{name}_dram", v.shape, _mybir.dt.from_np(v.dtype), kind="ExternalInput").ap()
    out = nc.dram_tensor("out_0_dram", (1, T, D), F32, kind="ExternalOutput").ap()
    build(nc, args, out)
    r = _run(nc, [arrays], core_ids=[0])
    return r.results[0]["out_0_dram"]
```

```python
from contextlib import ExitStack

import concourse.bass as bass
from concourse import mybir

F32 = mybir.dt.float32
F32R = mybir.dt.float32r
ALU = mybir.AluOpType
ACT = mybir.ActivationFunctionType
AX_X = mybir.AxisListType.X

P = 128
T = 256
D = 1024
KC = D // P
FF = 2816
FC = FF // P
UNIT_COLS = 512
M_PER_UNIT = UNIT_COLS // P
LOOKAHEAD = 3
EXP_MINUS_HALF = 0.6065306597126334
RMS_EPS, LN_EPS, GN_EPS = 1e-6, 1e-5, 64e-5

RWKV_HEADS, HEAD = 16, 64
CHUNK = 32
NCHUNK = T // CHUNK
CONV_TAPS = 31
SSD_INNER, SSD_HEADS, SSD_GROUPS, SSD_TAPS = 2048, 32, 4, 4
SSD_Z, SSD_XBC = SSD_INNER // P, (SSD_INNER + 2 * SSD_GROUPS * P) // P
FOX_HEADS = 16
GLU_TAPS = 3
MASKED = -1e30


class Layer:

    def __init__(self, name, sources, nkc, k_split=1, dmas=1):
        self.name, self.sources, self.nkc, self.k_split, self.dmas = name, sources, nkc, k_split, dmas

    def __len__(self):
        return len(self.nkc)

    def first_k(self, u):
        g = u % self.k_split
        return sum(self.nkc[:g])


def params_of(a):
    out = []
    for name in ("pre_mix_norm", "post_mix_norm", "pre_ffn_norm", "post_ffn_norm", "mu_rkv", "mu_wag", "decay_w0",
                 "a_0", "k_k", "k_a", "r_k", "gn_w", "gn_b", "conv_dw", "conv_b", "conv_ln_w", "conv_ln_b",
                 "mix_norm_g_2", "ffn_norm_g_2", "ssd_conv_w_2", "ssd_conv_b_2", "ssd_norm_g_2",
                 "ffn_conv_w_2", "ffn_conv_b_2", "final_norm_g_2"):
        ap = a[name]
        names = " ".join(f"d{i}" for i in range(len(ap.shape)))
        flat = ap.rearrange(f"{names} -> ({names})")
        n = flat.shape[0] // P
        out.append((name, n, flat.rearrange("(n p) -> n p", p=P)))
    return out


def build(nc, a, out):
    ctx = ExitStack()
    with ctx:
        sems = {}

        def sem(name):
            if name not in sems:
                sems[name] = ctx.enter_context(nc.semaphore(name))
            return sems[name]

        def sb(name, shape, dt=F32):
            return ctx.enter_context(nc.sbuf_tensor(name, shape, dt))

        raw = [sb(f"raw{i}", [P, KC, UNIT_COLS]) for i in range(2)]
        w_hi = [sb(f"w_hi{i}", [P, KC, P], F32R) for i in range(M_PER_UNIT)]
        w_lo = [sb(f"w_lo{i}", [P, KC, P], F32R) for i in range(M_PER_UNIT)]
        x_res = sb("x_res", [P, KC, T])
        x_hi = sb("x_hi", [P, KC, T], F32R)
        x_lo = sb("x_lo", [P, KC, T], F32R)
        tap_base = nc.sbuf_base - 2 * KC * T * 4
        tap_prod = [nc.alloc_sbuf_tensor_at(f"tap_prod{i}", [P, KC, T], F32, offset=tap_base + i * KC * T * 4) for i in range(2)]
        sub_base = nc.sbuf_base
        sub = sb("sub", [P, 12, T])
        arena_base = nc.sbuf_base
        pj = sb("pj", [P, 96, T])
        ident = sb("ident", [P, P])
        ones = sb("ones", [P, P])
        blk = sb("blk", [P, P])
        tri = sb("tri", [P, P])
        later = sb("later", [P, P])
        scan_mask = sb("scan_mask", [P, T])
        g_mask = sb("g_mask", [P, 2 * CHUNK])
        head_sel = sb("head_sel", [P, KC, RWKV_HEADS])
        eps = sb("eps", [P, 3])
        rs = sb("rs", [P, T])
        rstd = sb("rstd", [P, T])
        small = sb("small", [SSD_HEADS, T])
        bonus = small[0:RWKV_HEADS, :]
        chunk_decay = sb("chunk_decay", [P, KC, NCHUNK])
        heads_col = sb("heads_col", [SSD_HEADS, 4])
        fox_g = sb("fox_g", [P, 4])
        d_skip = sb("d_skip", [P, SSD_Z])

        par_rows = params_of(a)
        col, n_rows = {}, 0
        for name, n, _ in par_rows:
            col[name] = n_rows
            n_rows += n
        par_tiles = -(-n_rows // P)
        par = sb("par", [P, n_rows])

        def slot(i):
            return pj[:, 8 * i:8 * i + 8, :]

        R, K, V, U, GATE, BK, KK, A, TMP, W, G = 0, 1, 2, 3, 4, 5, 7, 8, 9, 10, 11
        ZR, ZC, OUT1 = K, A, R
        mix_tmp, rate_tmp = slot(BK), slot(BK + 1)
        y_hi = nc.alloc_sbuf_tensor_at("y_hi", [P, KC, T], F32R, offset=arena_base + 8 * BK * T * 4)
        y_lo = nc.alloc_sbuf_tensor_at("y_lo", [P, KC, T], F32R, offset=arena_base + 8 * (BK + 1) * T * 4)
        POOL_TILES = 4
        DVE_EARLY = 7
        EARLY_TAPS = 3
        x_tok = pj[:, 40:48, :].rearrange("p a b -> p (a b)").rearrange("p (c d) -> p c d", c=2)
        par_tok = pj[:, 48:52, :].rearrange("p a b -> p (a b)")[:, 0:par_tiles * P].rearrange("p (t c) -> p t c", c=P)
        tmp2 = sub[:, 0:8, :]
        lora_w, lora_a, lora_g = sub[0:64, 8, :], sub[0:64, 9, :], sub[:, 10, :]
        bk = pj[:, 40:56, :].rearrange("p a b -> p (a b)").rearrange("p (k c j s) -> p k c j s", k=KC, c=NCHUNK, j=2)
        region = pj[:, 72:88, :].rearrange("p a b -> p (a b)")
        lab_t = region[0:CHUNK, :].rearrange("s (y t) -> s y t", t=CHUNK)
        g_buf = [region[64:128, 1024 * q:1024 * q + 1024].rearrange("p (h n) -> p h n", h=RWKV_HEADS) for q in range(2)]
        uv = [region[64:128, 2048 + 1024 * q:3072 + 1024 * q] for q in range(2)]
        flat_sub = sub[:, :, :].rearrange("p a b -> p (a b)")
        lt = flat_sub[:, 0:1024].rearrange("p (s t) -> p s t", t=CHUNK)
        mt = flat_sub[:, 1024:2048].rearrange("p (s t) -> p s t", t=CHUNK)
        prod = flat_sub[:, 2048:3072].rearrange("p (s t) -> p s t", t=CHUNK)
        bk_t = [flat_sub[64:128, 1024 * q:1024 * q + 1024] for q in range(2)]
        x_buf = flat_sub[0:CHUNK, 0:1024]
        state = flat_sub[:, 2048:3072].rearrange("p (m v) -> p m v", m=KC)
        act_hi = nc.alloc_sbuf_tensor_at("act_hi", [P, FC, T], F32R, offset=arena_base)
        act_lo = nc.alloc_sbuf_tensor_at("act_lo", [P, FC, T], F32R, offset=arena_base + FC * T * 4)
        OUT_FFN = 8
        g_tile = [sub[:, i, :] for i in (0, 1)]
        s_tile = [sub[:, i, :] for i in (2, 3)]
        u_tile = [sub[:, i, :] for i in (4, 5)]
        a_tile = [sub[:, i, :] for i in (6, 7)]
        c_tile = [sub[:, i, :] for i in (8, 9)]
        z_t, xbc, y_ssd = pj[:, 0:16, :], pj[:, 16:40, :], pj[:, 40:56, :]
        x_gain = pj[:, 40:48, :]
        z_sig = pj[:, 56:72, :]
        xdt = pj[:, 56:72, :].rearrange("p a b -> p (a b)").rearrange("p (c f) -> p c f", c=2)
        xdt_end = pj[:, 72:80, :].rearrange("p a b -> p (a b)")
        NATT = 4
        att = [pj[:, t:t + 2, :].rearrange("p a b -> p (a b)").rearrange("p (h l) -> p h l", l=P) for t in (80, 82, 72, 74)]
        seg = [pj[:, t:t + 2, :].rearrange("p a b -> p (a b)") for t in (76, 78)]
        cbm = pj[:, 84:88, :].rearrange("p a b -> p (a b)").rearrange("p (c g l) -> p c g l", c=2, g=SSD_GROUPS)
        st_ssd = pj[:, 88:96, :].rearrange("p a b -> p (a b)")
        conv_in = [sub[:, i, :] for i in range(4)]
        conv_sig = [sub[:, 4 + i, :] for i in range(4)]
        dt_z, dt_e, dt, acs = (sub[0:SSD_HEADS, i, :] for i in (8, 9, 10, 11))
        tok_heads = sb("tok_heads", [P, 5, SSD_HEADS])
        da_end, da_exp = small[:, 0:P], small[:, P:T]
        eab = sub[:, 0:8, :].rearrange("p a b -> p (a b)").rearrange("p (m l) -> p m l", l=P)
        b_tok = x_gain[:, 0:2, :].rearrange("p a b -> p (a b)").rearrange("p (g n) -> p g n", g=SSD_GROUPS)
        yz_hi = nc.alloc_sbuf_tensor_at("yz_hi", [P, SSD_Z, T], F32R, offset=arena_base + 56 * T * 4)
        yz_lo = nc.alloc_sbuf_tensor_at("yz_lo", [P, SSD_Z, T], F32R, offset=arena_base + 16 * T * 4)
        q_t, k_t, v_t, gate_t = (pj[:, 8 * i:8 * i + 8, :] for i in range(4))
        fox_tmp = pj[:, 32:40, :]
        v_tok = pj[:, 48:56, :].rearrange("p a b -> p (a b)").rearrange("p (c f) -> p c f", c=2)
        NS = 4
        score_banks = (0, 1, 6, 7)
        sc = [pj[:, 56 + 2 * i:58 + 2 * i, :] for i in range(NS)]
        pt = [pj[:, 64 + 2 * i:66 + 2 * i, :].rearrange("p a b -> p (a b)") for i in range(NS)]
        o_fox = pj[:, 72:80, :]
        fox_stat = pj[:, 80, :].rearrange("p (s h) -> p s h", h=FOX_HEADS)
        fox_mask = pj[:, 81, :]
        pj4 = pj[:, :, :].rearrange("p (s k) t -> p s k t", k=KC)
        y_tok = pj[:, 0:8, :].rearrange("p a b -> p (a b)").rearrange("p (c d) -> p c d", c=2)
        cum_neg = dt_z

        pb = [ctx.enter_context(nc.psum_tensor(f"pb{i}", [P, 512], F32)) for i in range(8)]
        sub_in = nc.dram_tensor("sub_in", [CHUNK, P, CHUNK], F32, kind="Internal").ap()
        sub_out = nc.dram_tensor("sub_out", [P, CHUNK, CHUNK], F32, kind="Internal").ap()

        def cols(ap, first, n=UNIT_COLS):
            v = ap.rearrange("(k p) n -> p k n", p=P)
            return lambda u: [(slice(0, n), v[:, :, bass.ds(first + n * u, n)])]

        def gate_up(g, up):
            h = UNIT_COLS // 2
            gv, uv_ = g.rearrange("(k p) n -> p k n", p=P), up.rearrange("(k p) n -> p k n", p=P)
            return lambda u: [(slice(0, h), gv[:, :, bass.ds(h * u, h)]), (slice(h, 2 * h), uv_[:, :, bass.ds(h * u, h)])]

        def k_split(ap, nkc, parts):
            v = ap.rearrange("(k p) n -> p k n", p=P)

            def source(u):
                k0 = sum(nkc[:u % parts])
                n0 = UNIT_COLS * (u // parts)
                return [(slice(0, UNIT_COLS), v[:, k0:k0 + nkc[u % parts], n0:n0 + UNIT_COLS])]
            return source

        w_in = a["w_in"][0]
        down_kc = [8, 7, 7]
        up2, down2 = a["ffn_w_up_2"], a["ffn_w_down_2"]
        L = {}
        order = []

        def layer(name, sources, nkc, **kw):
            L[name] = Layer(name, sources, nkc, **kw)
            order.append(L[name])

        def lora_in(u):
            return [(slice(0, 64), a["decay_w1"][0].rearrange("(k p) n -> p k n", p=P)),
                    (slice(64, 128), a["a_1"][0].rearrange("(k p) n -> p k n", p=P)),
                    (slice(128, 256), a["g_1"][0].rearrange("(k p) n -> p k n", p=P))]

        def narrow(ap, first, n):
            return lambda u: [(slice(0, n), ap.rearrange("(k p) n -> p k n", p=P)[:, :, first:first + n])]

        layer("rkv", cols(w_in, 0), [KC] * 6)
        layer("lora_in", lora_in, [KC], dmas=3)
        layer("lora_out", None, [KC], dmas=3)
        layer("ug", cols(w_in, 3 * D), [KC] * 4)
        layer("z", cols(w_in, 5 * D), [KC] * 4)
        layer("conv_out", cols(a["w_conv_out"][0], 0), [KC] * 2)
        layer("rwkv_out", cols(a["w_rwkv_out"][0], 0), [KC] * 2)
        layer("w_out", cols(a["w_out"][0], 0), [KC] * 2)
        layer("up0", gate_up(a["ffn_w_gate"][0], a["ffn_w_up"][0]), [KC] * 11, dmas=2)
        layer("down0", k_split(a["ffn_w_down"][0], down_kc, 3), down_kc * 2, k_split=3)
        layer("ssd_z", cols(a["ssd_w_in_2"][0], 0), [KC] * 4)
        layer("ssd_xbc", cols(a["ssd_w_in_2"][0], SSD_INNER), [KC] * 6)
        layer("ssd_dt", narrow(a["ssd_w_in_2"][0], 5120, SSD_HEADS), [KC])
        layer("ssd_out", k_split(a["ssd_w_out_2"][0], [8, 8], 2), [8, 8] * 2, k_split=2)
        layer("up1", gate_up(up2[0][:, 0:FF], up2[0][:, FF:2 * FF]), [KC] * 11, dmas=2)
        layer("down1", k_split(down2[0], down_kc, 3), down_kc * 2, k_split=3)
        layer("fox_qk", cols(a["fox_w_in_2"][0], 0), [KC] * 4)
        layer("fox_f", narrow(a["fox_w_in_2"][0], 4 * D, FOX_HEADS), [KC])
        layer("fox_vg", cols(a["fox_w_in_2"][0], 2 * D), [KC] * 4)
        layer("fox_out", cols(a["fox_w_out_2"][0], 0), [KC] * 2)
        layer("up2", gate_up(up2[1][:, 0:FF], up2[1][:, FF:2 * FF]), [KC] * 11, dmas=2)
        layer("down2", k_split(down2[1], down_kc, 3), down_kc * 2, k_split=3)
        special = {"lora_in": ("lora1_done", 3), "lora_out": ("lora2_done", 12), "ssd_dt": ("narrow_done", 1), "fox_f": ("narrow_done", 2)}
        landed = [0, 0]
        unit, item, evac = 0, 0, 0
        occupant = [None, None]
        for ly in order:
            ly.u0, ly.item0, ly.evac0 = unit, item, evac
            ly.landed, ly.free = [], []
            for u in range(len(ly)):
                s = unit % 2
                landed[s] += 16 * ly.dmas
                ly.landed.append(landed[s])
                ly.free.append(occupant[s])
                unit += 1
                if ly.name in special:
                    occupant[s] = special[ly.name]
                else:
                    item += M_PER_UNIT
                    occupant[s] = ("w_lo_ready", item)
                    if u % ly.k_split == ly.k_split - 1:
                        evac += M_PER_UNIT
            ly.item1, ly.evac1 = item, evac

        def units(eng, ly, body, lead=0):
            n = len(ly)
            pairs = (n - lead - 2) // 2 if n >= 6 and ly.k_split == 1 else 0
            for u in range(lead if pairs else 0):
                body(u, u % 2, False)
            if pairs:
                with eng.Fori(lead // 2, lead // 2 + pairs) as i:
                    for p in range(2):
                        body(2 * i + p, p, False)
            for u in range(lead + 2 * pairs if pairs else 0, n):
                body(u, u % 2, u == n - 1)

        def nth(ly, u, p, table):
            return table[u] if isinstance(u, int) else table[p] + (u - p) * ((table[p + 2] - table[p]) // 2)

        BANKS = M_PER_UNIT

        def pe_layer(pe, ly, hi, lo, in_ready, in_base, hook=None):
            def body(u, p, last):
                part = u % ly.k_split if isinstance(u, int) else 0
                k0, nk = (ly.first_k(u), ly.nkc[u]) if isinstance(u, int) else (0, KC)
                first, final = part == 0, part == ly.k_split - 1
                group = u // ly.k_split if isinstance(u, int) else u
                for m in range(M_PER_UNIT):
                    pe.wait_ge(sem("w_lo_ready"), ly.item0 + M_PER_UNIT * u + m + 1)
                    if first:
                        pe.wait_ge(sem("evac_done"), ly.evac0 + M_PER_UNIT * group + m + 1)
                    if isinstance(u, int) and u < ly.k_split and m == 0:
                        pe.wait_ge(sem(in_ready), in_base + k0 + nk)
                    for k in range(nk):
                        o = pb[m][:, 0:T]
                        pe.matmul(o, w_hi[m][:, k, :], hi[:, k0 + k, :], start=first and k == 0, stop=False)
                        pe.matmul(o, w_hi[m][:, k, :], lo[:, k0 + k, :], start=False, stop=False)
                        mm = pe.matmul(o, w_lo[m][:, k, :], hi[:, k0 + k, :], start=False, stop=final and k == nk - 1)
                    mm.then_inc(sem("block_done"), 1)
                    if hook:
                        hook(u, m)
            pe.wait_ge(sem(in_ready), in_base + ly.nkc[0])
            units(pe, ly, body)

        def act_head(act, ly, u, p, m):
            s = (ly.u0 + p) % 2
            nk = ly.nkc[u] if isinstance(u, int) else KC
            if m == 0:
                act.wait_ge(sem(f"landed{s}"), nth(ly, u, p, ly.landed))
            act.wait_ge(sem("block_done"), ly.item0 + M_PER_UNIT * u + m + 1)
            act.activation(w_hi[m][:, 0:nk, :], raw[s][:, 0:nk, m * P:(m + 1) * P], ACT.Copy).then_inc(sem("w_hi_ready"), 1)

        def dve_rest(dve, ly, u, p, m):
            s = (ly.u0 + p) % 2
            nk = ly.nkc[u] if isinstance(u, int) else KC
            dve.wait_ge(sem("w_hi_ready"), ly.item0 + M_PER_UNIT * u + m + 1)
            dve.tensor_tensor(w_lo[m][:, 0:nk, :], raw[s][:, 0:nk, m * P:(m + 1) * P], w_hi[m][:, 0:nk, :].bitcast(F32),
                              ALU.subtract).then_inc(sem("w_lo_ready"), 1)

        def ahead(split, eng, ly):
            for m in range(LOOKAHEAD):
                split(eng, ly, 0, 0, m)

        def split_next(split, eng, ly, u, p, m, last):
            if m + LOOKAHEAD < M_PER_UNIT:
                split(eng, ly, u, p, m + LOOKAHEAD)
            elif not last:
                split(eng, ly, u + 1, (p + 1) % 2, m + LOOKAHEAD - M_PER_UNIT)

        def act_layer(act, ly, hook=None, lead=0):
            def body(u, p, last):
                for m in range(M_PER_UNIT):
                    split_next(act_head, act, ly, u, p, m, last)
                    if hook:
                        hook(u, m)
            units(act, ly, body, lead)

        def dve_layer(dve, ly, out_block, hook=None, rest_last=False):
            def body(u, p, last):
                for m in range(M_PER_UNIT):
                    if not rest_last:
                        split_next(dve_rest, dve, ly, u, p, m, last)
                    if not isinstance(u, int) or u % ly.k_split == ly.k_split - 1:
                        dve.wait_ge(sem("block_done"), ly.item0 + M_PER_UNIT * u + m + 1 + BANKS)
                        out_block(u // ly.k_split if isinstance(u, int) else u, m)
                    if rest_last:
                        split_next(dve_rest, dve, ly, u, p, m, last)
                    if hook:
                        hook(u, m)
            units(dve, ly, body)

        def par_col(name, i):
            c = col[name]
            return par[:, c + i:c + i + 1] if isinstance(i, int) else par[:, bass.ds(c + i, 1)]

        def tile(base, i):
            return pj[:, base + i, :]

        class Chain:

            def __init__(self, eng, name):
                self.eng, self.sem, self.n = eng, sem(name), 0

            def go(self, ins):
                ins.then_inc(self.sem, 1)
                self.n += 1

            def sync(self):
                self.eng.wait_ge(self.sem, self.n)

            def link(self, ins):
                self.go(ins)
                self.sync()

        X_BASE = {0: 0, 1: 4 * KC, 2: 5 * KC, 3: 6 * KC, 4: 7 * KC, "fox": 8 * KC, 5: 9 * KC}
        par_dmas = sum(1 + (col[n] + r - 1) // P - col[n] // P for n, r, _ in par_rows)
        NORMS = [("pre_mix_norm", 0), ("pre_ffn_norm", 0), ("mix_norm_g_2", 0), ("ffn_norm_g_2", 0),
                 ("mix_norm_g_2", KC), ("ffn_norm_g_2", KC)]
        block = ctx.enter_context(nc.Block())


        @block.sync
        def _(sp):
            sp.dma_start(x_tok, a["x"][0].rearrange("(c p) d -> p c d", p=P)).then_inc(sem("x_loaded"), 16)
            for ly in order:
                s0 = ly.u0 % 2
                if ly.name == "lora_out":
                    sp.wait_ge(sem(ly.free[0][0]), ly.free[0][1])
                    flat = raw[s0][:, :, :].rearrange("p k n -> p (k n)")
                    for i, (n, rows) in enumerate((("decay_w2", 64), ("a_2", 64), ("g_2", 128))):
                        sp.dma_start(flat[0:rows, D * i:D * i + D], a[n][0]).then_inc(sem(f"landed{s0}"), 16)
                    continue

                def body(u, p, last):
                    s = (ly.u0 + p) % 2
                    nk = KC
                    if isinstance(u, int):
                        nk = ly.nkc[u]
                        if ly.free[u]:
                            sp.wait_ge(sem(ly.free[u][0]), ly.free[u][1])
                    else:
                        sp.wait_ge(sem("w_lo_ready"), ly.item0 + M_PER_UNIT * (u - 1))
                    for c, src in ly.sources(u):
                        sp.dma_start(raw[s][:, 0:nk, c], src).then_inc(sem(f"landed{s}"), 16)
                if ly is order[0]:
                    for u in range(len(ly)):
                        body(u, u % 2, False)
                else:
                    units(sp, ly, body)
            for c in range(2):
                sp.wait_ge(sem("y_tok_ready"), 2 * (c + 1))
                sp.dma_start(out[0, c * P:(c + 1) * P, :], y_tok[:, c, :]).then_inc(sem("out_done"), 16)
            sp.wait_ge(sem("out_done"), 32)

        @block.gpsimd
        def _(pool):
            ch = Chain(pool, "pool_chain")
            go, sync, link = ch.go, ch.sync, ch.link

            go(pool.memset(ident[:, :], 0.0))
            go(pool.memset(tri[:, :], 1.0))
            go(pool.memset(blk[:, :], 0.0))
            go(pool.memset(scan_mask[:, :], 1.0))
            go(pool.memset(head_sel[:, :, :], 0.0))
            go(pool.memset(ones[:, :], 1.0))
            for i, e in enumerate((RMS_EPS, LN_EPS, GN_EPS)):
                go(pool.memset(eps[:, i:i + 1], e))
            sync()
            link(pool.affine_select(out=ident[:, :], in_=ident[:, :], compare_op=ALU.not_equal, fill=1.0, base=0,
                                  pattern=[[-1, P]], channel_multiplier=1))
            link(pool.affine_select(out=tri[:, :], in_=tri[:, :], compare_op=ALU.is_ge, fill=0.0, base=0,
                                  pattern=[[1, P]], channel_multiplier=-1))
            link(pool.tensor_tensor(later[:, :], ones[:, :], tri[:, :], ALU.subtract))
            for h in range(2):
                link(pool.memset(blk[64 * h:64 * h + 64, 64 * h:64 * h + 64], 1.0))
                link(pool.affine_select(out=head_sel[64 * h:64 * h + 64, :, :], in_=head_sel[64 * h:64 * h + 64, :, :],
                                      compare_op=ALU.not_equal, fill=1.0, base=-h,
                                      pattern=[[-2, KC], [1, RWKV_HEADS]], channel_multiplier=0))
            link(pool.memset(scan_mask[:, :].rearrange("p (c s) -> p c s", s=CHUNK)[:, :, 0:1], 0.0))
            sync()
            for b in range(4):
                rows = slice(32 * b, 32 * b + 32)
                link(pool.tensor_copy(g_mask[rows, 0:CHUNK], tri[rows, rows]))
                link(pool.tensor_tensor(g_mask[rows, CHUNK:2 * CHUNK], tri[rows, rows], ident[rows, rows], ALU.subtract))
            sync()
            pool.nop().then_inc(sem("const_ready"), 1)

            pool.wait_ge(sem("evac_done"), L["rkv"].evac1 + BANKS)
            v = slot(V)
            go(pool.tensor_tensor(tmp2[:, :, 1:T], v[:, :, 0:T - 1], v[:, :, 1:T], ALU.subtract))
            go(pool.tensor_scalar(tmp2[:, :, 0:1], v[:, :, 0:1], -1.0, None, ALU.mult))
            sync()
            mu_v = par[:, col["mu_rkv"] + 2 * KC:col["mu_rkv"] + 3 * KC].unsqueeze(2).broadcast_to([P, KC, T])
            link(pool.tensor_tensor(tmp2, tmp2, mu_v, ALU.mult))
            link(pool.tensor_tensor(v, v, tmp2, ALU.add))
            pool.wait_ge(sem("decay_ready"), 2)
            link(pool.tensor_tensor(slot(R), slot(R), slot(W), ALU.mult))
            pool.nop().then_inc(sem("pool_stages"), 1)

            pool.wait_ge(sem("gate_ready"), 1)
            link(pool.tensor_tensor(slot(U), slot(U), slot(GATE), ALU.mult))
            pool.nop().then_inc(sem("pool_stages"), 1)

            def conv_tap(s):
                o = slot(GATE)[:, 0:POOL_TILES, s:T]
                pool.wait_ge(sem("tap_ready"), s + 1)
                if s >= 2:
                    pool.wait_ge(sem("tap_summed"), s - 1)
                if s:
                    pool.tensor_tensor(o, o, tap_prod[s % 2][:, 0:POOL_TILES, 0:T - s], ALU.add).then_inc(sem("tap_summed"), 1)

            pool.wait_ge(sem("lab_ready"), NCHUNK)
            pool.wait_ge(sem("bonus_ready"), 1)
            pool.dma_start(sub_in, lab_t).then_inc(sem("sub_dma"), 16)
            pool.wait_ge(sem("sub_dma"), 16)
            pool.dma_start(lt, sub_in.rearrange("s y t -> y s t")).then_inc(sem("sub_dma"), 16)
            pool.wait_ge(sem("inverse_ready"), 1)
            pool.dma_start(sub_out, mt).then_inc(sem("sub_dma"), 16)
            pool.wait_ge(sem("sub_dma"), 48)
            pool.dma_start(lab_t, sub_out.rearrange("y j t -> j y t")).then_inc(sem("sub_dma"), 16)
            link(pool.memset(state, 0.0))
            pool.nop().then_inc(sem("pool_stages"), 1)
            for t in range(CONV_TAPS):
                conv_tap(t)

            def silu_tiles(ly, n):
                src = g_tile if n == 0 else c_tile

                def body(u, p, last):
                    for m in range(2):
                        pool.wait_ge(sem("glu_sig"), FC * n + 2 * u + m + 1)
                        pool.tensor_tensor(s_tile[m], s_tile[m], src[m], ALU.mult).then_inc(sem("silu_step"), 1)
                    for m in range(2):
                        pool.wait_ge(sem("silu_step"), FC * n + 2 * u + m + 1)
                        pool.tensor_tensor(s_tile[m], s_tile[m], rstd[:, :], ALU.mult).then_inc(sem("glu_silu"), 1)
                units(pool, ly, body)
            silu_tiles(L["up0"], 0)
            for u in range(len(L["ssd_z"])):
                q = slice(M_PER_UNIT * u, M_PER_UNIT * (u + 1))
                pool.wait_ge(sem("z_sig"), u + 1)
                pool.tensor_tensor(z_t[:, q, :], z_t[:, q, :], z_sig[:, q, :], ALU.mult).then_inc(sem("z_silu"), 1)
            ly = L["ssd_xbc"]
            for m in range(M_PER_UNIT):
                pool.nop().then_inc(sem("xbc_ready"), 1)

            def xbc_silu(u, p, last):
                for m in range(M_PER_UNIT):
                    j = 4 * u + m
                    t = xbc[:, j, :] if isinstance(u, int) else pj[:, bass.ds(SSD_Z + j, 1), :].rearrange("p a b -> p (a b)")
                    pool.wait_ge(sem("xbc_sig"), j + 1)
                    pool.tensor_tensor(t, t, conv_sig[m], ALU.mult).then_inc(sem("xbc_ready"), 1)
            units(pool, ly, xbc_silu)
            pool.wait_ge(sem("xdt_ready"), 4)
            pool.tensor_tensor(xdt_end.rearrange("p (h d) -> p h d", d=HEAD),
                               xdt[:, 0, :].rearrange("p (h d) -> p h d", d=HEAD),
                               tok_heads[:, 4, :].unsqueeze(2).broadcast_to([P, SSD_HEADS, HEAD]), ALU.mult).then_inc(sem("xdt_end_ready"), 1)
            pool.wait_ge(sem("st_done"), SSD_GROUPS)
            for i in range(16):
                c, hq = divmod(i, 8)
                if i >= 2:
                    pool.wait_ge(sem("bc_done"), i - 1)
                pool.tensor_tensor(seg[i % 2].rearrange("p (h l) -> p h l", l=P), tri[:, :].unsqueeze(1).broadcast_to([P, 4, P]),
                                   tok_heads[:, c, 4 * hq:4 * hq + 4].unsqueeze(2).broadcast_to([P, 4, P]), ALU.mult).then_inc(sem("seg_ready"), 1)
            silu_tiles(L["up1"], 1)
            pool.wait_ge(sem("fox_arena_free"), 1)
            link(pool.memset(fox_mask, 0.0))
            link(pool.affine_select(out=fox_mask[:, P:T], in_=fox_mask[:, P:T], compare_op=ALU.is_ge, fill=MASKED,
                                    base=0, pattern=[[-1, P]], channel_multiplier=1))
            pool.nop().then_inc(sem("fox_mask_ready"), 1)
            silu_tiles(L["up2"], 2)

        @block.scalar
        def _(act):
            ch = Chain(act, "act_chain")
            go, sync, link = ch.go, ch.sync, ch.link
            n = 0
            for name, rows, src in par_rows:
                c0, r0 = col[name], 0
                while r0 < rows:
                    t, p0 = divmod(c0 + r0, P)
                    m = min(rows - r0, P - p0)
                    act.dma_start(par_tok[p0:p0 + m, t, :], src[r0:r0 + m, :]).then_inc(sem("par_loaded"), 16)
                    n += 1
                    r0 += m
            assert n == par_dmas
            for i, name in enumerate(("ssd_dt_bias_2", "ssd_a_log_2")):
                act.dma_start(heads_col[:, i:i + 1], a[name][0].rearrange("(h a) -> h a", a=1)).then_inc(sem("small_loaded"), 16)
            act.dma_start(heads_col[0:FOX_HEADS, 2:3], a["fox_b_f_2"][0].rearrange("(h a) -> h a", a=1)).then_inc(sem("small_loaded"), 16)
            for h in range(2):
                for i, name in enumerate(("fox_q_norm_g_2", "fox_k_norm_g_2")):
                    act.dma_start(fox_g[64 * h:64 * h + 64, i:i + 1], a[name][0].rearrange("(d a) -> d a", a=1)).then_inc(sem("small_loaded"), 16)
                act.dma_start(d_skip[64 * h:64 * h + 64, :],
                              a["ssd_d_2"][0].rearrange("(m t a) -> t a m", t=2, a=1)[h].broadcast_to([64, SSD_Z]), allow_slow_non_contiguous=True).then_inc(sem("small_loaded"), 16)

            def norm_in(n):
                name, o = NORMS[n]
                for k in range(KC):
                    act.wait_ge(sem("x_ready"), KC * n + k + 1)
                    act.activation(sub[:, k, :], x_res[:, k, :], ACT.Square).then_inc(sem("sq_ready"), 1)
                    act.activation(x_hi[:, k, :], x_res[:, k, :], ACT.Copy, scale=par_col(name, o + k)).then_inc(sem("x_hi_ready"), 1)

            def norm_root(n, bank=7):
                act.wait_ge(sem("ssq_done"), n + 1)
                act.activation(rs[:, :], pb[bank][:, 0:T], ACT.Sqrt, bias=eps[:, 0:1], scale=1.0 / D).then_inc(sem("rs_ready"), 1)

            act.wait_ge(sem("const_ready"), 1)
            norm_in(0)
            ahead(act_head, act, L["rkv"])
            norm_root(0)
            act_layer(act, L["rkv"])
            act.wait_ge(sem("lora1_done"), 1)
            act.activation(lora_w, pb[4][0:64, 0:T], ACT.Tanh).then_inc(sem("lora_mid"), 1)
            act.wait_ge(sem("lora1_done"), 2)
            act.activation(lora_a, pb[5][0:64, 0:T], ACT.Copy).then_inc(sem("lora_mid"), 1)
            act.wait_ge(sem("lora1_done"), 3)
            act.activation(lora_g, pb[6][:, 0:T], ACT.Sigmoid).then_inc(sem("lora_mid"), 1)
            for f, (dst, bias) in enumerate(((W, "decay_w0"), (A, "a_0"), (G, None))):
                for j in range(4):
                    i = 4 * f + j
                    act.wait_ge(sem("lora2_done"), i + 1)
                    bank = pb[4 + i % 3]
                    if bias:
                        go(act.activation(slot(dst)[:, 2 * j, :], bank[:, 0:T], ACT.Sigmoid, bias=par_col(bias, 2 * j)))
                        act.activation(slot(dst)[:, 2 * j + 1, :], bank[:, T:2 * T], ACT.Sigmoid,
                                       bias=par_col(bias, 2 * j + 1)).then_inc(sem("lora_ready"), 1)
                    else:
                        act.activation(slot(dst)[:, 2 * j:2 * j + 2, :], bank[:, :], ACT.Copy).then_inc(sem("lora_ready"), 1)
            act.wait_ge(sem("kk_ready"), 1)
            act.activation(slot(TMP), slot(KK), ACT.Square).then_inc(sem("kk_sq"), 1)

            def prep(u, m):
                i = M_PER_UNIT * u + m
                if i == 0:
                    act.wait_ge(sem("kk_max"), 4)
                    link(act.activation(slot(TMP), slot(TMP), ACT.Ln))
                    act.activation(slot(TMP), slot(TMP), ACT.Exp, scale=-0.5).then_inc(sem("kk_root"), 1)
                if i == 3:
                    act.wait_ge(sem("bonus_done"), 1)
                    act.activation(bonus, pb[3 + 1][0:RWKV_HEADS, 0:T], ACT.Copy).then_inc(sem("bonus_ready"), 1)
                if i == 7:
                    act.wait_ge(sem("cum_ready"), KC)
                    act.activation(slot(W), slot(TMP), ACT.Exp, scale=-EXP_MINUS_HALF).then_inc(sem("decay_ready"), 1)
                    act.wait_ge(sem("decay_ready"), 1)
                    act.activation(slot(TMP), slot(TMP), ACT.Exp, scale=EXP_MINUS_HALF).then_inc(sem("decay_ready"), 1)
            ahead(act_head, act, L["ug"])
            act_layer(act, L["ug"], prep)
            ahead(act_head, act, L["z"])
            act.wait_ge(sem("evac_done"), L["ug"].evac1 + BANKS)
            act.activation(slot(GATE), slot(GATE), ACT.Sigmoid).then_inc(sem("gate_ready"), 1)
            act_layer(act, L["z"])

            def v_rows(c):
                act.wait_ge(sem("v_turned"), c + 1)
                if c >= 2:
                    act.wait_ge(sem("y2_done"), c - 1)
                go(act.activation(uv[c % 2][0:CHUNK, 0:512], pb[2][0:CHUNK, :], ACT.Copy))
                act.activation(uv[c % 2][0:CHUNK, 512:1024], pb[3][0:CHUNK, :], ACT.Copy).then_inc(sem("v_rows"), 1)

            def bk_rows(c):
                act.wait_ge(sem("bk_turned"), c + 1)
                if c >= 2:
                    act.wait_ge(sem("y2_done"), c - 1)
                go(act.activation(bk_t[c % 2][:, 0:512], pb[0][0:64, :], ACT.Copy))
                act.activation(bk_t[c % 2][:, 512:1024], pb[1][0:64, :], ACT.Copy).then_inc(sem("bk_rows"), 1)

            def tap_products(first, last):
                for s in range(first, min(last, CONV_TAPS)):
                    if s >= 3:
                        act.wait_ge(sem("tap_summed"), s - 2)
                    for k in range(POOL_TILES):
                        w = par_col("conv_dw", KC * (CONV_TAPS - 1 - s) + k)
                        if s == 0:
                            ins = act.activation(slot(GATE)[:, k, :], slot(U)[:, k, :], ACT.Identity, scale=w, bias=par_col("conv_b", k))
                        else:
                            ins = act.activation(tap_prod[s % 2][:, k, 0:T - s], slot(U)[:, k, 0:T - s], ACT.Copy, scale=w)
                        if k == POOL_TILES - 1:
                            ins.then_inc(sem("tap_ready"), 1)
                        else:
                            go(ins)

            act.wait_ge(sem("pool_stages"), 2)
            act.wait_ge(sem("block_done"), L["z"].item1 + BANKS)
            tap_products(0, EARLY_TAPS)
            act.wait_ge(sem("sub_dma"), 64)
            v_rows(0)
            bk_rows(0)
            for c in range(NCHUNK):
                act.wait_ge(sem("x_done"), c + 1)
                act.activation(x_buf[:, 512:1024], pb[5][0:CHUNK, :], ACT.Copy).then_inc(sem("x_rows_a"), 1)
                if c + 1 < NCHUNK:
                    v_rows(c + 1)
                act.wait_ge(sem("u_done"), c + 1)
                act.activation(uv[c % 2][CHUNK:2 * CHUNK, 512:1024], pb[5][0:CHUNK, :], ACT.Copy).then_inc(sem("u_rows_a"), 1)
                if c + 1 < NCHUNK:
                    bk_rows(c + 1)
                tap_products(EARLY_TAPS + 4 * c, EARLY_TAPS + 4 + 4 * c)
            act.wait_ge(sem("evac_done"), L["z"].evac1 + BANKS)
            act.activation(slot(ZR), slot(ZR), ACT.Sigmoid).then_inc(sem("z_ready"), 1)
            act.activation(slot(ZC), slot(ZC), ACT.Sigmoid).then_inc(sem("z_ready"), 1)
            act.wait_ge(sem("ln_centred"), 1)
            act.activation(slot(U), slot(GATE), ACT.Square).then_inc(sem("ln_sq"), 1)
            act.wait_ge(sem("ln_var"), 1)
            link(act.activation(rs[:, :], pb[6][:, T:2 * T], ACT.Ln, bias=eps[:, 1:2], scale=1.0 / D))
            act.activation(rs[:, :], rs[:, :], ACT.Exp, scale=-0.5).then_inc(sem("ln_root"), 1)
            ahead(act_head, act, L["conv_out"])
            act.wait_ge(sem("ln_ready"), 1)
            act.activation(slot(U), slot(GATE), ACT.Sigmoid).then_inc(sem("ln_sig"), 1)
            act.wait_ge(sem("gn_centred"), 4)
            act.activation(tmp2, slot(R), ACT.Square).then_inc(sem("gn_sq"), 1)

            def heads_of(i, src, dst):
                act.wait_ge(sem("mix_in"), i + 1)
                for k in range(KC):
                    act.activation(dst[:, k, :], slot(src)[:, k, :], ACT.Copy).then_inc(sem("x_hi_ready"), 1)
            heads_of(0, GATE, x_hi)
            act.wait_ge(sem("gn_var"), 1)
            for b in range(4):
                go(act.activation(slot(TMP)[:, 2 * b:2 * b + 2, :], pb[4 + b][:, :], ACT.Ln, bias=eps[:, 2:3], scale=1.0 / HEAD))
            sync()
            act.activation(slot(TMP), slot(TMP), ACT.Exp, scale=-0.5).then_inc(sem("gn_root"), 1)
            act_layer(act, L["conv_out"])
            ahead(act_head, act, L["rwkv_out"])
            heads_of(1, R, y_hi)
            act_layer(act, L["rwkv_out"])
            ahead(act_head, act, L["w_out"])
            heads_of(2, ZC, x_hi)
            act_layer(act, L["w_out"])

            def post_norm(i, first, bank):
                for k in range(KC):
                    act.wait_ge(sem("evac_done"), first + k + 1 + BANKS)
                    act.activation(sub[:, k, :], tile(64 if i else 0, k), ACT.Square).then_inc(sem("osq_ready"), 1)
                act.wait_ge(sem("osum_done"), i + 1)
                act.activation(rs[:, :], pb[bank][:, 0:T], ACT.Sqrt, bias=eps[:, 0:1], scale=1.0 / D).then_inc(sem("ors_ready"), 1)

            ahead(act_head, act, L["up0"])
            post_norm(0, L["w_out"].evac0, 7)
            norm_in(1)
            norm_root(1)

            def ffn(n, up, down):
                src = g_tile if n == 0 else c_tile

                def sig(u, m):
                    if n == 0:
                        act.wait_ge(sem("evac_done"), up.evac0 + M_PER_UNIT * u + m + 1 + BANKS)
                    else:
                        act.wait_ge(sem("glu_gate"), FC * (n - 1) + 2 * u + m + 1)
                    act.activation(s_tile[m], src[m], ACT.Sigmoid).then_inc(sem("glu_sig"), 1)

                def head(u, m):
                    act.wait_ge(sem("evac_done"), up.evac0 + M_PER_UNIT * u + m + 3 + BANKS)
                    j = 2 * u + m
                    o = act_hi[:, j, :] if isinstance(u, int) else act_hi[:, bass.ds(j, 1), :].rearrange("p a b -> p (a b)")
                    act.activation(o, a_tile[m], ACT.Copy).then_inc(sem("act_hi_ready"), 1)

                def hook(u, m):
                    if m == 1:
                        sig(u, 0)
                        sig(u, 1)
                    if m == 3:
                        head(u, 0)
                        head(u, 1)
                act_layer(act, up, hook)
                ahead(act_head, act, down)
                act_layer(act, down)

            ffn(0, L["up0"], L["down0"])
            ahead(act_head, act, L["ssd_z"])
            post_norm(1, L["down0"].evac0, 7)
            norm_in(2)
            norm_root(2)
            def z_sigmoids(u):
                act.wait_ge(sem("evac_done"), L["ssd_z"].evac0 + M_PER_UNIT * (u + 1) + BANKS)
                q = slice(M_PER_UNIT * u, M_PER_UNIT * (u + 1))
                act.activation(z_sig[:, q, :], z_t[:, q, :], ACT.Sigmoid).then_inc(sem("z_sig"), 1)

            def z_hook(u, m):
                if m == 1 and u:
                    z_sigmoids(u - 1)
            act_layer(act, L["ssd_z"], z_hook)
            ahead(act_head, act, L["ssd_xbc"])
            z_sigmoids(len(L["ssd_z"]) - 1)

            def xbc_hook(u, m):
                def tile_of(j):
                    return xbc[:, j, :] if isinstance(j, int) else pj[:, bass.ds(SSD_Z + j, 1), :].rearrange("p a b -> p (a b)")
                j = M_PER_UNIT * u + m
                act.wait_ge(sem("evac_done"), L["ssd_xbc"].evac0 + j + 1 + BANKS)
                act.activation(tile_of(j), conv_in[m], ACT.Identity, scale=par_col("ssd_conv_w_2", (SSD_TAPS - 1) * SSD_XBC + j),
                               bias=par_col("ssd_conv_b_2", j)).then_inc(sem("xbc_begun"), 1)
                if m == 1 and (not isinstance(u, int) or u):
                    xbc_sigmoids(u - 1)

            def xbc_sigmoids(u):
                for i in range(M_PER_UNIT):
                    j = M_PER_UNIT * u + i
                    act.wait_ge(sem("xbc_conv"), M_PER_UNIT + j + 1)
                    act.wait_ge(sem("xbc_ready"), j + 1)
                    t = xbc[:, j, :] if isinstance(u, int) else pj[:, bass.ds(M_PER_UNIT * (u + SSD_Z // M_PER_UNIT) + i, 1), :].rearrange("p a b -> p (a b)")
                    act.activation(conv_sig[i], t, ACT.Sigmoid).then_inc(sem("xbc_sig"), 1)
            act_layer(act, L["ssd_xbc"], xbc_hook, lead=2)
            xbc_sigmoids(len(L["ssd_xbc"]) - 1)
            act.wait_ge(sem("abs_ready"), 1)
            link(act.activation(dt_e, dt_e, ACT.Exp, scale=-1.0))
            act.wait_ge(sem("small_loaded"), 16 * 9)
            go(act.activation(heads_col[:, 3:4], heads_col[:, 1:2], ACT.Exp))
            act.activation(dt_e, dt_e, ACT.Ln, bias=1.0).then_inc(sem("log_ready"), 1)
            act.wait_ge(sem("acs_ready"), 2)
            go(act.activation(da_end, acs[:, 0:P], ACT.Exp, scale=-1.0, bias=acs[:, P - 1:P]))
            act.activation(da_exp, acs[:, P:T], ACT.Exp).then_inc(sem("da_ready"), 1)
            act.wait_ge(sem("xbc_ready"), M_PER_UNIT + SSD_XBC)
            for b in range(4):
                act.wait_ge(sem("eab_done"), b + 1)
                act.activation(eab[:, 4 * b:4 * b + 4, :].rearrange("p m l -> p (m l)"), pb[4 + b % 2][:, :], ACT.Copy).then_inc(sem("eab_ready"), 1)
            ahead(act_head, act, L["ssd_out"])
            act.wait_ge(sem("evac_done"), L["ssd_z"].evac1 + BANKS)

            def square(q):
                act.wait_ge(sem("yz_ready"), q + 1)
                if q >= 4:
                    act.wait_ge(sem("yz_sum"), q // 2 - 1)
                act.activation(sub[:, 2 * (q % 4):2 * (q % 4) + 2, :], y_ssd[:, 2 * q:2 * q + 2, :], ACT.Square).then_inc(sem("yz_sq"), 1)

            def root(g):
                act.wait_ge(sem("yz_sum"), g + 1)
                act.activation(sub[:, 8 + g, :], pb[4 + g][:, 0:T], ACT.Sqrt, bias=eps[:, 0:1], scale=1.0 / (4 * P)).then_inc(sem("yz_root"), 1)

            def yz_heads(g):
                for m in range(4 * g, 4 * g + 4):
                    act.wait_ge(sem("yn_ready"), m + 1)
                    act.activation(yz_hi[:, m, :], y_ssd[:, m, :], ACT.Copy).then_inc(sem("yz_hi_ready"), 1)

            for i in range(16):
                c, hq = divmod(i, 8)
                act.wait_ge(sem("bc_done"), i + 1)
                if i >= NATT:
                    act.wait_ge(sem("y_done"), i - NATT + 1)
                act.activation(att[i % NATT].rearrange("p h l -> p (h l)"), pb[i % 2][:, :], ACT.Exp).then_inc(sem("att_exp"), 1)
                if i == 0:
                    act.wait_ge(sem("eab_used"), 4)
                if i >= 11:
                    square(i - 11)
                if i == 14:
                    root(0)
            square(5)
            square(6)
            root(1)
            square(7)
            yz_heads(0)
            root(2)
            root(3)
            for g in range(1, 4):
                yz_heads(g)
            act_layer(act, L["ssd_out"])
            ahead(act_head, act, L["up1"])
            norm_in(3)
            norm_root(3)
            ffn(1, L["up1"], L["down1"])
            ahead(act_head, act, L["fox_qk"])
            norm_in(4)
            norm_root(4)

            def head_roots(i, t):
                act.wait_ge(sem("fox_sum"), i + 1)
                if i:
                    act.wait_ge(sem("qk_ready"), i)
                for b in range(4):
                    ins = act.activation(tmp2[:, 2 * b:2 * b + 2, :], pb[4 + b][:, :], ACT.Ln, bias=eps[:, 0:1], scale=1.0 / HEAD)
                    ins.then_inc(sem("fox_root"), 1)
                act.wait_ge(sem("fox_root"), 4 * (i + 1))
                act.activation(tmp2, tmp2, ACT.Exp, scale=-0.5).then_inc(sem("fox_rms"), 1)

            def head_squares(i, t, blocks):
                act.wait_ge(sem("evac_done"), blocks + BANKS)
                if i:
                    act.wait_ge(sem("fox_sum"), i)
                act.activation(fox_tmp, t, ACT.Square).then_inc(sem("fox_sq"), 1)

            def q_norm(u, m):
                if (u, m) == (2, 0):
                    head_squares(0, q_t, L["fox_qk"].evac0 + KC)
                if (u, m) == (3, 0):
                    head_roots(0, q_t)
            act_layer(act, L["fox_qk"], q_norm)
            ahead(act_head, act, L["fox_vg"])

            def k_norm(u, m):
                if (u, m) == (0, 0):
                    head_squares(1, k_t, L["fox_qk"].evac1)
                if (u, m) == (0, 2):
                    act.wait_ge(sem("abs_ready"), 2)
                    link(act.activation(dt_e[0:FOX_HEADS, :], dt_e[0:FOX_HEADS, :], ACT.Exp, scale=-1.0))
                    act.activation(dt_e[0:FOX_HEADS, :], dt_e[0:FOX_HEADS, :], ACT.Ln, bias=1.0).then_inc(sem("log_ready"), 1)
                if (u, m) == (1, 0):
                    head_roots(1, k_t)
            act_layer(act, L["fox_vg"], k_norm)
            act.wait_ge(sem("evac_done"), L["fox_vg"].evac1 + BANKS)
            act.activation(gate_t, gate_t, ACT.Sigmoid).then_inc(sem("fox_gate"), 1)
            ahead(act_head, act, L["fox_out"])

            def o_head(k):
                act.wait_ge(sem("o_ready"), k + 1)
                act.activation(x_hi[:, k, :], o_fox[:, k, :], ACT.Copy).then_inc(sem("x_hi_ready"), 1)

            steps = 2 * FOX_HEADS
            for i in range(steps + 1):
                if i < steps:
                    n, s = (i % 2 + 1) * P, i % NS
                    act.wait_ge(sem("max_ready"), i + 1)
                    act.activation(sc[s][:, 0, 0:n], sc[s][:, 1, 0:n], ACT.Exp, bias=fox_stat[:, 2 * (i % 2), i // 2:i // 2 + 1],
                                   accum_out=fox_stat[:, 2 * (i % 2) + 1, i // 2:i // 2 + 1]).then_inc(sem("exp_ready"), 1)
                if i >= 1:
                    j = i - 1
                    n, s = (j % 2 + 1) * P, j % NS
                    act.wait_ge(sem("share_ready"), j + 1)
                    act.activation(sc[s][:, 0, 0:n], sc[s][:, 0, 0:n], ACT.Copy,
                                   scale=fox_stat[:, 4 + j % 2, j // 2:j // 2 + 1]).then_inc(sem("p_ready"), 1)
                if i >= 10 and (i - 10) % 4 == 0:
                    o_head((i - 10) // 4)
            for k in range(KC - 2, KC):
                o_head(k)
            act_layer(act, L["fox_out"])
            ahead(act_head, act, L["up2"])
            act.wait_ge(sem("block_done"), L["fox_out"].item1 + BANKS)
            norm_in(5)
            norm_root(5)
            ffn(2, L["up2"], L["down2"])
            for k in range(KC):
                act.wait_ge(sem("x_ready"), KC * 6 + k + 1)
                act.activation(sub[:, k, :], x_res[:, k, :], ACT.Square).then_inc(sem("sq_ready"), 1)
            norm_root(6)

        @block.vector
        def _(dve):
            ch = Chain(dve, "dve_chain")
            go, sync, link = ch.go, ch.sync, ch.link
            stt, tt, ts = dve.scalar_tensor_tensor, dve.tensor_tensor, dve.tensor_scalar

            def norm_rest(n):
                name, o = NORMS[n]
                for k in range(KC):
                    dve.wait_ge(sem("x_hi_ready"), X_BASE[n] + k + 1)
                    stt(x_lo[:, k, :], x_res[:, k, :], par_col(name, o + k), x_hi[:, k, :].bitcast(F32),
                        ALU.mult, ALU.subtract).then_inc(sem("x_lo_ready"), 1)

            def norm_scale(n):
                dve.wait_ge(sem("rs_ready"), n + 1)
                link(dve.reciprocal(rstd[:, :], rs[:, :]))

            def scaled(dst):
                def out_block(u, m):
                    j = M_PER_UNIT * u + m
                    o = dst(j) if isinstance(u, int) else pj[:, bass.ds(j + dst(None), 1), :].rearrange("p a b -> p (a b)")
                    tt(o, pb[m][:, 0:T], rstd[:, :], ALU.mult).then_inc(sem("evac_done"), 1)
                return out_block

            for i in range(BANKS):
                dve.nop().then_inc(sem("evac_done"), 1)
            for b in range(2):
                dve.wait_ge(sem("par_turned"), b + 1)
                n = min(n_rows - 512 * b, 512)
                go(dve.tensor_copy(par[:, 512 * b:512 * b + n], pb[1 + b][:, 0:n]))
            sync()
            for k in range(KC):
                dve.wait_ge(sem("x_turned"), k // 2 + 1)
                dve.tensor_copy(x_res[:, k, :], pb[3 + k // 2][:, T * (k % 2):T * (k % 2) + T]).then_inc(sem("x_ready"), 1)
            dve.wait_ge(sem("x_ready"), KC)
            norm_rest(0)
            ahead(dve_rest, dve, L["rkv"])
            norm_scale(0)
            h, xx = slot(TMP), slot(W)
            for k in range(KC):
                go(stt(h[:, k, :], x_res[:, k, :], par_col("pre_mix_norm", k), rstd[:, :], ALU.mult, ALU.mult))
            sync()

            def shift_less(o, s):
                go(tt(o[:, :, 1:T], s[:, :, 0:T - 1], s[:, :, 1:T], ALU.subtract))
                link(ts(o[:, :, 0:1], s[:, :, 0:1], -1.0, None, ALU.mult))

            shift_less(xx, h)
            for i, s in enumerate((KK, A, G)):
                for k in range(KC):
                    ins = stt(slot(s)[:, k, :], xx[:, k, :], par_col("mu_wag", KC * i + k), h[:, k, :], ALU.mult, ALU.add)
                    ins.then_inc(sem("lora_x"), 1)
            dve_layer(dve, L["rkv"], scaled(lambda j: tile(0, j) if j is not None else 0))
            dve.wait_ge(sem("evac_done"), L["rkv"].evac1 + BANKS)

            def lerp(s, i):
                shift_less(mix_tmp, slot(s))
                for k in range(KC):
                    go(stt(slot(s)[:, k, :], mix_tmp[:, k, :], par_col("mu_rkv", KC * i + k), slot(s)[:, k, :], ALU.mult, ALU.add))
                sync()
            lerp(K, 1)
            dve.wait_ge(sem("lora1_done"), 1)
            for k in range(KC):
                go(ts(slot(KK)[:, k, :], slot(K)[:, k, :], par_col("k_k", k), None, ALU.mult))
            sync()
            dve.nop().then_inc(sem("kk_ready"), 1)
            ahead(dve_rest, dve, L["ug"])
            lerp(R, 0)
            dve.wait_ge(sem("lora_ready"), 8)
            for k in range(KC):
                go(ts(rate_tmp[:, k, :], slot(A)[:, k, :], 1.0, par_col("k_a", k), ALU.subtract, ALU.mult))
            sync()
            link(stt(slot(K), rate_tmp, 1.0, slot(K), ALU.add, ALU.mult))
            dve.wait_ge(sem("kk_sum"), 1)
            for b in range(4):
                ts(slot(TMP)[:, 2 * b:2 * b + 2, :], pb[4 + b][:, :], 1e-24, None, ALU.max).then_inc(sem("kk_max"), 1)
            for k in range(KC):
                go(stt(mix_tmp[:, k, :], slot(R)[:, k, :], par_col("r_k", k), slot(K)[:, k, :], ALU.mult, ALU.mult))
            sync()
            dve.nop().then_inc(sem("bonus_in"), 1)

            def chunks(i):
                return slot(i).rearrange("p k (c s) -> p (k c) s", s=CHUNK)

            bk_v = bk.rearrange("p k c j s -> p (k c) j s")

            def prep(u, m):
                i = M_PER_UNIT * u + m
                if i == 2:
                    dve.wait_ge(sem("kk_root"), 1)
                    link(tt(slot(KK), slot(KK), slot(TMP), ALU.mult))
                if i == 3:
                    go(tt(slot(A), slot(KK), slot(A), ALU.mult))
                if i in (3, 4, 5, 6):
                    if i == 3:
                        dve.wait_ge(sem("lora_ready"), 12)
                    for k in (2 * (i - 3), 2 * (i - 3) + 1):
                        dve.tensor_tensor_scan(slot(TMP)[:, k, :], scan_mask[:, :], slot(W)[:, k, :], 0.0, ALU.mult,
                                               ALU.add).then_inc(sem("cum_ready"), 1)
                if i == 9:
                    dve.wait_ge(sem("decay_ready"), 1)
                    go(stt(chunks(KK)[:, :, 1:CHUNK], chunks(KK)[:, :, 1:CHUNK], -1.0, chunks(W)[:, :, 0:CHUNK - 1], ALU.mult, ALU.mult))
                    go(ts(chunks(KK)[:, :, 0:1], chunks(KK)[:, :, 0:1], -1.0, None, ALU.mult))
                if i == 10:
                    dve.wait_ge(sem("decay_ready"), 2)
                    dve.wait_ge(sem("bonus_done"), 1)
                    go(tt(bk_v[:, :, 1, :], chunks(A), chunks(TMP), ALU.mult))
                if i == 11:
                    go(dve.tensor_copy(chunk_decay[:, :, :].rearrange("p k c -> p (k c)"), chunks(W)[:, :, CHUNK - 1]))
                    sync()
                    dve.nop().then_inc(sem("scan_in"), 1)
                if i == 12:
                    go(tt(bk_v[:, :, 0, :], chunks(K), chunks(TMP), ALU.mult))
            dve_layer(dve, L["ug"], scaled(lambda j: tile(24, j)), prep)
            ahead(dve_rest, dve, L["z"])
            sync()
            dve.wait_ge(sem("pool_stages"), 1)
            for c in range(NCHUNK):
                dve.wait_ge(sem("lab_done"), c + 1)
                dst = lab_t[:, 16 * c:16 * c + 16, :].rearrange("s (m h) t -> s h m t", h=2)
                for h in range(2):
                    ins = tt(dst[:, h], pb[4 + 2 * h + c % 2][0:CHUNK, 0:T].rearrange("s (m t) -> s m t", t=CHUNK),
                             g_mask[0:CHUNK, CHUNK:2 * CHUNK].unsqueeze(1).broadcast_to([CHUNK, 8, CHUNK]), ALU.mult)
                    if h:
                        ins.then_inc(sem("lab_ready"), 1)
                    else:
                        go(ins)
            dve.wait_ge(sem("lab_ready"), NCHUNK)

            def substitute(first, last):
                for t in range(first, min(last, CHUNK)):
                    if t == 1:
                        dve.wait_ge(sem("sub_dma"), 32)
                        link(dve.memset(mt, 0.0))
                        link(dve.memset(mt.rearrange("p s t -> p (s t)")[:, 0:CHUNK * CHUNK:CHUNK + 1], 1.0))
                    link(tt(prod[:, 0:t, 0:t], mt[:, 0:t, 0:t], lt[:, 0:t, t].unsqueeze(1).broadcast_to([P, t, t]), ALU.mult))
                    link(dve.tensor_reduce(mt[:, 0:t, t], prod[:, 0:t, 0:t], AX_X, ALU.add))

            def z_hook(u, m):
                i = M_PER_UNIT * u + m
                if i >= 2:
                    substitute(1 + 3 * (i - 2), 4 + 3 * (i - 2))
            dve_layer(dve, L["z"], scaled(lambda j: slot(ZR)[:, j, :] if j < KC else slot(ZC)[:, j - KC, :]), z_hook)
            dve.nop().then_inc(sem("inverse_ready"), 1)

            def conv_taps(first, last):
                for s in range(first, min(last, CONV_TAPS)):
                    for k in range(POOL_TILES, KC):
                        w = par_col("conv_dw", KC * (CONV_TAPS - 1 - s) + k)
                        o, c = slot(GATE)[:, k, :], slot(U)[:, k, :]
                        if s == 0:
                            go(ts(o, c, w, par_col("conv_b", k), ALU.mult, ALU.add))
                        else:
                            go(stt(o[:, s:T], c[:, 0:T - s], w, o[:, s:T], ALU.mult, ALU.add))
                    sync()
            dve.wait_ge(sem("pool_stages"), 2)
            conv_taps(0, DVE_EARLY)

            def mask_products(c):
                dve.wait_ge(sem("g_done"), c + 1)
                if c >= 2:
                    dve.wait_ge(sem("y2_done"), c - 1)
                for h in range(2):
                    go(tt(g_buf[c % 2][:, h::2, :], pb[h][64:128, :].rearrange("s (m n) -> s m n", n=64),
                          g_mask[64:128, :].unsqueeze(1).broadcast_to([64, 8, 64]), ALU.mult))
                sync()
                dve.nop().then_inc(sem("g_masked"), 1)
                v = bk[:, :, c, :, :].rearrange("p k j s -> p k (j s)")
                tt(v, v, chunk_decay[:, :, c:c + 1].broadcast_to([P, KC, 2 * CHUNK]), ALU.mult).then_inc(sem("bk_scaled"), 1)

            def state_sum(c):
                dve.wait_ge(sem("s_done"), c + 1)
                for h in range(2):
                    rows = slice(64 * h, 64 * h + 64)
                    go(tt(state[rows, :, rows], state[rows, :, rows],
                          pb[6][rows, :].rearrange("k (m v) -> k m v", v=64), ALU.add))
                sync()
                dve.nop().then_inc(sem("state_ready"), 1)

            dve.wait_ge(sem("sub_dma"), 64)
            mask_products(0)
            dve.wait_ge(sem("pool_stages"), 3)
            dve.nop().then_inc(sem("state_ready"), 1)
            cv = slot(GATE)
            for c in range(NCHUNK):
                dve.wait_ge(sem("x_done"), c + 1)
                dve.tensor_copy(x_buf[:, 0:512], pb[4][0:CHUNK, :]).then_inc(sem("x_rows_v"), 1)
                if c + 1 < NCHUNK:
                    dve.wait_ge(sem("y1_done"), c + 1)
                    go(tt(state, state, chunk_decay[:, :, c:c + 1].broadcast_to([P, KC, P]), ALU.mult))
                    mask_products(c + 1)
                else:
                    dve.wait_ge(sem("ln_mean"), 1)
                    link(ts(rstd[:, :], pb[6][:, 0:T], 1.0 / D, None, ALU.mult))
                    link(tt(cv, cv, rstd[:, :].unsqueeze(1).broadcast_to([P, KC, T]), ALU.subtract))
                    dve.nop().then_inc(sem("ln_centred"), 1)
                dve.wait_ge(sem("u_done"), c + 1)
                dve.tensor_copy(uv[c % 2][CHUNK:2 * CHUNK, 0:512], pb[4][0:CHUNK, :]).then_inc(sem("u_rows_v"), 1)
                conv_taps(DVE_EARLY + 4 * c, DVE_EARLY + 2 + 4 * c)
                if c + 1 < NCHUNK:
                    state_sum(c)
                conv_taps(DVE_EARLY + 2 + 4 * c, DVE_EARLY + 4 + 4 * c)
                if c == 6:
                    dve.nop().then_inc(sem("conv_ready"), 1)
                dve.wait_ge(sem("y2_done"), c + 1)
                dve.tensor_copy(slot(R)[:, :, CHUNK * c:CHUNK * c + CHUNK],
                                pb[7][:, 0:T].rearrange("p (m t) -> p m t", t=CHUNK)).then_inc(sem("y_out"), 1)
            dve.wait_ge(sem("y_out"), NCHUNK)

            y = slot(R)
            dve.wait_ge(sem("ln_root"), 1)
            link(tt(cv, cv, rs[:, :].unsqueeze(1).broadcast_to([P, KC, T]), ALU.mult))
            for k in range(KC):
                go(ts(cv[:, k, :], cv[:, k, :], par_col("conv_ln_w", k), par_col("conv_ln_b", k), ALU.mult, ALU.add))
            sync()
            dve.nop().then_inc(sem("ln_ready"), 1)
            dve.wait_ge(sem("gn_mean"), 1)
            for b in range(4):
                yb = y[:, 2 * b:2 * b + 2, :].rearrange("p k t -> p (k t)")
                stt(yb, pb[4 + b][:, :], -1.0 / HEAD, yb, ALU.mult, ALU.add).then_inc(sem("gn_centred"), 1)
            ahead(dve_rest, dve, L["conv_out"])
            dve.wait_ge(sem("ln_sig"), 1)
            link(tt(cv, cv, slot(U), ALU.mult))

            def mix_rest(i, src, hi, lo):
                dve.nop().then_inc(sem("mix_in"), 1)
                for k in range(KC):
                    dve.wait_ge(sem("x_hi_ready"), KC * (i + 1) + k + 1)
                    tt(lo[:, k, :], slot(src)[:, k, :], hi[:, k, :].bitcast(F32), ALU.subtract).then_inc(sem("x_lo_ready"), 1)

            mix_rest(0, GATE, x_hi, x_lo)

            def gate_conv(u, m):
                o = slot(ZC)[:, M_PER_UNIT * u + m, :]
                tt(o, o, pb[m][:, 0:T], ALU.mult).then_inc(sem("evac_done"), 1)

            def gn_steps(u, m):
                i = M_PER_UNIT * u + m
                if i == 0:
                    dve.wait_ge(sem("gn_root"), 1)
                    link(tt(y, y, slot(TMP), ALU.mult))
                if i == 1:
                    for k in range(KC):
                        go(ts(y[:, k, :], y[:, k, :], par_col("gn_w", k), par_col("gn_b", k), ALU.mult, ALU.add))
                if i == 2:
                    dve.wait_ge(sem("bonus_out"), 1)
                    for b in range(4):
                        go(tt(slot(TMP)[:, 2 * b:2 * b + 2, :].rearrange("p k t -> p (k t)"),
                              slot(V)[:, 2 * b:2 * b + 2, :].rearrange("p k t -> p (k t)"), pb[4 + b][:, :], ALU.mult))
                if i == 3:
                    sync()
                    link(tt(y, y, slot(TMP), ALU.add))
                if i == 4:
                    link(tt(y, y, slot(G), ALU.mult))
            dve.wait_ge(sem("z_ready"), 2)
            dve_layer(dve, L["conv_out"], gate_conv, gn_steps)
            ahead(dve_rest, dve, L["rwkv_out"])
            mix_rest(1, R, y_hi, y_lo)

            def gate_rwkv(u, m):
                o, z = slot(ZC)[:, M_PER_UNIT * u + m, :], slot(ZR)[:, M_PER_UNIT * u + m, :]
                tt(z, z, pb[m][:, 0:T], ALU.mult).then_inc(sem("evac_done"), 1)
                dve.wait_ge(sem("evac_done"), L["rwkv_out"].evac0 + M_PER_UNIT * u + m + 1 + BANKS)
                go(tt(o, o, z, ALU.add))
            dve_layer(dve, L["rwkv_out"], gate_rwkv)
            sync()
            ahead(dve_rest, dve, L["w_out"])
            mix_rest(2, ZC, x_hi, x_lo)

            def plain(dst):
                def out_block(u, m):
                    dve.tensor_copy(tile(dst, M_PER_UNIT * u + m), pb[m][:, 0:T]).then_inc(sem("evac_done"), 1)
                return out_block

            def post_norm(i, src, name):
                dve.wait_ge(sem("ors_ready"), i + 1)
                link(dve.reciprocal(rstd[:, :], rs[:, :]))
                for k in range(KC):
                    go(stt(tile(src, k), tile(src, k), par_col(name, k), rstd[:, :], ALU.mult, ALU.mult))
                sync()
                for k in range(KC):
                    tt(x_res[:, k, :], x_res[:, k, :], tile(src, k), ALU.add).then_inc(sem("x_ready"), 1)

            def norm_begin(n):
                dve.wait_ge(sem("x_ready"), KC * (n + 1))
                norm_rest(n)
                norm_scale(n)

            dve_layer(dve, L["w_out"], plain(0))
            ahead(dve_rest, dve, L["up0"])
            post_norm(0, 0, "post_mix_norm")
            norm_begin(1)

            def ffn(n, up, down, out_block):
                w = lambda tap, j: par_col("ffn_conv_w_2", (n - 1) * GLU_TAPS * FC + tap * FC + j)

                def hidden(u, m):
                    if m < 2:
                        tt(g_tile[m], pb[m][:, 0:T], rstd[:, :], ALU.mult).then_inc(sem("evac_done"), 1)
                        if n and m == 1:
                            glu_conv(u)
                    else:
                        dve.wait_ge(sem("glu_silu"), FC * n + 2 * u + m - 1)
                        tt(a_tile[m - 2], pb[m][:, 0:T], s_tile[m - 2], ALU.mult).then_inc(sem("evac_done"), 1)
                    if m == 3:
                        for i in range(2):
                            j = 2 * u + i
                            if isinstance(u, int):
                                hi_, lo_ = act_hi[:, j, :], act_lo[:, j, :]
                            else:
                                hi_, lo_ = (t[:, bass.ds(j, 1), :].rearrange("p a b -> p (a b)") for t in (act_hi, act_lo))
                            dve.wait_ge(sem("act_hi_ready"), FC * n + j + 1)
                            tt(lo_, a_tile[i], hi_.bitcast(F32), ALU.subtract).then_inc(sem("act_lo_ready"), 1)

                def glu_conv(u):
                    for s in range(GLU_TAPS):
                        for m in range(2):
                            j = 2 * u + m
                            if s == 0:
                                dve.wait_ge(sem("evac_done"), up.evac0 + M_PER_UNIT * u + m + 1 + BANKS)
                                ins = ts(c_tile[m], g_tile[m], w(2, j), par_col("ffn_conv_b_2", (n - 1) * FC + j), ALU.mult, ALU.add)
                            else:
                                dve.wait_ge(sem("glu_step"), 4 * (len(up) * (n - 1) + u) + 2 * s + m - 1)
                                ins = stt(c_tile[m][:, s:T], g_tile[m][:, 0:T - s], w(2 - s, j), c_tile[m][:, s:T], ALU.mult, ALU.add)
                            ins.then_inc(sem("glu_gate" if s == GLU_TAPS - 1 else "glu_step"), 1)
                dve_layer(dve, up, hidden, rest_last=True)
                ahead(dve_rest, dve, down)
                dve_layer(dve, down, out_block)

            def residual(u, m):
                x = x_res[:, M_PER_UNIT * u + m, :]
                ins = tt(x, x, pb[m][:, 0:T], ALU.add)
                ins.then_inc(sem("x_ready"), 1)
                dve.nop().then_inc(sem("evac_done"), 1)

            ffn(0, L["up0"], L["down0"], plain(64))
            ahead(dve_rest, dve, L["ssd_z"])
            post_norm(1, 64, "post_ffn_norm")
            norm_begin(2)

            def gain_in(n):
                name, o = NORMS[n]
                for k in range(KC):
                    ts(x_gain[:, k, :], x_res[:, k, :], par_col(name, o + k), None, ALU.mult).then_inc(sem("gain_ready"), 1)

            gain_in(2)
            dve_layer(dve, L["ssd_z"], scaled(lambda j: z_t[:, j, :]))
            ahead(dve_rest, dve, L["ssd_xbc"])
            ly = L["ssd_xbc"]
            n_xbc = SSD_XBC

            def xbc_tile(j):
                return xbc[:, j, :] if isinstance(j, int) else pj[:, bass.ds(SSD_Z + j, 1), :].rearrange("p a b -> p (a b)")

            for m in range(M_PER_UNIT):
                dve.nop().then_inc(sem("xbc_conv"), 1)

            def xbc_block(u, m):
                dve.wait_ge(sem("xbc_conv"), M_PER_UNIT * u + m + 1)
                tt(conv_in[m], pb[m][:, 0:T], rstd[:, :], ALU.mult).then_inc(sem("evac_done"), 1)
                if m >= 2:
                    xbc_taps(u, 2 * (m - 2))

            def xbc_taps(u, first):
                for s in range(1, SSD_TAPS):
                    for i in range(2):
                        m = first + i
                        j = M_PER_UNIT * u + m
                        t = xbc_tile(j)
                        if s == 1:
                            dve.wait_ge(sem("xbc_begun"), j + 1)
                        else:
                            dve.wait_ge(sem("xbc_step"), 8 * u + 2 * first + 2 * (s - 2) + i + 1)
                        stt(t[:, s:T], conv_in[m][:, 0:T - s], par_col("ssd_conv_w_2", (SSD_TAPS - 1 - s) * n_xbc + j), t[:, s:T],
                            ALU.mult, ALU.add).then_inc(sem("xbc_conv" if s == SSD_TAPS - 1 else "xbc_step"), 1)
            dve_layer(dve, ly, xbc_block, rest_last=True)
            dve.wait_ge(sem("narrow_done"), 1)
            dve.wait_ge(sem("small_loaded"), 16 * 9)
            link(tt(dt_z, pb[4][0:SSD_HEADS, 0:T], rstd[0:SSD_HEADS, :], ALU.mult))
            link(ts(dt_z, dt_z, heads_col[:, 0:1], None, ALU.add))
            stt(dt_e, dt_z, -1.0, dt_z, ALU.mult, ALU.max).then_inc(sem("abs_ready"), 1)
            dve.wait_ge(sem("log_ready"), 1)
            link(stt(dt, dt_z, 0.0, dt_e, ALU.max, ALU.add))
            link(ts(dt_z, dt, heads_col[:, 3:4], -1.0, ALU.mult, ALU.mult))
            for c in range(2):
                s = slice(c * P, c * P + P)
                dve.tensor_tensor_scan(acs[:, s], ones[0:SSD_HEADS, :], dt_z[:, s], 0.0, ALU.mult, ALU.add).then_inc(sem("acs_ready"), 1)
            for c in range(2):
                dve.wait_ge(sem("cb_done"), c + 1)
                tt(cbm[:, c], pb[6 + c][:, :].rearrange("p (g l) -> p g l", l=P),
                   tri[:, :].unsqueeze(1).broadcast_to([P, SSD_GROUPS, P]), ALU.mult).then_inc(sem("cbm_ready"), 1)
            dve.wait_ge(sem("b_turned"), 1)
            dve.tensor_copy(b_tok.rearrange("p g n -> p (g n)"), pb[5][:, :]).then_inc(sem("b_tok_ready"), 1)
            dve.wait_ge(sem("heads_turned"), 1)
            flat_heads = tok_heads[:, :, :].rearrange("p a h -> p (a h)")
            link(dve.tensor_copy(flat_heads, pb[4][:, 0:5 * SSD_HEADS]))
            dve.nop().then_inc(sem("heads_ready"), 1)
            for i in range(8):
                c, b = divmod(i, 4)
                dve.wait_ge(sem("xs_turned"), i + 1)
                tt(xdt[:, c, 512 * b:512 * b + 512].rearrange("p (h d) -> p h d", d=HEAD),
                   pb[6 + i % 2][:, :].rearrange("p (h d) -> p h d", d=HEAD),
                   tok_heads[:, 2 + c, 8 * b:8 * b + 8].unsqueeze(2).broadcast_to([P, 8, HEAD]), ALU.mult).then_inc(sem("xdt_ready"), 1)
            for g in range(SSD_GROUPS):
                dve.wait_ge(sem("st_done"), g + 1)
                dve.tensor_copy(st_ssd[:, 512 * g:512 * g + 512], pb[6 + g % 2][:, :]).then_inc(sem("st_ready"), 1)
            for b in range(4):
                dve.wait_ge(sem("yoff_done"), b + 1)
                dve.wait_ge(sem("eab_ready"), b + 1)
                tt(y_ssd[:, 4 * b:4 * b + 4, P:T], pb[4 + b % 2][:, :].rearrange("p (m l) -> p m l", l=P),
                   eab[:, 4 * b:4 * b + 4, :], ALU.mult).then_inc(sem("eab_used"), 1)
            dve.wait_ge(sem("eab_used"), 4)
            for m in range(SSD_Z):
                go(stt(y_ssd[:, m, P:T], xbc[:, m, P:T], d_skip[:, m:m + 1], y_ssd[:, m, P:T], ALU.mult, ALU.add))
            sync()
            ahead(dve_rest, dve, L["ssd_out"])

            def yz_norm(g):
                dve.wait_ge(sem("yz_root"), g + 1)
                link(dve.reciprocal(sub[:, 8 + g, :], sub[:, 8 + g, :]))
                for m in range(4 * g, 4 * g + 4):
                    stt(y_ssd[:, m, :], y_ssd[:, m, :], par_col("ssd_norm_g_2", m), sub[:, 8 + g, :], ALU.mult, ALU.mult).then_inc(sem("yn_ready"), 1)

            for i in range(17):
                if i < 16:
                    c, hq = divmod(i, 8)
                    dve.wait_ge(sem("att_exp"), i + 1)
                    t = att[i % NATT]
                    tt(t, t, cbm[:, c, hq // 2, :].unsqueeze(1).broadcast_to([P, 4, P]), ALU.mult).then_inc(sem("att_ready"), 1)
                if i >= 1:
                    c, hq = divmod(i - 1, 8)
                    dve.wait_ge(sem("y_done"), i)
                    src = pb[2 + (i - 1) % 2][:, 0:T].rearrange("p (m l) -> p m l", l=P)
                    if c == 0:
                        for r in range(2):
                            m = 2 * hq + r
                            ins = stt(y_ssd[:, m, 0:P], xbc[:, m, 0:P], d_skip[:, m:m + 1], src[:, r, :], ALU.mult, ALU.add)
                            if r == 0:
                                go(ins)
                        ins.then_inc(sem("y_out_ssd"), 1)
                    else:
                        yy = y_ssd[:, 2 * hq:2 * hq + 2, :]
                        tt(yy[:, :, P:T], yy[:, :, P:T], src, ALU.add).then_inc(sem("y_out_ssd"), 1)
                        dve.wait_ge(sem("z_silu"), 4)
                        dve.wait_ge(sem("y_out_ssd"), i)
                        tt(yy, yy, z_t[:, 2 * hq:2 * hq + 2, :], ALU.mult).then_inc(sem("yz_ready"), 1)
                if i == 15:
                    yz_norm(0)
            for g in range(1, 4):
                yz_norm(g)
                for m in range(4 * g - 4, 4 * g if g < 3 else SSD_Z):
                    dve.wait_ge(sem("yz_hi_ready"), m + 1)
                    tt(yz_lo[:, m, :], y_ssd[:, m, :], yz_hi[:, m, :].bitcast(F32), ALU.subtract).then_inc(sem("yz_lo_ready"), 1)
            dve_layer(dve, L["ssd_out"], residual)
            ahead(dve_rest, dve, L["up1"])
            norm_begin(3)
            ffn(1, L["up1"], L["down1"], residual)
            ahead(dve_rest, dve, L["fox_qk"])
            norm_begin(4)

            dve.nop().then_inc(sem("fox_arena_free"), 1)
            nh = FOX_HEADS

            def norm_head(i):
                t, g = ((q_t, fox_g[:, 2:3]), (k_t, fox_g[:, 1:2]))[i]
                dve.wait_ge(sem("fox_rms"), i + 1)
                stt(t, t, g, tmp2, ALU.mult, ALU.mult).then_inc(sem("qk_ready"), 1)

            def qk_hook(u, m):
                if (u, m) == (0, 0):
                    gain_in(4)
                    go(ts(fox_g[:, 2:3], fox_g[:, 0:1], HEAD ** -0.5, None, ALU.mult))
                if (u, m) == (3, 2):
                    sync()
                    norm_head(0)
            dve_layer(dve, L["fox_qk"], scaled(lambda j: tile(0, j)), qk_hook)
            ahead(dve_rest, dve, L["fox_vg"])

            def vg_hook(u, m):
                if (u, m) == (0, 0):
                    dve.wait_ge(sem("narrow_done"), 2)
                    link(tt(dt_z[0:nh, :], pb[4][0:nh, 0:T], rstd[0:nh, :], ALU.mult))
                    link(ts(dt_z[0:nh, :], dt_z[0:nh, :], heads_col[0:nh, 2:3], None, ALU.add))
                    stt(dt_e[0:nh, :], dt_z[0:nh, :], -1.0, dt_z[0:nh, :], ALU.mult, ALU.max).then_inc(sem("abs_ready"), 1)
                if (u, m) == (1, 0):
                    dve.wait_ge(sem("log_ready"), 2)
                    link(stt(dt[0:nh, :], dt_z[0:nh, :], 0.0, dt_e[0:nh, :], ALU.min, ALU.subtract))
                    link(dve.tensor_tensor_scan(acs[0:nh, 0:P], ones[0:nh, :], dt[0:nh, 0:P], 0.0, ALU.mult, ALU.add))
                    link(dve.tensor_tensor_scan(acs[0:nh, P:T], ones[0:nh, :], dt[0:nh, P:T], acs[0:nh, P - 1:P], ALU.mult, ALU.add))
                    link(ts(cum_neg[0:nh, :], acs[0:nh, :], -1.0, None, ALU.mult))
                    dve.nop().then_inc(sem("cum_fox"), 1)
                if (u, m) == (1, 3):
                    norm_head(1)
                if (u, m) == (2, 1):
                    dve.wait_ge(sem("cq_turned"), 1)
                    dve.tensor_copy(tok_heads[:, 0:2, 0:nh], pb[4][:, 0:2 * nh].rearrange("p (c h) -> p c h", c=2)).then_inc(sem("cq_ready"), 1)
                if u == 3:
                    dve.wait_ge(sem("v_fox_turned"), m + 1)
                    dve.tensor_copy(v_tok[:, m // 2, 512 * (m % 2):512 * (m % 2) + 512], pb[4 + m][:, :]).then_inc(sem("v_fox_ready"), 1)
            dve_layer(dve, L["fox_vg"], scaled(lambda j: tile(16, j)), vg_hook)
            dve.wait_ge(sem("fox_mask_ready"), 1)
            dve.wait_ge(sem("cq_ready"), 1)
            ahead(dve_rest, dve, L["fox_out"])

            def o_rest(k):
                dve.wait_ge(sem("x_hi_ready"), X_BASE["fox"] + k + 1)
                tt(x_lo[:, k, :], o_fox[:, k, :], x_hi[:, k, :].bitcast(F32), ALU.subtract).then_inc(sem("x_lo_ready"), 1)

            steps = 2 * nh
            for i in range(steps + 4):
                if i < steps:
                    h, qc = divmod(i, 2)
                    n, s = (qc + 1) * P, i % NS
                    dve.wait_ge(sem("score_done"), i + 1)
                    if i >= NS:
                        dve.wait_ge(sem("turned"), i - NS + 1)
                    stt(sc[s][:, 1, 0:n], pb[score_banks[s]][:, 0:n], tok_heads[:, qc, h:h + 1], fox_mask[:, T - n:T],
                        ALU.add, ALU.add).then_inc(sem("masked"), 1)
                if 1 <= i <= steps:
                    h, qc = divmod(i - 1, 2)
                    dve.wait_ge(sem("exp_ready"), i)
                    dve.reciprocal(fox_stat[:, 4 + qc, h:h + 1], fox_stat[:, 2 * qc + 1, h:h + 1]).then_inc(sem("share_ready"), 1)
                if i < steps:
                    h, qc = divmod(i, 2)
                    n, s = (qc + 1) * P, i % NS
                    dve.wait_ge(sem("masked"), i + 1)
                    link(dve.tensor_reduce(fox_stat[:, 6, h:h + 1], sc[s][:, 1, 0:n], AX_X, ALU.max))
                    ts(fox_stat[:, 2 * qc, h:h + 1], fox_stat[:, 6, h:h + 1], -1.0, None, ALU.mult).then_inc(sem("max_ready"), 1)
                if 3 <= i < steps + 3:
                    j = i - 3
                    n, s = (j % 2 + 1) * P, j % NS
                    dve.wait_ge(sem("turned"), j + 1)
                    if j >= NS:
                        dve.wait_ge(sem("pv_done"), j - NS + 1)
                    dve.tensor_copy(pt[s][:, 0:n], pb[2 + j % 2][:, 0:n]).then_inc(sem("pt_ready"), 1)
                if i >= 4 and (i - 4) % 4 == 3:
                    m = (i - 4) // 4
                    dve.wait_ge(sem("pv_done"), 4 * (m + 1))
                    dve.wait_ge(sem("fox_gate"), 1)
                    tt(o_fox[:, m, :], pb[4 + m % 2][:, 0:T], gate_t[:, m, :], ALU.mult).then_inc(sem("o_ready"), 1)
                    if m >= 1:
                        o_rest(m - 1)
            o_rest(KC - 1)
            dve_layer(dve, L["fox_out"], residual)
            ahead(dve_rest, dve, L["up2"])
            norm_begin(5)
            ffn(2, L["up2"], L["down2"], residual)
            dve.wait_ge(sem("x_ready"), KC * 7)
            norm_scale(6)
            for k in range(KC):
                stt(tile(16, k), x_res[:, k, :], par_col("final_norm_g_2", k), rstd[:, :], ALU.mult, ALU.mult).then_inc(sem("y_ready"), 1)
            for i in range(4):
                c, b = divmod(i, 2)
                dve.wait_ge(sem("x_turned"), 4 + i + 1)
                dve.tensor_copy(y_tok[:, c, 512 * b:512 * b + 512], pb[3 + i][:, :]).then_inc(sem("y_tok_ready"), 1)

        @block.tensor
        def _(pe):
            mm = pe.matmul

            def sum_squares(n, bank=7):
                for k in range(KC):
                    pe.wait_ge(sem("sq_ready"), KC * n + k + 1)
                    ins = mm(pb[bank][:, 0:T], ones[:, :], sub[:, k, :], start=k == 0, stop=k == KC - 1)
                ins.then_inc(sem("ssq_done"), 1)

            def head_sums(src, bank0=4):
                for k in range(KC):
                    ins = mm(pb[bank0 + k // 2][:, T * (k % 2):T * (k % 2) + T], blk[:, :], src[:, k, :], start=True, stop=True)
                return ins

            def feature_sums(o, src):
                for k in range(KC):
                    ins = mm(o, ones[:, :], src[:, k, :], start=k == 0, stop=k == KC - 1)
                return ins

            def turn(o, i):
                n = i.shape[0]
                return pe.transpose(o, i, ident[0:n, 0:n])

            for i in range(BANKS):
                pe.nop().then_inc(sem("block_done"), 1)
            pe.wait_ge(sem("const_ready"), 1)
            pe.wait_ge(sem("par_loaded"), 16 * par_dmas)
            for t in range(par_tiles):
                n = min(P, n_rows - P * t)
                ins = turn(pb[1 + t // 4][:, P * (t % 4):P * (t % 4) + n], par_tok[0:n, t, :])
                if t % 4 == 3 or t == par_tiles - 1:
                    ins.then_inc(sem("par_turned"), 1)
            pe.wait_ge(sem("x_loaded"), 16)
            for k in range(KC):
                for c in range(2):
                    ins = turn(pb[3 + k // 2][:, T * (k % 2) + P * c:T * (k % 2) + P * c + P], x_tok[:, c, P * k:P * k + P])
                if k % 2:
                    ins.then_inc(sem("x_turned"), 1)
            sum_squares(0)
            pe_layer(pe, L["rkv"], x_hi, x_lo, "x_lo_ready", X_BASE[0])

            s = L["lora_in"].u0 % 2
            pe.wait_ge(sem(f"landed{s}"), L["lora_in"].landed[0])
            for i, (c, n, src) in enumerate(((0, 64, KK), (64, 64, A), (128, 128, G))):
                pe.wait_ge(sem("lora_x"), KC * (i + 1))
                for k in range(KC):
                    ins = mm(pb[4 + i][0:n, 0:T], raw[s][:, k, c:c + n], slot(src)[:, k, :], start=k == 0, stop=k == KC - 1)
                ins.then_inc(sem("lora1_done"), 1)
            s = L["lora_out"].u0 % 2
            pe.wait_ge(sem(f"landed{s}"), L["lora_out"].landed[0])
            w2 = raw[s][:, :, :].rearrange("p k n -> p (k n)")
            for f, (rows, src) in enumerate(((64, lora_w), (64, lora_a), (128, lora_g))):
                pe.wait_ge(sem("lora_mid"), 3)
                for j in range(4):
                    i = 4 * f + j
                    if i >= 3:
                        pe.wait_ge(sem("lora_ready"), i - 2)
                    for m in (2 * j, 2 * j + 1):
                        ins = mm(pb[4 + i % 3][:, T * (m % 2):T * (m % 2) + T], w2[0:rows, D * f + P * m:D * f + P * m + P], src,
                                 start=True, stop=True)
                    ins.then_inc(sem("lora2_done"), 1)
            pe.wait_ge(sem("lora_ready"), 12)
            pe.wait_ge(sem("kk_sq"), 1)
            head_sums(slot(TMP)).then_inc(sem("kk_sum"), 1)

            def bonus_sums(u, m):
                if M_PER_UNIT * u + m == 1:
                    pe.wait_ge(sem("bonus_in"), 1)
                    for k in range(KC):
                        ins = mm(pb[4][0:RWKV_HEADS, 0:T], head_sel[:, k, :], mix_tmp[:, k, :], start=k == 0, stop=k == KC - 1)
                    ins.then_inc(sem("bonus_done"), 1)
            pe_layer(pe, L["ug"], x_hi, x_lo, "x_lo_ready", X_BASE[0], bonus_sums)
            pe.wait_ge(sem("scan_in"), 1)
            for c in range(NCHUNK):
                if c >= 2:
                    pe.wait_ge(sem("lab_ready"), c - 1)
                for h in range(RWKV_HEADS):
                    m, rows = h // 2, slice(64 * (h % 2), 64 * (h % 2) + 64)
                    ins = mm(pb[4 + 2 * (h % 2) + c % 2][0:CHUNK, CHUNK * m:CHUNK * m + CHUNK], bk[rows, m, c, 1, :],
                             slot(KK)[rows, m, CHUNK * c:CHUNK * c + CHUNK], start=True, stop=True)
                ins.then_inc(sem("lab_done"), 1)
            pe_layer(pe, L["z"], x_hi, x_lo, "x_lo_ready", X_BASE[0])

            def chunk_products(c):
                if c == 0:
                    pe.wait_ge(sem("pool_stages"), 1)
                if c:
                    pe.wait_ge(sem("bk_rows"), c)
                    pe.wait_ge(sem("v_rows"), c)
                t = slice(CHUNK * c, CHUNK * c + CHUNK)
                for h in range(RWKV_HEADS):
                    m, rows = h // 2, slice(64 * (h % 2), 64 * (h % 2) + 64)
                    ins = mm(pb[h % 2][64:128, 64 * m:64 * m + 64], bk[rows, m, c, :, :].rearrange("p j s -> p (j s)"),
                             pj4[rows, 0:KK + 1:KK, m, t], start=True, stop=True)
                ins.then_inc(sem("g_done"), 1)
                for m in range(KC):
                    ins = turn(pb[2 + m // 4][0:CHUNK, P * (m % 4):P * (m % 4) + P], slot(V)[:, m, t])
                ins.then_inc(sem("v_turned"), 1)

            def chunk_keys(c):
                pe.wait_ge(sem("g_masked"), c + 1)
                pe.wait_ge(sem("bk_scaled"), c + 1)
                for m in range(KC):
                    ins = turn(pb[m // 4][0:64, P * (m % 4):P * (m % 4) + P], bk[:, m, c, :, :].rearrange("p j s -> p (j s)"))
                ins.then_inc(sem("bk_turned"), 1)

            pe.wait_ge(sem("evac_done"), L["z"].evac1 + BANKS)
            chunk_products(0)
            chunk_keys(0)
            pe.wait_ge(sem("sub_dma"), 64)
            for c in range(NCHUNK):
                t, q = slice(CHUNK * c, CHUNK * c + CHUNK), c % 2
                pe.wait_ge(sem("v_rows"), c + 1)
                pe.wait_ge(sem("g_masked"), c + 1)
                if c:
                    pe.wait_ge(sem("u_rows_v"), c)
                    pe.wait_ge(sem("u_rows_a"), c)
                for h in range(RWKV_HEADS):
                    mm(pb[4 + h // 8][0:CHUNK, 64 * (h % 8):64 * (h % 8) + 64], g_buf[q][0:CHUNK, h, CHUNK:2 * CHUNK],
                       uv[q][0:CHUNK, 64 * h:64 * h + 64], start=h % 8 == 0, stop=False, skip_group_check=True)
                pe.wait_ge(sem("state_ready"), c + 1)
                for m in range(KC):
                    ins = mm(pb[4 + m // 4][0:CHUNK, P * (m % 4):P * (m % 4) + P], slot(KK)[:, m, t], state[:, m, :],
                             start=False, stop=m % 4 == 3, skip_group_check=True)
                ins.then_inc(sem("x_done"), 1)
                if c == NCHUNK - 1:
                    pe.wait_ge(sem("conv_ready"), 1)
                    pe.wait_ge(sem("tap_summed"), CONV_TAPS - 1)
                    feature_sums(pb[6][:, 0:T], slot(GATE)).then_inc(sem("ln_mean"), 1)
                if c:
                    pe.wait_ge(sem("y_out"), c)
                for m in range(KC):
                    ins = mm(pb[7][:, CHUNK * m:CHUNK * m + CHUNK], state[:, m, :], slot(R)[:, m, t],
                             start=m == 0, stop=False, skip_group_check=True)
                ins.then_inc(sem("y1_done"), 1)
                if c + 1 < NCHUNK:
                    chunk_products(c + 1)
                pe.wait_ge(sem("x_rows_v"), c + 1)
                pe.wait_ge(sem("x_rows_a"), c + 1)
                for h in range(RWKV_HEADS):
                    ins = mm(pb[4 + h // 8][0:CHUNK, 64 * (h % 8):64 * (h % 8) + 64], lab_t[:, 16 * c + h, :],
                             x_buf[:, 64 * h:64 * h + 64], start=True, stop=True)
                ins.then_inc(sem("u_done"), 1)
                if c + 1 < NCHUNK:
                    chunk_keys(c + 1)
                pe.wait_ge(sem("u_rows_v"), c + 1)
                pe.wait_ge(sem("u_rows_a"), c + 1)
                pe.wait_ge(sem("bk_rows"), c + 1)
                if c + 1 < NCHUNK:
                    for h in range(RWKV_HEADS):
                        ins = mm(pb[6][64 * (h % 2):64 * (h % 2) + 64, 64 * (h // 2):64 * (h // 2) + 64],
                                 bk_t[q][:, 64 * h:64 * h + 64], uv[q][:, 64 * h:64 * h + 64], start=True, stop=True)
                    ins.then_inc(sem("s_done"), 1)
                for h in range(RWKV_HEADS):
                    ins = mm(pb[7][64 * (h % 2):64 * (h % 2) + 64, CHUNK * (h // 2):CHUNK * (h // 2) + CHUNK],
                             uv[q][:, 64 * h:64 * h + 64], g_buf[q][:, h, 0:CHUNK], start=False, stop=h >= 14, skip_group_check=True)
                ins.then_inc(sem("y2_done"), 1)
            pe.wait_ge(sem("ln_sq"), 1)
            feature_sums(pb[6][:, T:2 * T], slot(U)).then_inc(sem("ln_var"), 1)
            pe.wait_ge(sem("ln_root"), 1)
            pe.wait_ge(sem("y_out"), NCHUNK)
            head_sums(slot(R)).then_inc(sem("gn_mean"), 1)
            pe.wait_ge(sem("gn_sq"), 1)
            head_sums(tmp2).then_inc(sem("gn_var"), 1)

            def bonus_heads(u, m):
                if M_PER_UNIT * u + m == 0:
                    pe.wait_ge(sem("gn_root"), 1)
                    for h in range(RWKV_HEADS):
                        m = h // 2
                        ins = mm(pb[4 + m // 2][64 * (h % 2):64 * (h % 2) + 64, T * (m % 2):T * (m % 2) + T],
                                 ident[0:RWKV_HEADS, h:h + 1].broadcast_to([RWKV_HEADS, 64]), bonus, start=True, stop=True)
                    ins.then_inc(sem("bonus_out"), 1)
            pe_layer(pe, L["conv_out"], x_hi, x_lo, "x_lo_ready", KC, bonus_heads)
            pe_layer(pe, L["rwkv_out"], y_hi, y_lo, "x_lo_ready", 2 * KC)
            pe_layer(pe, L["w_out"], x_hi, x_lo, "x_lo_ready", 3 * KC)

            def post_squares(i):
                for k in range(KC):
                    pe.wait_ge(sem("osq_ready"), KC * i + k + 1)
                    ins = mm(pb[7][:, 0:T], ones[:, :], sub[:, k, :], start=k == 0, stop=k == KC - 1)
                ins.then_inc(sem("osum_done"), 1)

            post_squares(0)
            sum_squares(1)
            pe_layer(pe, L["up0"], x_hi, x_lo, "x_lo_ready", X_BASE[1])
            pe_layer(pe, L["down0"], act_hi, act_lo, "act_lo_ready", 0)
            post_squares(1)
            sum_squares(2)

            def narrow_product(ly, n, nth):
                s = ly.u0 % 2
                pe.wait_ge(sem(f"landed{s}"), ly.landed[0])
                pe.wait_ge(sem("gain_ready"), KC * nth)
                for k in range(KC):
                    ins = mm(pb[4][0:n, 0:T], raw[s][:, k, 0:n], x_gain[:, k, :], start=k == 0, stop=k == KC - 1)
                ins.then_inc(sem("narrow_done"), 1)

            pe_layer(pe, L["ssd_z"], x_hi, x_lo, "x_lo_ready", X_BASE[2])
            pe_layer(pe, L["ssd_xbc"], x_hi, x_lo, "x_lo_ready", X_BASE[2])
            narrow_product(L["ssd_dt"], SSD_HEADS, 1)
            pe.wait_ge(sem("xbc_ready"), M_PER_UNIT + SSD_XBC)
            for c in range(2):
                t = slice(P * c, P * c + P)
                for g in range(SSD_GROUPS):
                    ins = mm(pb[6 + c][:, P * g:P * g + P], xbc[:, 16 + g, t], xbc[:, 20 + g, t], start=True, stop=True)
                ins.then_inc(sem("cb_done"), 1)
            for g in range(SSD_GROUPS):
                ins = turn(pb[5][:, P * g:P * g + P], xbc[:, 16 + g, 0:P])
            ins.then_inc(sem("b_turned"), 1)
            pe.wait_ge(sem("da_ready"), 1)
            for i, src in enumerate((dt_z[:, 0:P], dt_z[:, P:T], dt[:, 0:P], dt[:, P:T], da_end)):
                ins = turn(pb[4][:, SSD_HEADS * i:SSD_HEADS * i + SSD_HEADS], src)
            ins.then_inc(sem("heads_turned"), 1)
            pe.wait_ge(sem("cbm_ready"), 2)
            for i in range(8):
                c, b = divmod(i, 4)
                if i >= 2:
                    pe.wait_ge(sem("xdt_ready"), i - 1)
                for r in range(4):
                    ins = turn(pb[6 + i % 2][:, P * r:P * r + P], xbc[:, 4 * b + r, P * c:P * c + P])
                ins.then_inc(sem("xs_turned"), 1)
            pe.wait_ge(sem("heads_ready"), 1)
            pe.wait_ge(sem("b_tok_ready"), 1)

            def on_head(o, h, src):
                return mm(o, ident[0:SSD_HEADS, h:h + 1].broadcast_to([SSD_HEADS, o.shape[0]]), src, start=True, stop=True)

            for b in range(4):
                if b >= 2:
                    pe.wait_ge(sem("eab_ready"), b - 1)
                for h in range(8 * b, 8 * b + 8):
                    m = h // 2
                    ins = on_head(pb[4 + b % 2][64 * (h % 2):64 * (h % 2) + 64, P * (m % 4):P * (m % 4) + P], h, da_exp)
                ins.then_inc(sem("eab_done"), 1)
            pe.wait_ge(sem("xdt_end_ready"), 1)
            pe.wait_ge(sem("xdt_ready"), 8)
            for g in range(SSD_GROUPS):
                if g >= 2:
                    pe.wait_ge(sem("st_ready"), g - 1)
                mm(pb[6 + g % 2][:, :], b_tok[:, g, :], xdt_end[:, 512 * g:512 * g + 512], start=True, stop=True).then_inc(sem("st_done"), 1)
            pe.wait_ge(sem("eab_ready"), 4)
            for b in range(4):
                pe.wait_ge(sem("st_ready"), b + 1)
                if b >= 2:
                    pe.wait_ge(sem("eab_used"), b - 1)
                for m in range(4 * b, 4 * b + 4):
                    ins = mm(pb[4 + b % 2][:, P * (m % 4):P * (m % 4) + P], st_ssd[:, P * m:P * m + P], xbc[:, 20 + b, P:T], start=True, stop=True)
                ins.then_inc(sem("yoff_done"), 1)
            pe.wait_ge(sem("evac_done"), L["ssd_xbc"].evac1 + BANKS)
            def group_squares(g):
                pe.wait_ge(sem("yz_sq"), 2 * (g + 1))
                for m in range(4):
                    ins = mm(pb[4 + g][:, 0:T], ones[:, :], sub[:, 4 * (g % 2) + m, :], start=m == 0, stop=m == 3)
                ins.then_inc(sem("yz_sum"), 1)

            for i in range(17):
                if i < 16:
                    c, hq = divmod(i, 8)
                    if i >= 2:
                        pe.wait_ge(sem("att_exp"), i - 1)
                    pe.wait_ge(sem("seg_ready"), i + 1)
                    mm(pb[i % 2][:, :], later[:, :], seg[i % 2], start=True, stop=True).then_inc(sem("bc_done"), 1)
                if i >= 1:
                    j = i - 1
                    c, hq = divmod(j, 8)
                    pe.wait_ge(sem("att_ready"), j + 1)
                    if j >= 2:
                        pe.wait_ge(sem("y_out_ssd"), j - 1)
                    for r in range(4):
                        h = 4 * hq + r
                        ins = mm(pb[2 + j % 2][64 * (h % 2):64 * (h % 2) + 64, P * (r // 2):P * (r // 2) + P],
                                 xdt[:, c, 64 * h:64 * h + 64], att[j % NATT][:, r, :], start=True, stop=True)
                    ins.then_inc(sem("y_done"), 1)
                if i in (13, 15):
                    group_squares((i - 13) // 2)
            for g in (2, 3):
                group_squares(g)
            pe.wait_ge(sem("y_out_ssd"), 16)
            pe_layer(pe, L["ssd_out"], yz_hi, yz_lo, "yz_lo_ready", 0)
            sum_squares(3)
            pe_layer(pe, L["up1"], x_hi, x_lo, "x_lo_ready", X_BASE[3])
            pe_layer(pe, L["down1"], act_hi, act_lo, "act_lo_ready", FC * 1)
            sum_squares(4)

            def q_sums(u, m):
                if (u, m) == (2, 2):
                    pe.wait_ge(sem("fox_sq"), 1)
                    head_sums(fox_tmp).then_inc(sem("fox_sum"), 1)
            pe_layer(pe, L["fox_qk"], x_hi, x_lo, "x_lo_ready", X_BASE[4], q_sums)
            pe.wait_ge(sem("fox_root"), 4)
            narrow_product(L["fox_f"], FOX_HEADS, 2)

            def vg_products(u, m):
                if (u, m) == (0, 2):
                    pe.wait_ge(sem("fox_sq"), 2)
                    pe.wait_ge(sem("abs_ready"), 2)
                    head_sums(fox_tmp).then_inc(sem("fox_sum"), 1)
                if (u, m) == (2, 0):
                    pe.wait_ge(sem("cum_fox"), 1)
                    pe.wait_ge(sem("fox_root"), 8)
                    for c in range(2):
                        ins = turn(pb[4][:, FOX_HEADS * c:FOX_HEADS * c + FOX_HEADS], acs[0:FOX_HEADS, P * c:P * c + P])
                    ins.then_inc(sem("cq_turned"), 1)
                if (u, m) == (2, 3):
                    pe.wait_ge(sem("cq_ready"), 1)
                    for i in range(4):
                        for r in range(4):
                            t = 4 * (i % 2) + r
                            ins = turn(pb[4 + i][:, P * r:P * r + P], v_t[:, t, P * (i // 2):P * (i // 2) + P])
                        ins.then_inc(sem("v_fox_turned"), 1)
            pe_layer(pe, L["fox_vg"], x_hi, x_lo, "x_lo_ready", X_BASE[4], vg_products)
            pe.wait_ge(sem("evac_done"), L["fox_vg"].evac1 + BANKS)
            pe.wait_ge(sem("qk_ready"), 2)
            pe.wait_ge(sem("v_fox_ready"), 4)
            steps = 2 * FOX_HEADS
            for i in range(steps + 4):
                if i < steps:
                    h, qc = divmod(i, 2)
                    m, rows, n = h // 2, slice(64 * (h % 2), 64 * (h % 2) + 64), (qc + 1) * P
                    bank = pb[score_banks[i % NS]]
                    if i >= NS:
                        pe.wait_ge(sem("masked"), i - NS + 1)
                    mm(bank[:, 0:n], q_t[rows, m, P * qc:P * qc + P], k_t[rows, m, 0:n], start=True, stop=False)
                    mm(bank[:, 0:n], ident[0:FOX_HEADS, h:h + 1].broadcast_to([FOX_HEADS, P]), cum_neg[0:FOX_HEADS, 0:n],
                       start=False, stop=True).then_inc(sem("score_done"), 1)
                if 3 <= i < steps + 3:
                    j = i - 3
                    pe.wait_ge(sem("p_ready"), j + 1)
                    if j >= 2:
                        pe.wait_ge(sem("pt_ready"), j - 1)
                    for b in range(j % 2 + 1):
                        ins = turn(pb[2 + j % 2][:, P * b:P * b + P], sc[j % NS][:, 0, P * b:P * b + P])
                    ins.then_inc(sem("turned"), 1)
                if i >= 4:
                    j = i - 4
                    h, qc = divmod(j, 2)
                    m = h // 2
                    pe.wait_ge(sem("pt_ready"), j + 1)
                    if m >= 2:
                        pe.wait_ge(sem("o_ready"), m - 1)
                    for b in range(qc + 1):
                        ins = mm(pb[4 + m % 2][64 * (h % 2):64 * (h % 2) + 64, P * qc:P * qc + P],
                                 v_tok[:, b, 64 * h:64 * h + 64], pt[j % NS][:, P * b:P * b + P], start=b == 0, stop=b == qc)
                    ins.then_inc(sem("pv_done"), 1)
            pe_layer(pe, L["fox_out"], x_hi, x_lo, "x_lo_ready", X_BASE["fox"])
            sum_squares(5)
            pe_layer(pe, L["up2"], x_hi, x_lo, "x_lo_ready", X_BASE[5])
            pe_layer(pe, L["down2"], act_hi, act_lo, "act_lo_ready", FC * 2)
            sum_squares(6)
            for i in range(4):
                c, b = divmod(i, 2)
                pe.wait_ge(sem("y_ready"), 4 * b + 4)
                for r in range(4):
                    ins = turn(pb[3 + i][:, P * r:P * r + P], tile(16, 4 * b + r)[:, P * c:P * c + P])
                ins.then_inc(sem("x_turned"), 1)


def kernel(**inputs):
    import numpy as _np
    import concourse.bacc as _bacc
    from concourse import mybir as _mybir
    from concourse.bass_utils import run_bass_kernel_spmd as _run

    nc = _bacc.Bacc("TRN2", target_bir_lowering=False, num_devices=1)
    arrays, args = {}, {}
    for name, value in inputs.items():
        v = _np.ascontiguousarray(value)
        if v.size == 0:
            continue
        arrays[f"in_{name}_dram"] = v
        args[name] = nc.dram_tensor(f"in_{name}_dram", v.shape, _mybir.dt.from_np(v.dtype), kind="ExternalInput").ap()
    out = nc.dram_tensor("out_0_dram", (1, T, D), F32, kind="ExternalOutput").ap()
    build(nc, args, out)
    r = _run(nc, [arrays], core_ids=[0])
    return r.results[0]["out_0_dram"]
```

```python
from contextlib import ExitStack

import concourse.bass as bass
from concourse import mybir

F32 = mybir.dt.float32
F32R = mybir.dt.float32r
ALU = mybir.AluOpType
ACT = mybir.ActivationFunctionType
AX_X = mybir.AxisListType.X

P = 128
T = 256
D = 1024
KC = D // P
FF = 2816
FC = FF // P
UNIT_COLS = 512
M_PER_UNIT = UNIT_COLS // P
LOOKAHEAD = 3
EXP_MINUS_HALF = 0.6065306597126334
RMS_EPS, LN_EPS, GN_EPS = 1e-6, 1e-5, 64e-5

RWKV_HEADS, HEAD = 16, 64
CHUNK = 32
NCHUNK = T // CHUNK
CONV_TAPS = 31
SSD_INNER, SSD_HEADS, SSD_GROUPS, SSD_TAPS = 2048, 32, 4, 4
SSD_Z, SSD_XBC = SSD_INNER // P, (SSD_INNER + 2 * SSD_GROUPS * P) // P
FOX_HEADS = 16
GLU_TAPS = 3
MASKED = -1e30


class Layer:

    def __init__(self, name, sources, nkc, k_split=1, dmas=(1, 1)):
        self.name, self.sources, self.nkc, self.k_split, self.dmas = name, sources, nkc, k_split, dmas

    def __len__(self):
        return len(self.nkc)

    def first_k(self, u):
        g = u % self.k_split
        return sum(self.nkc[:g])


def params_of(a):
    out = []
    for name in ("pre_mix_norm", "post_mix_norm", "pre_ffn_norm", "post_ffn_norm", "mu_rkv", "mu_wag", "decay_w0",
                 "a_0", "k_k", "k_a", "r_k", "gn_w", "gn_b", "conv_dw", "conv_b", "conv_ln_w", "conv_ln_b",
                 "mix_norm_g_2", "ffn_norm_g_2", "ssd_conv_w_2", "ssd_conv_b_2", "ssd_norm_g_2",
                 "ffn_conv_w_2", "ffn_conv_b_2", "final_norm_g_2"):
        ap = a[name]
        names = " ".join(f"d{i}" for i in range(len(ap.shape)))
        flat = ap.rearrange(f"{names} -> ({names})")
        n = flat.shape[0] // P
        out.append((name, n, flat.rearrange("(n p) -> n p", p=P)))
    return out


def build(nc, a, out):
    ctx = ExitStack()
    with ctx:
        sems = {}

        def sem(name):
            if name not in sems:
                sems[name] = ctx.enter_context(nc.semaphore(name))
            return sems[name]

        def sb(name, shape, dt=F32):
            return ctx.enter_context(nc.sbuf_tensor(name, shape, dt))

        raw = [sb(f"raw{i}", [P, KC, UNIT_COLS]) for i in range(2)]
        w_hi = [sb(f"w_hi{i}", [P, KC, P], F32R) for i in range(M_PER_UNIT)]
        w_lo = [sb(f"w_lo{i}", [P, KC, P], F32R) for i in range(M_PER_UNIT)]
        x_res = sb("x_res", [P, KC, T])
        x_hi = sb("x_hi", [P, KC, T], F32R)
        x_lo = sb("x_lo", [P, KC, T], F32R)
        sub_base = nc.sbuf_base
        sub = sb("sub", [P, 12, T])
        arena_base = nc.sbuf_base
        pj = sb("pj", [P, 96, T])
        ident = sb("ident", [P, P])
        ones = sb("ones", [P, P])
        blk = sb("blk", [P, P])
        tri = sb("tri", [P, P])
        later = sb("later", [P, P])
        scan_mask = sb("scan_mask", [P, T])
        g_mask = sb("g_mask", [P, 2 * CHUNK])
        head_sel = sb("head_sel", [P, KC, RWKV_HEADS])
        eps = sb("eps", [P, 3])
        rs = sb("rs", [P, T])
        rstd = sb("rstd", [P, T])
        small = sb("small", [SSD_HEADS, T])
        bonus = small[0:RWKV_HEADS, :]
        chunk_decay = sb("chunk_decay", [P, KC, NCHUNK])
        heads_col = sb("heads_col", [SSD_HEADS, 4])
        fox_g = sb("fox_g", [P, 4])
        d_skip = sb("d_skip", [P, SSD_Z])

        par_rows = params_of(a)
        col, n_rows = {}, 0
        for name, n, _ in par_rows:
            col[name] = n_rows
            n_rows += n
        par_tiles = -(-n_rows // P)
        par = sb("par", [P, n_rows])

        def slot(i):
            return pj[:, 8 * i:8 * i + 8, :]

        R, K, V, U, GATE, BK, KK, A, TMP, W, G = 0, 1, 2, 3, 4, 5, 7, 8, 9, 10, 11
        ZR, ZC, OUT1 = K, A, R
        mix_tmp, rate_tmp = slot(BK), slot(BK + 1)
        y_hi = nc.alloc_sbuf_tensor_at("y_hi", [P, KC, T], F32R, offset=arena_base + 8 * BK * T * 4)
        y_lo = nc.alloc_sbuf_tensor_at("y_lo", [P, KC, T], F32R, offset=arena_base + 8 * (BK + 1) * T * 4)
        POOL_TILES = 3
        tap_prod = [slot(ZC)[:, POOL_TILES * i:POOL_TILES * (i + 1), :] for i in range(2)]
        Z_EARLY, Z_CHUNK = 2, 2
        DVE_EARLY, DVE_CHUNK = 7, 4
        LAB_BLOCK, SUB_BLOCK, SUB_STEPS = 6, 11, 3
        EARLY_TAPS, CHUNK_TAPS = 12, 7
        x_tok = pj[:, 40:48, :].rearrange("p a b -> p (a b)").rearrange("p (c d) -> p c d", c=2)
        par_tok = pj[:, 48:52, :].rearrange("p a b -> p (a b)")[:, 0:par_tiles * P].rearrange("p (t c) -> p t c", c=P)
        tmp2 = sub[:, 0:8, :]
        lora_w, lora_a, lora_g = sub[0:64, 8, :], sub[0:64, 9, :], sub[:, 10, :]
        bk = pj[:, 40:56, :].rearrange("p a b -> p (a b)").rearrange("p (k c j s) -> p k c j s", k=KC, c=NCHUNK, j=2)
        region = pj[:, 72:88, :].rearrange("p a b -> p (a b)")
        lab_t = region[0:CHUNK, :].rearrange("s (y t) -> s y t", t=CHUNK)
        g_buf = [region[64:128, 1024 * q:1024 * q + 1024].rearrange("p (h n) -> p h n", h=RWKV_HEADS) for q in range(2)]
        uv = [region[64:128, 2048 + 1024 * q:3072 + 1024 * q] for q in range(2)]
        flat_sub = sub[:, :, :].rearrange("p a b -> p (a b)")
        lt = flat_sub[:, 0:1024].rearrange("p (s t) -> p s t", t=CHUNK)
        mt = flat_sub[:, 1024:2048].rearrange("p (s t) -> p s t", t=CHUNK)
        prod = flat_sub[:, 2048:3072].rearrange("p (s t) -> p s t", t=CHUNK)
        bk_t = [flat_sub[64:128, 1024 * q:1024 * q + 1024] for q in range(2)]
        x_buf = flat_sub[0:CHUNK, 0:1024]
        state = flat_sub[:, 2048:3072].rearrange("p (m v) -> p m v", m=KC)
        act_hi = nc.alloc_sbuf_tensor_at("act_hi", [P, FC, T], F32R, offset=arena_base)
        act_lo = nc.alloc_sbuf_tensor_at("act_lo", [P, FC, T], F32R, offset=arena_base + FC * T * 4)
        OUT_FFN = 8
        g_tile = [sub[:, i, :] for i in (0, 1)]
        s_tile = [sub[:, i, :] for i in (2, 3)]
        u_tile = [sub[:, i, :] for i in (4, 5)]
        a_tile = [sub[:, i, :] for i in (6, 7)]
        c_tile = [sub[:, i, :] for i in (8, 9)]
        z_t, xbc, y_ssd = pj[:, 0:16, :], pj[:, 16:40, :], pj[:, 40:56, :]
        x_gain = pj[:, 40:48, :]
        z_sig = pj[:, 56:72, :]
        xdt = pj[:, 56:72, :].rearrange("p a b -> p (a b)").rearrange("p (c f) -> p c f", c=2)
        xdt_end = pj[:, 72:80, :].rearrange("p a b -> p (a b)")
        NATT = 4
        att = [pj[:, t:t + 2, :].rearrange("p a b -> p (a b)").rearrange("p (h l) -> p h l", l=P) for t in (80, 82, 72, 74)]
        seg = [pj[:, t:t + 2, :].rearrange("p a b -> p (a b)") for t in (76, 78)]
        cbm = pj[:, 84:88, :].rearrange("p a b -> p (a b)").rearrange("p (c g l) -> p c g l", c=2, g=SSD_GROUPS)
        st_ssd = pj[:, 88:96, :].rearrange("p a b -> p (a b)")
        conv_in = [sub[:, i, :] for i in range(4)]
        conv_sig = [sub[:, 4 + i, :] for i in range(4)]
        dt_z, dt_e, dt, acs = (sub[0:SSD_HEADS, i, :] for i in (8, 9, 10, 11))
        tok_heads = sb("tok_heads", [P, 5, SSD_HEADS])
        da_end, da_exp = small[:, 0:P], small[:, P:T]
        eab = sub[:, 0:8, :].rearrange("p a b -> p (a b)").rearrange("p (m l) -> p m l", l=P)
        b_tok = x_gain[:, 0:2, :].rearrange("p a b -> p (a b)").rearrange("p (g n) -> p g n", g=SSD_GROUPS)
        yz_hi = nc.alloc_sbuf_tensor_at("yz_hi", [P, SSD_Z, T], F32R, offset=arena_base + 56 * T * 4)
        yz_lo = nc.alloc_sbuf_tensor_at("yz_lo", [P, SSD_Z, T], F32R, offset=arena_base + 16 * T * 4)
        q_t, k_t, v_t, gate_t = (pj[:, 8 * i:8 * i + 8, :] for i in range(4))
        fox_tmp = pj[:, 32:40, :]
        v_tok = pj[:, 48:56, :].rearrange("p a b -> p (a b)").rearrange("p (c f) -> p c f", c=2)
        NS = 4
        score_banks = (0, 1, 6, 7)
        sc = [pj[:, 56 + 2 * i:58 + 2 * i, :] for i in range(NS)]
        pt = [pj[:, 64 + 2 * i:66 + 2 * i, :].rearrange("p a b -> p (a b)") for i in range(NS)]
        o_fox = pj[:, 72:80, :]
        fox_stat = pj[:, 80, :].rearrange("p (s h) -> p s h", h=FOX_HEADS)
        fox_mask = pj[:, 81, :]
        pj4 = pj[:, :, :].rearrange("p (s k) t -> p s k t", k=KC)
        y_tok = pj[:, 0:8, :].rearrange("p a b -> p (a b)").rearrange("p (c d) -> p c d", c=2)
        cum_neg = dt_z

        pb = [ctx.enter_context(nc.psum_tensor(f"pb{i}", [P, 512], F32)) for i in range(8)]
        sub_in = nc.dram_tensor("sub_in", [CHUNK, P, CHUNK], F32, kind="Internal").ap()

        HALF = UNIT_COLS // 2
        halves = (slice(0, HALF), slice(HALF, UNIT_COLS))

        def cols(ap, first):
            v = ap.rearrange("(k p) n -> p k n", p=P)
            return lambda u: [(c, v[:, :, bass.ds(first + UNIT_COLS * u + c.start, HALF)]) for c in halves]

        def gate_up(g, up):
            parts = [w.rearrange("(k p) n -> p k n", p=P) for w in (g, up)]
            return lambda u: [(c, v[:, :, bass.ds(HALF * u, HALF)]) for c, v in zip(halves, parts)]

        def k_split(ap, nkc, parts):
            v = ap.rearrange("(k p) n -> p k n", p=P)

            def source(u):
                k0 = sum(nkc[:u % parts])
                n0 = UNIT_COLS * (u // parts)
                return [(c, v[:, k0:k0 + nkc[u % parts], n0 + c.start:n0 + c.stop]) for c in halves]
            return source

        w_in = a["w_in"][0]
        down_kc = [8, 7, 7]
        up2, down2 = a["ffn_w_up_2"], a["ffn_w_down_2"]
        L = {}
        order = []

        def layer(name, sources, nkc, **kw):
            L[name] = Layer(name, sources, nkc, **kw)
            order.append(L[name])

        def lora_in(u):
            return [(slice(0, 64), a["decay_w1"][0].rearrange("(k p) n -> p k n", p=P)),
                    (slice(64, 128), a["a_1"][0].rearrange("(k p) n -> p k n", p=P)),
                    (slice(128, 256), a["g_1"][0].rearrange("(k p) n -> p k n", p=P))]

        def narrow(ap, first, n):
            return lambda u: [(slice(0, n), ap.rearrange("(k p) n -> p k n", p=P)[:, :, first:first + n])]

        layer("rk", cols(w_in, 0), [KC] * 4)
        layer("lora_in", lora_in, [KC], dmas=(3, 0))
        layer("lora_out", None, [KC], dmas=(3, 0))
        layer("v", cols(w_in, 2 * D), [KC] * 2)
        layer("ug", cols(w_in, 3 * D), [KC] * 4)
        layer("z", cols(w_in, 5 * D), [KC] * 4)
        layer("conv_out", cols(a["w_conv_out"][0], 0), [KC] * 2)
        layer("rwkv_out", cols(a["w_rwkv_out"][0], 0), [KC] * 2)
        layer("w_out", cols(a["w_out"][0], 0), [KC] * 2)
        layer("up0", gate_up(a["ffn_w_gate"][0], a["ffn_w_up"][0]), [KC] * 11)
        layer("down0", k_split(a["ffn_w_down"][0], down_kc, 3), down_kc * 2, k_split=3)
        layer("ssd_z", cols(a["ssd_w_in_2"][0], 0), [KC] * 4)
        layer("ssd_xbc", cols(a["ssd_w_in_2"][0], SSD_INNER), [KC] * 6)
        layer("ssd_dt", narrow(a["ssd_w_in_2"][0], 5120, SSD_HEADS), [KC], dmas=(1, 0))
        layer("ssd_out", k_split(a["ssd_w_out_2"][0], [8, 8], 2), [8, 8] * 2, k_split=2)
        layer("up1", gate_up(up2[0][:, 0:FF], up2[0][:, FF:2 * FF]), [KC] * 11)
        layer("down1", k_split(down2[0], down_kc, 3), down_kc * 2, k_split=3)
        layer("fox_qk", cols(a["fox_w_in_2"][0], 0), [KC] * 4)
        layer("fox_f", narrow(a["fox_w_in_2"][0], 4 * D, FOX_HEADS), [KC], dmas=(1, 0))
        layer("fox_vg", cols(a["fox_w_in_2"][0], 2 * D), [KC] * 4)
        layer("fox_out", cols(a["fox_w_out_2"][0], 0), [KC] * 2)
        layer("up2", gate_up(up2[1][:, 0:FF], up2[1][:, FF:2 * FF]), [KC] * 11)
        layer("down2", k_split(down2[1], down_kc, 3), down_kc * 2, k_split=3)
        special = {"lora_in": ("lora1_done", 3), "lora_out": ("lora2_done", 12), "ssd_dt": ("narrow_done", 1), "fox_f": ("narrow_done", 2)}
        landed = [[0, 0], [0, 0]]
        unit, item, evac = 0, 0, 0
        occupant = [[None, None], [None, None]]
        for ly in order:
            ly.u0, ly.item0, ly.evac0 = unit, item, evac
            ly.landed, ly.free = ([], []), ([], [])
            for u in range(len(ly)):
                s = unit % 2
                for half in range(2):
                    landed[s][half] += 16 * ly.dmas[half]
                    ly.landed[half].append(landed[s][half])
                    ly.free[half].append(occupant[s][half])
                    if ly.name in special:
                        occupant[s][half] = special[ly.name]
                    else:
                        occupant[s][half] = ("w_lo_ready", item + M_PER_UNIT // 2 * (half + 1))
                unit += 1
                if ly.name not in special:
                    item += M_PER_UNIT
                    if u % ly.k_split == ly.k_split - 1:
                        evac += M_PER_UNIT
            ly.item1, ly.evac1 = item, evac

        def units(eng, ly, body, lead=0):
            n = len(ly)
            pairs = (n - lead - 2) // 2 if n >= 6 and ly.k_split == 1 else 0
            for u in range(lead if pairs else 0):
                body(u, u % 2, False)
            if pairs:
                with eng.Fori(lead // 2, lead // 2 + pairs) as i:
                    for p in range(2):
                        body(2 * i + p, p, False)
            for u in range(lead + 2 * pairs if pairs else 0, n):
                body(u, u % 2, u == n - 1)

        def nth(ly, u, p, table):
            return table[u] if isinstance(u, int) else table[p] + (u - p) * ((table[p + 2] - table[p]) // 2)

        BANKS = M_PER_UNIT
        INV_GROUP = 512 // P

        def z_bank(j):
            return pb[7 - j % 2][:, T:2 * T]

        KEYS_MADE, BONUS_MADE, PAIRS_MADE, INVERSES_MADE = 1, 2, 3, 4
        R_DECAYED, GLU_MADE, STATE_ZEROED, GN_SQUARED, GN_ROOTED = 1, 2, 3, 4, 5

        def pe_layer(pe, ly, hi, lo, in_ready, in_base, hook=None, after_two=None):
            def body(u, p, last):
                part = u % ly.k_split if isinstance(u, int) else 0
                k0, nk = (ly.first_k(u), ly.nkc[u]) if isinstance(u, int) else (0, KC)
                first, final = part == 0, part == ly.k_split - 1
                group = u // ly.k_split if isinstance(u, int) else u
                for m in range(M_PER_UNIT):
                    pe.wait_ge(sem("w_lo_ready"), ly.item0 + M_PER_UNIT * u + m + 1)
                    if first:
                        pe.wait_ge(sem("evac_done"), ly.evac0 + M_PER_UNIT * group + m + 1)
                    for k in range(nk):
                        if isinstance(u, int) and u < ly.k_split and m == 0:
                            pe.wait_ge(sem(in_ready), in_base + k0 + k + 1)
                        o = pb[m][:, 0:T]
                        pe.matmul(o, w_hi[m][:, k, :], hi[:, k0 + k, :], start=first and k == 0, stop=False)
                        pe.matmul(o, w_hi[m][:, k, :], lo[:, k0 + k, :], start=False, stop=False)
                        mm = pe.matmul(o, w_lo[m][:, k, :], hi[:, k0 + k, :], start=False, stop=final and k == nk - 1)
                    mm.then_inc(sem("block_done"), 1)
                    if after_two and isinstance(u, int) and (u, m) == (0, 1):
                        after_two()
                    if hook:
                        hook(u, m)
            units(pe, ly, body, lead=2)

        def act_head(act, ly, u, p, m):
            s = (ly.u0 + p) % 2
            nk = ly.nkc[u] if isinstance(u, int) else KC
            if m % (M_PER_UNIT // 2) == 0:
                half = m // (M_PER_UNIT // 2)
                act.wait_ge(sem(f"landed{s}{half}"), nth(ly, u, p, ly.landed[half]))
            act.wait_ge(sem("block_done"), ly.item0 + M_PER_UNIT * u + m + 1)
            act.activation(w_hi[m][:, 0:nk, :], raw[s][:, 0:nk, m * P:(m + 1) * P], ACT.Copy).then_inc(sem("w_hi_ready"), 1)

        def dve_rest(dve, ly, u, p, m):
            s = (ly.u0 + p) % 2
            nk = ly.nkc[u] if isinstance(u, int) else KC
            dve.wait_ge(sem("w_hi_ready"), ly.item0 + M_PER_UNIT * u + m + 1)
            dve.tensor_tensor(w_lo[m][:, 0:nk, :], raw[s][:, 0:nk, m * P:(m + 1) * P], w_hi[m][:, 0:nk, :].bitcast(F32),
                              ALU.subtract).then_inc(sem("w_lo_ready"), 1)

        def ahead(split, eng, ly):
            for m in range(LOOKAHEAD):
                split(eng, ly, 0, 0, m)

        def split_next(split, eng, ly, nxt, u, p, m, last):
            if m + LOOKAHEAD < M_PER_UNIT:
                split(eng, ly, u, p, m + LOOKAHEAD)
            elif not last:
                split(eng, ly, u + 1, (p + 1) % 2, m + LOOKAHEAD - M_PER_UNIT)
            elif nxt:
                split(eng, nxt, 0, 0, m + LOOKAHEAD - M_PER_UNIT)

        def act_layer(act, ly, hook=None, lead=0, nxt=None, begin=None):
            def body(u, p, last):
                for m in range(M_PER_UNIT):
                    split_next(act_head, act, ly, nxt, u, p, m, last)
                    if begin and isinstance(u, int) and u + m == 0:
                        begin()
                    if hook:
                        hook(u, m)
            units(act, ly, body, 2 if begin else lead)

        def dve_layer(dve, ly, out_block, hook=None, rest_last=False, nxt=None, begin=None):
            def body(u, p, last):
                for m in range(M_PER_UNIT):
                    at_first = begin and isinstance(u, int) and u + m == 0
                    if not rest_last or at_first:
                        split_next(dve_rest, dve, ly, nxt, u, p, m, last)
                    if at_first:
                        begin()
                    if not isinstance(u, int) or u % ly.k_split == ly.k_split - 1:
                        dve.wait_ge(sem("block_done"), ly.item0 + M_PER_UNIT * u + m + 1 + BANKS)
                        out_block(u // ly.k_split if isinstance(u, int) else u, m)
                    if rest_last and not at_first:
                        split_next(dve_rest, dve, ly, nxt, u, p, m, last)
                    if hook:
                        hook(u, m)
            units(dve, ly, body, 2 if begin else 0)

        def par_col(name, i):
            c = col[name]
            return par[:, c + i:c + i + 1] if isinstance(i, int) else par[:, bass.ds(c + i, 1)]

        def tile(base, i):
            return pj[:, base + i, :]

        class Chain:

            def __init__(self, eng, name):
                self.eng, self.sem, self.n = eng, sem(name), 0

            def go(self, ins):
                ins.then_inc(self.sem, 1)
                self.n += 1

            def sync(self):
                self.eng.wait_ge(self.sem, self.n)

            def link(self, ins):
                self.go(ins)
                self.sync()

        X_BASE = {0: 0, 1: 4 * KC, 2: 5 * KC, 3: 6 * KC, 4: 7 * KC, "fox": 8 * KC, 5: 9 * KC}
        RSTD_NORM, RSTD_BRANCH = (1, 3, 5, 6, 7, 8, 9), (2, 4)

        def param_pieces(tiles):
            for name, rows, src in par_rows:
                r0 = 0
                while r0 < rows:
                    t, p0 = divmod(col[name] + r0, P)
                    m = min(rows - r0, P - p0)
                    if t in tiles:
                        yield t, p0, m, src[r0:r0 + m, :]
                    r0 += m

        def load_params(eng, tiles, signal, share=slice(None)):
            for t, p0, m, src in list(param_pieces(tiles))[share]:
                eng.dma_start(par_tok[p0:p0 + m, t, :], src).then_inc(sem(signal), 16)

        def n_pieces(tiles):
            return len(list(param_pieces(tiles)))
        NORMS = [("pre_mix_norm", 0), ("pre_ffn_norm", 0), ("mix_norm_g_2", 0), ("ffn_norm_g_2", 0),
                 ("mix_norm_g_2", KC), ("ffn_norm_g_2", KC)]
        block = ctx.enter_context(nc.Block())


        @block.sync
        def _(sp):
            sp.dma_start(x_tok, a["x"][0].rearrange("(c p) d -> p c d", p=P)).then_inc(sem("x_loaded"), 16)
            load_params(sp, range(1), "par_first", slice(0, None, 2))
            for ly in order:
                s0 = ly.u0 % 2
                if ly.name == "lora_out":
                    for half in range(2):
                        sp.wait_ge(sem(ly.free[half][0][0]), ly.free[half][0][1])
                    flat = raw[s0][:, :, :].rearrange("p k n -> p (k n)")
                    for i, (n, rows) in enumerate((("decay_w2", 64), ("a_2", 64), ("g_2", 128))):
                        sp.dma_start(flat[0:rows, D * i:D * i + D], a[n][0]).then_inc(sem(f"landed{s0}0"), 16)
                    continue

                def body(u, p, last):
                    s = (ly.u0 + p) % 2
                    nk = ly.nkc[u] if isinstance(u, int) else KC
                    for half in range(2):
                        parts = [x for x in ly.sources(u) if x[0].start // HALF == half]
                        if not parts:
                            continue
                        if not isinstance(u, int):
                            sp.wait_ge(sem("w_lo_ready"), ly.item0 + M_PER_UNIT * (u - 2) + M_PER_UNIT // 2 * (half + 1))
                        elif ly.free[half][u]:
                            sp.wait_ge(sem(ly.free[half][u][0]), ly.free[half][u][1])
                        for c, src in parts:
                            sp.dma_start(raw[s][:, 0:nk, c], src).then_inc(sem(f"landed{s}{half}"), 16)
                if ly is order[0]:
                    for u in range(len(ly)):
                        if u == 2:
                            load_params(sp, range(1, par_tiles), "par_loaded")
                            for i, name in enumerate(("ssd_dt_bias_2", "ssd_a_log_2")):
                                sp.dma_start(heads_col[:, i:i + 1], a[name][0].rearrange("(h a) -> h a", a=1)).then_inc(sem("small_loaded"), 16)
                            sp.dma_start(heads_col[0:FOX_HEADS, 2:3], a["fox_b_f_2"][0].rearrange("(h a) -> h a", a=1)).then_inc(sem("small_loaded"), 16)
                            for h in range(2):
                                for i, name in enumerate(("fox_q_norm_g_2", "fox_k_norm_g_2")):
                                    sp.dma_start(fox_g[64 * h:64 * h + 64, i:i + 1], a[name][0].rearrange("(d a) -> d a", a=1)).then_inc(sem("small_loaded"), 16)
                                sp.dma_start(d_skip[64 * h:64 * h + 64, :],
                                              a["ssd_d_2"][0].rearrange("(m t a) -> t a m", t=2, a=1)[h].broadcast_to([64, SSD_Z]), allow_slow_non_contiguous=True).then_inc(sem("small_loaded"), 16)
                        body(u, u % 2, False)
                else:
                    units(sp, ly, body)
            for c in range(2):
                sp.wait_ge(sem("y_tok_ready"), 2 * (c + 1))
                sp.dma_start(out[0, c * P:(c + 1) * P, :], y_tok[:, c, :]).then_inc(sem("out_done"), 16)
            sp.wait_ge(sem("out_done"), 32)

        @block.gpsimd
        def _(pool):
            ch = Chain(pool, "pool_chain")
            go, sync, link = ch.go, ch.sync, ch.link

            go(pool.memset(ident[:, :], 0.0))
            go(pool.memset(tri[:, :], 1.0))
            go(pool.memset(blk[:, :], 0.0))
            go(pool.memset(scan_mask[:, :], 1.0))
            go(pool.memset(head_sel[:, :, :], 0.0))
            go(pool.memset(ones[:, :], 1.0))
            for i, e in enumerate((RMS_EPS, LN_EPS, GN_EPS)):
                go(pool.memset(eps[:, i:i + 1], e))
            sync()
            link(pool.affine_select(out=ident[:, :], in_=ident[:, :], compare_op=ALU.not_equal, fill=1.0, base=0,
                                  pattern=[[-1, P]], channel_multiplier=1))
            link(pool.affine_select(out=tri[:, :], in_=tri[:, :], compare_op=ALU.is_ge, fill=0.0, base=0,
                                  pattern=[[1, P]], channel_multiplier=-1))
            link(pool.tensor_tensor(later[:, :], ones[:, :], tri[:, :], ALU.subtract))
            for h in range(2):
                link(pool.memset(blk[64 * h:64 * h + 64, 64 * h:64 * h + 64], 1.0))
                link(pool.affine_select(out=head_sel[64 * h:64 * h + 64, :, :], in_=head_sel[64 * h:64 * h + 64, :, :],
                                      compare_op=ALU.not_equal, fill=1.0, base=-h,
                                      pattern=[[-2, KC], [1, RWKV_HEADS]], channel_multiplier=0))
            link(pool.memset(scan_mask[:, :].rearrange("p (c s) -> p c s", s=CHUNK)[:, :, 0:1], 0.0))
            sync()
            for b in range(4):
                rows = slice(32 * b, 32 * b + 32)
                link(pool.tensor_copy(g_mask[rows, 0:CHUNK], tri[rows, rows]))
                link(pool.tensor_tensor(g_mask[rows, CHUNK:2 * CHUNK], tri[rows, rows], ident[rows, rows], ALU.subtract))
            sync()
            pool.nop().then_inc(sem("const_ready"), 1)

            def par_tiles_of(name, i):
                c = col[name] + KC * i
                return par[:, c:c + KC].unsqueeze(2).broadcast_to([P, KC, T])

            def shift_less(o, s):
                go(pool.tensor_tensor(o[:, :, 1:T], s[:, :, 0:T - 1], s[:, :, 1:T], ALU.subtract))
                go(pool.tensor_scalar(o[:, :, 0:1], s[:, :, 0:1], -1.0, None, ALU.mult))
                sync()

            def add_squares(n):
                def add(i, j):
                    link(pool.tensor_tensor(sub[:, i:i + 2, :], sub[:, i:i + 2, :], sub[:, j:j + 2, :], ALU.add))
                for i in (0, 4):
                    pool.wait_ge(sem("sq_ready"), KC * n + i + 4)
                    add(i, i + 2)
                add(0, 4)
                pool.tensor_tensor(sub[:, 0, :], sub[:, 0, :], sub[:, 1, :], ALU.add).then_inc(sem("sq_added"), 1)

            add_squares(0)
            h, xx = slot(TMP), slot(W)
            pool.wait_ge(sem("x_ready"), KC)
            link(pool.tensor_tensor(h, x_res[:, :, :], par_tiles_of("pre_mix_norm", 0), ALU.mult))
            pool.wait_ge(sem("rstd_ready"), RSTD_NORM[0])
            link(pool.tensor_tensor(h, h, rstd[:, :].unsqueeze(1).broadcast_to([P, KC, T]), ALU.mult))
            shift_less(xx, h)
            for i, dst in enumerate((KK, A, G)):
                link(pool.tensor_tensor(slot(dst), xx, par_tiles_of("mu_wag", i), ALU.mult))
                pool.tensor_tensor(slot(dst), slot(dst), h, ALU.add).then_inc(sem("lora_x"), 1)
            pool.wait_ge(sem("decay_ready"), 2)
            link(pool.tensor_tensor(slot(R), slot(R), slot(W), ALU.mult))
            pool.nop().then_inc(sem("pool_stages"), 1)
            pool.wait_ge(sem("evac_done"), L["v"].evac1 + BANKS)
            v = slot(V)
            shift_less(tmp2, v)
            link(pool.tensor_tensor(tmp2, tmp2, par_tiles_of("mu_rkv", 2), ALU.mult))
            link(pool.tensor_tensor(v, v, tmp2, ALU.add))

            pool.wait_ge(sem("lab_ready"), NCHUNK)
            pool.wait_ge(sem("bonus_ready"), 1)
            pool.dma_start(sub_in, lab_t).then_inc(sem("sub_dma"), 16)
            pool.wait_ge(sem("sub_dma"), 16)
            pool.dma_start(lt, sub_in.rearrange("s y t -> y s t")).then_inc(sem("sub_dma"), 16)
            pool.wait_ge(sem("gate_ready"), 1)
            link(pool.tensor_tensor(slot(U), slot(U), slot(GATE), ALU.mult))
            pool.nop().then_inc(sem("pool_stages"), 1)

            def conv_tap(s):
                o = slot(GATE)[:, 0:POOL_TILES, s:T]
                pool.wait_ge(sem("tap_ready"), s + 1)
                if s >= 2:
                    pool.wait_ge(sem("tap_summed"), s - 1)
                if s:
                    pool.tensor_tensor(o, o, tap_prod[s % 2][:, 0:POOL_TILES, 0:T - s], ALU.add).then_inc(sem("tap_summed"), 1)

            for t in range(EARLY_TAPS):
                conv_tap(t)
            pool.wait_ge(sem("dve_stages"), INVERSES_MADE)
            link(pool.memset(state, 0.0))
            pool.nop().then_inc(sem("pool_stages"), 1)
            for t in range(EARLY_TAPS, CONV_TAPS):
                conv_tap(t)
            pool.wait_ge(sem("gn_centred"), 4)
            pool.tensor_tensor(tmp2, slot(R), slot(R), ALU.mult).then_inc(sem("pool_stages"), 1)
            pool.wait_ge(sem("gn_root"), 4 + 1)
            pool.tensor_tensor(slot(R), slot(R), slot(TMP), ALU.mult).then_inc(sem("pool_stages"), 1)

            def silu_tiles(ly, n):
                src = g_tile if n == 0 else c_tile

                def body(u, p, last):
                    for m in range(2):
                        pool.wait_ge(sem("glu_sig"), FC * n + 2 * u + m + 1)
                        pool.tensor_tensor(s_tile[m], s_tile[m], src[m], ALU.mult).then_inc(sem("silu_step"), 1)
                    for m in range(2):
                        pool.wait_ge(sem("silu_step"), FC * n + 2 * u + m + 1)
                        pool.tensor_tensor(s_tile[m], s_tile[m], rstd[:, :], ALU.mult).then_inc(sem("glu_silu"), 1)
                units(pool, ly, body)
            add_squares(1)
            silu_tiles(L["up0"], 0)
            add_squares(2)
            for u in range(len(L["ssd_z"])):
                q = slice(M_PER_UNIT * u, M_PER_UNIT * (u + 1))
                pool.wait_ge(sem("z_sig"), u + 1)
                pool.tensor_tensor(z_t[:, q, :], z_t[:, q, :], z_sig[:, q, :], ALU.mult).then_inc(sem("z_silu"), 1)
            ly = L["ssd_xbc"]
            for m in range(M_PER_UNIT):
                pool.nop().then_inc(sem("xbc_ready"), 1)

            def xbc_silu(u, p, last):
                for m in range(M_PER_UNIT):
                    j = 4 * u + m
                    t = xbc[:, j, :] if isinstance(u, int) else pj[:, bass.ds(SSD_Z + j, 1), :].rearrange("p a b -> p (a b)")
                    pool.wait_ge(sem("xbc_sig"), j + 1)
                    pool.tensor_tensor(t, t, conv_sig[m], ALU.mult).then_inc(sem("xbc_ready"), 1)
            units(pool, ly, xbc_silu)
            pool.wait_ge(sem("xdt_ready"), 4)
            pool.tensor_tensor(xdt_end.rearrange("p (h d) -> p h d", d=HEAD),
                               xdt[:, 0, :].rearrange("p (h d) -> p h d", d=HEAD),
                               tok_heads[:, 4, :].unsqueeze(2).broadcast_to([P, SSD_HEADS, HEAD]), ALU.mult).then_inc(sem("xdt_end_ready"), 1)
            pool.wait_ge(sem("st_done"), SSD_GROUPS)
            for i in range(16):
                c, hq = divmod(i, 8)
                if i >= 2:
                    pool.wait_ge(sem("bc_done"), i - 1)
                pool.tensor_tensor(seg[i % 2].rearrange("p (h l) -> p h l", l=P), tri[:, :].unsqueeze(1).broadcast_to([P, 4, P]),
                                   tok_heads[:, c, 4 * hq:4 * hq + 4].unsqueeze(2).broadcast_to([P, 4, P]), ALU.mult).then_inc(sem("seg_ready"), 1)
            add_squares(3)
            silu_tiles(L["up1"], 1)
            add_squares(4)
            pool.wait_ge(sem("fox_arena_free"), 1)
            link(pool.memset(fox_mask, 0.0))
            link(pool.affine_select(out=fox_mask[:, P:T], in_=fox_mask[:, P:T], compare_op=ALU.is_ge, fill=MASKED,
                                    base=0, pattern=[[-1, P]], channel_multiplier=1))
            pool.nop().then_inc(sem("fox_mask_ready"), 1)
            add_squares(5)
            silu_tiles(L["up2"], 2)

        @block.scalar
        def _(act):
            ch = Chain(act, "act_chain")
            go, sync, link = ch.go, ch.sync, ch.link
            load_params(act, range(1), "par_first", slice(1, None, 2))

            def norm_in(n, between=None):
                name, o = NORMS[n]
                for k in range(KC):
                    act.wait_ge(sem("x_ready"), KC * n + k + 1)
                    act.activation(x_hi[:, k, :], x_res[:, k, :], ACT.Copy, scale=par_col(name, o + k)).then_inc(sem("x_hi_ready"), 1)
                if between:
                    between()
                for k in range(KC):
                    act.activation(sub[:, k, :], x_res[:, k, :], ACT.Square).then_inc(sem("sq_ready"), 1)

            def inverse_root(bank):
                link(act.activation(rs[:, :], pb[bank][:, 0:T], ACT.Ln, bias=eps[:, 0:1], scale=1.0 / D))
                act.activation(rstd[:, :], rs[:, :], ACT.Exp, scale=-0.5).then_inc(sem("rstd_ready"), 1)

            def norm_root(n, bank=7):
                act.wait_ge(sem("ssq_done"), n + 1)
                inverse_root(bank)

            act.wait_ge(sem("const_ready"), 1)
            norm_in(0, lambda: ahead(act_head, act, L["rk"]))
            act_layer(act, L["rk"], begin=lambda: norm_root(0))
            act.wait_ge(sem("lora1_done"), 1)
            act.activation(lora_w, pb[4][0:64, 0:T], ACT.Tanh).then_inc(sem("lora_mid"), 1)
            act.wait_ge(sem("lora1_done"), 2)
            act.activation(lora_a, pb[5][0:64, 0:T], ACT.Copy).then_inc(sem("lora_mid"), 1)
            act.wait_ge(sem("lora1_done"), 3)
            act.activation(lora_g, pb[6][:, 0:T], ACT.Sigmoid).then_inc(sem("lora_mid"), 1)
            for f, (dst, bias) in enumerate(((W, "decay_w0"), (A, "a_0"), (G, None))):
                for j in range(4):
                    i = 4 * f + j
                    act.wait_ge(sem("lora2_done"), i + 1)
                    bank = pb[4 + i % 3]
                    if bias:
                        go(act.activation(slot(dst)[:, 2 * j, :], bank[:, 0:T], ACT.Sigmoid, bias=par_col(bias, 2 * j)))
                        act.activation(slot(dst)[:, 2 * j + 1, :], bank[:, T:2 * T], ACT.Sigmoid,
                                       bias=par_col(bias, 2 * j + 1)).then_inc(sem("lora_ready"), 1)
                    else:
                        act.activation(slot(dst)[:, 2 * j:2 * j + 2, :], bank[:, :], ACT.Copy).then_inc(sem("lora_ready"), 1)
            act.wait_ge(sem("dve_stages"), KEYS_MADE)
            act.activation(slot(TMP), slot(KK), ACT.Square).then_inc(sem("kk_sq"), 1)

            def prep(u, m):
                i = M_PER_UNIT * u + m
                if i == 0:
                    act.wait_ge(sem("kk_max"), 4)
                    link(act.activation(slot(TMP), slot(TMP), ACT.Ln))
                    act.activation(slot(TMP), slot(TMP), ACT.Exp, scale=-0.5).then_inc(sem("kk_root"), 1)
                if i == 3:
                    act.wait_ge(sem("bonus_done"), 1)
                    act.activation(bonus, pb[3 + 1][0:RWKV_HEADS, 0:T], ACT.Copy).then_inc(sem("bonus_ready"), 1)

            def decays(u, m):
                if (u, m) == (0, 0):
                    act.wait_ge(sem("cum_ready"), KC)
                    act.activation(slot(W), slot(TMP), ACT.Exp, scale=-EXP_MINUS_HALF).then_inc(sem("decay_ready"), 1)
                    act.wait_ge(sem("decay_ready"), 1)
                    act.activation(slot(TMP), slot(TMP), ACT.Exp, scale=EXP_MINUS_HALF).then_inc(sem("decay_ready"), 1)
            ahead(act_head, act, L["v"])
            act_layer(act, L["v"], prep, nxt=L["ug"])
            act_layer(act, L["ug"], decays)
            def z_head(j):
                act_head(act, L["z"], j // M_PER_UNIT, j // M_PER_UNIT % 2, j % M_PER_UNIT)

            for j in range(BANKS):
                z_head(j)
            act.wait_ge(sem("evac_done"), L["ug"].evac1 + BANKS)
            act.activation(slot(GATE), slot(GATE), ACT.Sigmoid).then_inc(sem("gate_ready"), 1)

            def v_rows(c):
                act.wait_ge(sem("v_turned"), c + 1)
                if c >= 2:
                    act.wait_ge(sem("y2_done"), c - 1)
                go(act.activation(uv[c % 2][0:CHUNK, 0:512], pb[2][0:CHUNK, :], ACT.Copy))
                act.activation(uv[c % 2][0:CHUNK, 512:1024], pb[3][0:CHUNK, :], ACT.Copy).then_inc(sem("v_rows"), 1)

            def bk_rows(c):
                act.wait_ge(sem("bk_turned"), c + 1)
                if c >= 2:
                    act.wait_ge(sem("y2_done"), c - 1)
                go(act.activation(bk_t[c % 2][:, 0:512], pb[0][0:64, :], ACT.Copy))
                act.activation(bk_t[c % 2][:, 512:1024], pb[1][0:64, :], ACT.Copy).then_inc(sem("bk_rows"), 1)

            def tap_products(first, last):
                for s in range(first, min(last, CONV_TAPS)):
                    if s >= 3:
                        act.wait_ge(sem("tap_summed"), s - 2)
                    for k in range(POOL_TILES):
                        w = par_col("conv_dw", KC * (CONV_TAPS - 1 - s) + k)
                        if s == 0:
                            ins = act.activation(slot(GATE)[:, k, :], slot(U)[:, k, :], ACT.Identity, scale=w, bias=par_col("conv_b", k))
                        else:
                            ins = act.activation(tap_prod[s % 2][:, k, 0:T - s], slot(U)[:, k, 0:T - s], ACT.Copy, scale=w)
                        if k == POOL_TILES - 1:
                            ins.then_inc(sem("tap_ready"), 1)
                        else:
                            go(ins)

            act.wait_ge(sem("pool_stages"), GLU_MADE)
            act.wait_ge(sem("dve_stages"), PAIRS_MADE)
            for j in range(BANKS, BANKS + Z_EARLY):
                tap_products(3 * (j - BANKS), 3 * (j - BANKS + 1))
                z_head(j)
            tap_products(3 * Z_EARLY, EARLY_TAPS)
            for i in range(CHUNK // INV_GROUP):
                act.wait_ge(sem("inverse_turned"), i + 1)
                act.activation(lab_t[:, :, INV_GROUP * i:INV_GROUP * (i + 1)],
                               pb[4 + i % 4][0:CHUNK, :].rearrange("s (t y) -> s y t", y=P), ACT.Copy).then_inc(sem("inverse_rows"), 1)
            v_rows(0)
            bk_rows(0)
            for c in range(NCHUNK):
                act.wait_ge(sem("x_done"), c + 1)
                act.activation(x_buf[:, 512:1024], pb[5][0:CHUNK, :], ACT.Copy).then_inc(sem("x_rows_a"), 1)
                if c + 1 < NCHUNK:
                    v_rows(c + 1)
                else:
                    act.wait_ge(sem("ln_centred"), 1)
                    act.activation(slot(U), slot(GATE), ACT.Square).then_inc(sem("ln_sq"), 1)
                act.wait_ge(sem("u_done"), c + 1)
                act.activation(uv[c % 2][CHUNK:2 * CHUNK, 512:1024], pb[5][0:CHUNK, :], ACT.Copy).then_inc(sem("u_rows_a"), 1)
                if c + 1 < NCHUNK:
                    bk_rows(c + 1)
                for j in range(BANKS + Z_EARLY + Z_CHUNK * c, min(BANKS + Z_EARLY + Z_CHUNK * (c + 1), len(L["z"]) * M_PER_UNIT)):
                    z_head(j)
                tap_products(EARLY_TAPS + CHUNK_TAPS * c, EARLY_TAPS + CHUNK_TAPS * (c + 1))
                if c == NCHUNK - 2:
                    act.wait_ge(sem("evac_done"), L["z"].evac1 + BANKS)
                    act.activation(slot(ZC), slot(ZC), ACT.Sigmoid).then_inc(sem("z_ready"), 1)
                    act.activation(slot(ZR), slot(ZR), ACT.Sigmoid).then_inc(sem("z_ready"), 1)
                    ahead(act_head, act, L["conv_out"])
            act.wait_ge(sem("ln_var"), 1)
            link(act.activation(rs[:, :], pb[6][:, 0:T], ACT.Ln, bias=eps[:, 1:2], scale=1.0 / D))
            act.activation(rs[:, :], rs[:, :], ACT.Exp, scale=-0.5).then_inc(sem("ln_root"), 1)
            for k in range(KC):
                act.wait_ge(sem("ln_ready"), k + 1)
                w, s = par_col("conv_ln_w", k), par_col("conv_ln_b", k)
                go(act.activation(slot(U)[:, k, :], slot(GATE)[:, k, :], ACT.Sigmoid, scale=w, bias=s))
                act.activation(slot(TMP)[:, k, :], slot(GATE)[:, k, :], ACT.Identity, scale=w, bias=s).then_inc(sem("ln_sig"), 1)
            sync()
            for k in range(KC):
                act.wait_ge(sem("mix_in"), k + 1)
                act.activation(x_hi[:, k, :], slot(GATE)[:, k, :], ACT.Copy).then_inc(sem("x_hi_ready"), 1)
            act.wait_ge(sem("gn_var"), 1)
            for b in range(4):
                act.activation(slot(TMP)[:, 2 * b:2 * b + 2, :], pb[b][:, :], ACT.Ln, bias=eps[:, 2:3], scale=1.0 / HEAD).then_inc(sem("gn_root"), 1)
            act.wait_ge(sem("gn_root"), 4)
            act.activation(slot(TMP), slot(TMP), ACT.Exp, scale=-0.5).then_inc(sem("gn_root"), 1)

            def y_heads(u, m):
                if (u, m) == (0, 1):
                    act.wait_ge(sem("pool_stages"), GN_ROOTED)
                    for k in range(KC):
                        act.activation(slot(R)[:, k, :], slot(R)[:, k, :], ACT.Identity, scale=par_col("gn_w", k),
                                       bias=par_col("gn_b", k)).then_inc(sem("gn_root"), 1)
                if (u, m) == (0, 3):
                    act.wait_ge(sem("mix_in"), KC + 1)
                    for k in range(KC):
                        act.activation(y_hi[:, k, :], slot(R)[:, k, :], ACT.Copy).then_inc(sem("x_hi_ready"), 1)
            act_layer(act, L["conv_out"], y_heads, nxt=L["rwkv_out"])

            def mixed_head(j):
                act.wait_ge(sem("mix_in"), KC + 1 + j + 1)
                act.activation(x_hi[:, j, :], slot(ZC)[:, j, :], ACT.Copy).then_inc(sem("x_hi_ready"), 1)

            def mixed_heads(u, m):
                if M_PER_UNIT * u + m:
                    mixed_head(M_PER_UNIT * u + m - 1)
            act_layer(act, L["rwkv_out"], mixed_heads, nxt=L["w_out"])
            mixed_head(KC - 1)

            def branch_squares(i, first, tiles):
                for k in tiles:
                    act.wait_ge(sem("evac_done"), first + k + 1 + BANKS)
                    act.activation(sub[:, k, :], tile(64 if i else 0, k), ACT.Square).then_inc(sem("osq_ready"), 1)

            def post_norm(i, first, bank):
                branch_squares(i, first, range(KC - 2, KC))
                act.wait_ge(sem("osum_done"), i + 1)
                inverse_root(bank)

            def w_out_hook(u, m):
                j = M_PER_UNIT * u + m
                if j >= 2:
                    branch_squares(0, L["w_out"].evac0, [j - 2])

            act_layer(act, L["w_out"], w_out_hook, nxt=L["up0"])
            post_norm(0, L["w_out"].evac0, 7)
            norm_in(1)

            def ffn(n, up, down, nxt=None, down_hook=None):
                src = g_tile if n == 0 else c_tile

                def sig(u, m):
                    if n == 0:
                        act.wait_ge(sem("evac_done"), up.evac0 + M_PER_UNIT * u + m + 1 + BANKS)
                    else:
                        act.wait_ge(sem("glu_gate"), FC * (n - 1) + 2 * u + m + 1)
                    act.activation(s_tile[m], src[m], ACT.Sigmoid).then_inc(sem("glu_sig"), 1)

                def head(u, m):
                    act.wait_ge(sem("evac_done"), up.evac0 + M_PER_UNIT * u + m + 3 + BANKS)
                    j = 2 * u + m
                    o = act_hi[:, j, :] if isinstance(u, int) else act_hi[:, bass.ds(j, 1), :].rearrange("p a b -> p (a b)")
                    act.activation(o, a_tile[m], ACT.Copy).then_inc(sem("act_hi_ready"), 1)

                def hook(u, m):
                    if m == 1:
                        sig(u, 0)
                        sig(u, 1)
                    if m == 3:
                        head(u, 0)
                        head(u, 1)
                act_layer(act, up, hook, nxt=down, begin=lambda: norm_root((1, 3, 5)[n]))
                act_layer(act, down, down_hook, nxt=nxt)

            def down0_hook(u, m):
                first = L["down0"].evac0
                if u == L["down0"].k_split:
                    branch_squares(1, first, [m])
                if u == len(L["down0"]) - 1 and m >= 2:
                    branch_squares(1, first, [M_PER_UNIT + m - 2])

            ffn(0, L["up0"], L["down0"], L["ssd_z"], down0_hook)
            post_norm(1, L["down0"].evac0, 7)
            norm_in(2)
            def z_sigmoids(u):
                act.wait_ge(sem("evac_done"), L["ssd_z"].evac0 + M_PER_UNIT * (u + 1) + BANKS)
                q = slice(M_PER_UNIT * u, M_PER_UNIT * (u + 1))
                act.activation(z_sig[:, q, :], z_t[:, q, :], ACT.Sigmoid).then_inc(sem("z_sig"), 1)

            def z_hook(u, m):
                if m == 1 and u:
                    z_sigmoids(u - 1)
            act_layer(act, L["ssd_z"], z_hook, begin=lambda: norm_root(2), nxt=L["ssd_xbc"])
            z_sigmoids(len(L["ssd_z"]) - 1)

            def xbc_hook(u, m):
                def tile_of(j):
                    return xbc[:, j, :] if isinstance(j, int) else pj[:, bass.ds(SSD_Z + j, 1), :].rearrange("p a b -> p (a b)")
                j = M_PER_UNIT * u + m
                act.wait_ge(sem("evac_done"), L["ssd_xbc"].evac0 + j + 1 + BANKS)
                act.activation(tile_of(j), conv_in[m], ACT.Identity, scale=par_col("ssd_conv_w_2", (SSD_TAPS - 1) * SSD_XBC + j),
                               bias=par_col("ssd_conv_b_2", j)).then_inc(sem("xbc_begun"), 1)
                if m == 1 and (not isinstance(u, int) or u):
                    xbc_sigmoids(u - 1)

            def xbc_sigmoids(u):
                for i in range(M_PER_UNIT):
                    j = M_PER_UNIT * u + i
                    act.wait_ge(sem("xbc_conv"), M_PER_UNIT + j + 1)
                    act.wait_ge(sem("xbc_ready"), j + 1)
                    t = xbc[:, j, :] if isinstance(u, int) else pj[:, bass.ds(M_PER_UNIT * (u + SSD_Z // M_PER_UNIT) + i, 1), :].rearrange("p a b -> p (a b)")
                    act.activation(conv_sig[i], t, ACT.Sigmoid).then_inc(sem("xbc_sig"), 1)
            act_layer(act, L["ssd_xbc"], xbc_hook, lead=2)
            xbc_sigmoids(len(L["ssd_xbc"]) - 1)
            act.wait_ge(sem("abs_ready"), 1)
            link(act.activation(dt_e, dt_e, ACT.Exp, scale=-1.0))
            act.wait_ge(sem("small_loaded"), 16 * 9)
            go(act.activation(heads_col[:, 3:4], heads_col[:, 1:2], ACT.Exp))
            act.activation(dt_e, dt_e, ACT.Ln, bias=1.0).then_inc(sem("log_ready"), 1)
            act.wait_ge(sem("acs_ready"), 2)
            go(act.activation(da_end, acs[:, 0:P], ACT.Exp, scale=-1.0, bias=acs[:, P - 1:P]))
            act.activation(da_exp, acs[:, P:T], ACT.Exp).then_inc(sem("da_ready"), 1)
            act.wait_ge(sem("xbc_ready"), M_PER_UNIT + SSD_XBC)
            for b in range(4):
                act.wait_ge(sem("eab_done"), b + 1)
                act.activation(eab[:, 4 * b:4 * b + 4, :].rearrange("p m l -> p (m l)"), pb[4 + b % 2][:, :], ACT.Copy).then_inc(sem("eab_ready"), 1)
            ahead(act_head, act, L["ssd_out"])
            act.wait_ge(sem("evac_done"), L["ssd_z"].evac1 + BANKS)

            def square(q):
                act.wait_ge(sem("yz_ready"), q + 1)
                if q >= 4:
                    act.wait_ge(sem("yz_sum"), q // 2 - 1)
                act.activation(sub[:, 2 * (q % 4):2 * (q % 4) + 2, :], y_ssd[:, 2 * q:2 * q + 2, :], ACT.Square).then_inc(sem("yz_sq"), 1)

            def roots(groups):
                for g in groups:
                    act.wait_ge(sem("yz_sum"), g + 1)
                    go(act.activation(sub[:, 8 + g, :], pb[4 + g][:, 0:T], ACT.Ln, bias=eps[:, 0:1], scale=1.0 / (4 * P)))
                sync()
                for g in groups:
                    act.activation(sub[:, 8 + g, :], sub[:, 8 + g, :], ACT.Exp, scale=-0.5).then_inc(sem("yz_root"), 1)

            def yz_heads(g):
                for m in range(4 * g, 4 * g + 4):
                    act.wait_ge(sem("yn_ready"), m + 1)
                    act.activation(yz_hi[:, m, :], y_ssd[:, m, :], ACT.Copy).then_inc(sem("yz_hi_ready"), 1)

            for i in range(16):
                c, hq = divmod(i, 8)
                act.wait_ge(sem("bc_done"), i + 1)
                if i >= NATT:
                    act.wait_ge(sem("y_done"), i - NATT + 1)
                act.activation(att[i % NATT].rearrange("p h l -> p (h l)"), pb[i % 2][:, :], ACT.Exp).then_inc(sem("att_exp"), 1)
                if i == 0:
                    act.wait_ge(sem("eab_used"), 4)
                if i >= 11:
                    square(i - 11)
                if i == 14:
                    roots([0])
            square(5)
            square(6)
            roots([1])
            square(7)
            for g in (0, 1):
                yz_heads(g)
            roots([2, 3])
            for g in (2, 3):
                yz_heads(g)
            act_layer(act, L["ssd_out"], nxt=L["up1"])
            norm_in(3)
            ffn(1, L["up1"], L["down1"], L["fox_qk"])
            norm_in(4)

            def head_roots(i, t):
                act.wait_ge(sem("fox_sum"), i + 1)
                if i:
                    act.wait_ge(sem("qk_ready"), i)
                for b in range(4):
                    ins = act.activation(tmp2[:, 2 * b:2 * b + 2, :], pb[4 + b][:, :], ACT.Ln, bias=eps[:, 0:1], scale=1.0 / HEAD)
                    ins.then_inc(sem("fox_root"), 1)
                act.wait_ge(sem("fox_root"), 4 * (i + 1))
                act.activation(tmp2, tmp2, ACT.Exp, scale=-0.5).then_inc(sem("fox_rms"), 1)

            def head_squares(i, t, blocks):
                act.wait_ge(sem("evac_done"), blocks + BANKS)
                if i:
                    act.wait_ge(sem("fox_sum"), i)
                act.activation(fox_tmp, t, ACT.Square).then_inc(sem("fox_sq"), 1)

            def q_norm(u, m):
                if (u, m) == (2, 0):
                    head_squares(0, q_t, L["fox_qk"].evac0 + KC)
                if (u, m) == (3, 0):
                    head_roots(0, q_t)
            act_layer(act, L["fox_qk"], q_norm, begin=lambda: norm_root(4))
            ahead(act_head, act, L["fox_vg"])

            def k_norm(u, m):
                if (u, m) == (0, 0):
                    head_squares(1, k_t, L["fox_qk"].evac1)
                if (u, m) == (0, 2):
                    act.wait_ge(sem("abs_ready"), 2)
                    link(act.activation(dt_e[0:FOX_HEADS, :], dt_e[0:FOX_HEADS, :], ACT.Exp, scale=-1.0))
                    act.activation(dt_e[0:FOX_HEADS, :], dt_e[0:FOX_HEADS, :], ACT.Ln, bias=1.0).then_inc(sem("log_ready"), 1)
                if (u, m) == (1, 0):
                    head_roots(1, k_t)
            act_layer(act, L["fox_vg"], k_norm)

            def o_head(k):
                act.wait_ge(sem("o_ready"), k + 1)
                act.activation(x_hi[:, k, :], o_fox[:, k, :], ACT.Copy).then_inc(sem("x_hi_ready"), 1)

            steps = 2 * FOX_HEADS
            for i in range(steps + 1):
                if i < steps:
                    n, s = (i % 2 + 1) * P, i % NS
                    act.wait_ge(sem("max_ready"), i + 1)
                    act.activation(sc[s][:, 0, 0:n], sc[s][:, 1, 0:n], ACT.Exp, bias=fox_stat[:, 2 * (i % 2), i // 2:i // 2 + 1],
                                   accum_out=fox_stat[:, 2 * (i % 2) + 1, i // 2:i // 2 + 1]).then_inc(sem("exp_ready"), 1)
                if i >= 1:
                    j = i - 1
                    n, s = (j % 2 + 1) * P, j % NS
                    act.wait_ge(sem("share_ready"), j + 1)
                    act.activation(sc[s][:, 0, 0:n], sc[s][:, 0, 0:n], ACT.Copy,
                                   scale=fox_stat[:, 4 + j % 2, j // 2:j // 2 + 1]).then_inc(sem("p_ready"), 1)
                if i == 3:
                    act.wait_ge(sem("evac_done"), L["fox_vg"].evac1 + BANKS)
                    act.activation(gate_t, gate_t, ACT.Sigmoid).then_inc(sem("fox_gate"), 1)
                if 4 <= i < 4 + LOOKAHEAD:
                    act_head(act, L["fox_out"], 0, 0, i - 4)
                if i >= 10 and (i - 10) % 4 == 0:
                    o_head((i - 10) // 4)
            for k in range(KC - 2, KC):
                o_head(k)
            act_layer(act, L["fox_out"], nxt=L["up2"])
            act.wait_ge(sem("block_done"), L["fox_out"].item1 + BANKS)
            norm_in(5)
            ffn(2, L["up2"], L["down2"])
            for k in range(KC):
                act.wait_ge(sem("x_ready"), KC * 6 + k + 1)
                act.activation(sub[:, k, :], x_res[:, k, :], ACT.Square).then_inc(sem("sq_ready"), 1)
            norm_root(6)

        @block.vector
        def _(dve):
            ch = Chain(dve, "dve_chain")
            go, sync, link = ch.go, ch.sync, ch.link
            stt, tt, ts = dve.scalar_tensor_tensor, dve.tensor_tensor, dve.tensor_scalar

            def norm_rest(n):
                name, o = NORMS[n]
                for k in range(KC):
                    dve.wait_ge(sem("x_hi_ready"), X_BASE[n] + k + 1)
                    stt(x_lo[:, k, :], x_res[:, k, :], par_col(name, o + k), x_hi[:, k, :].bitcast(F32),
                        ALU.mult, ALU.subtract).then_inc(sem("x_lo_ready"), 1)

            def norm_scale(n):
                dve.wait_ge(sem("rstd_ready"), RSTD_NORM[n])

            def scaled(dst):
                def out_block(u, m):
                    j = M_PER_UNIT * u + m
                    o = dst(j) if isinstance(u, int) else pj[:, bass.ds(j + dst(None), 1), :].rearrange("p a b -> p (a b)")
                    tt(o, pb[m][:, 0:T], rstd[:, :], ALU.mult).then_inc(sem("evac_done"), 1)
                return out_block

            for i in range(BANKS):
                dve.nop().then_inc(sem("evac_done"), 1)
            dve.wait_ge(sem("par_turned"), 1)
            link(dve.tensor_copy(par[:, 0:P], pb[1][:, 0:P]))
            for k in range(KC):
                dve.wait_ge(sem("x_turned"), k // 2 + 1)
                dve.tensor_copy(x_res[:, k, :], pb[3 + k // 2][:, T * (k % 2):T * (k % 2) + T]).then_inc(sem("x_ready"), 1)
            norm_rest(0)
            ahead(dve_rest, dve, L["rk"])
            for b in range(-(-(par_tiles - 1) // 4)):
                dve.wait_ge(sem("par_turned"), b + 2)
                c0 = P + 512 * b
                n = min(n_rows - c0, 512)
                go(dve.tensor_copy(par[:, c0:c0 + n], pb[4 + b][:, 0:n]))
            sync()

            def shift_less(o, s):
                go(tt(o[:, :, 1:T], s[:, :, 0:T - 1], s[:, :, 1:T], ALU.subtract))
                link(ts(o[:, :, 0:1], s[:, :, 0:1], -1.0, None, ALU.mult))

            dve_layer(dve, L["rk"], scaled(lambda j: tile(0, j)), begin=lambda: norm_scale(0))
            dve.wait_ge(sem("evac_done"), L["rk"].evac1 + BANKS)

            def lerp(s, i):
                shift_less(mix_tmp, slot(s))
                for k in range(KC):
                    go(stt(slot(s)[:, k, :], mix_tmp[:, k, :], par_col("mu_rkv", KC * i + k), slot(s)[:, k, :], ALU.mult, ALU.add))
                sync()
            lerp(K, 1)
            dve.wait_ge(sem("lora1_done"), 1)
            for k in range(KC):
                go(ts(slot(KK)[:, k, :], slot(K)[:, k, :], par_col("k_k", k), None, ALU.mult))
            sync()
            dve.nop().then_inc(sem("dve_stages"), 1)
            lerp(R, 0)
            dve.wait_ge(sem("lora_ready"), 8)
            for k in range(KC):
                go(ts(rate_tmp[:, k, :], slot(A)[:, k, :], 1.0, par_col("k_a", k), ALU.subtract, ALU.mult))
            sync()
            link(stt(slot(K), rate_tmp, 1.0, slot(K), ALU.add, ALU.mult))
            ahead(dve_rest, dve, L["v"])
            dve.wait_ge(sem("kk_sum"), 1)
            for b in range(4):
                ts(slot(TMP)[:, 2 * b:2 * b + 2, :], pb[4 + b][:, :], 1e-24, None, ALU.max).then_inc(sem("kk_max"), 1)
            for k in range(KC):
                go(stt(mix_tmp[:, k, :], slot(R)[:, k, :], par_col("r_k", k), slot(K)[:, k, :], ALU.mult, ALU.mult))
            sync()
            dve.nop().then_inc(sem("dve_stages"), 1)

            def chunks(i):
                return slot(i).rearrange("p k (c s) -> p (k c) s", s=CHUNK)

            bk_v = bk.rearrange("p k c j s -> p (k c) j s")

            def prep(i):
                if i == 2:
                    dve.wait_ge(sem("kk_root"), 1)
                    link(tt(slot(KK), slot(KK), slot(TMP), ALU.mult))
                if i == 3:
                    go(tt(slot(A), slot(KK), slot(A), ALU.mult))
                if i in (3, 4, 5, 6):
                    if i == 3:
                        dve.wait_ge(sem("lora_ready"), 12)
                    for k in (2 * (i - 3), 2 * (i - 3) + 1):
                        dve.tensor_tensor_scan(slot(TMP)[:, k, :], scan_mask[:, :], slot(W)[:, k, :], 0.0, ALU.mult,
                                               ALU.add).then_inc(sem("cum_ready"), 1)
                if i == 9:
                    dve.wait_ge(sem("decay_ready"), 1)
                    go(stt(chunks(KK)[:, :, 1:CHUNK], chunks(KK)[:, :, 1:CHUNK], -1.0, chunks(W)[:, :, 0:CHUNK - 1], ALU.mult, ALU.mult))
                    go(ts(chunks(KK)[:, :, 0:1], chunks(KK)[:, :, 0:1], -1.0, None, ALU.mult))
                if i == 10:
                    dve.wait_ge(sem("decay_ready"), 2)
                    dve.wait_ge(sem("bonus_done"), 1)
                    go(tt(bk_v[:, :, 1, :], chunks(A), chunks(TMP), ALU.mult))
                if i == 11:
                    go(dve.tensor_copy(chunk_decay[:, :, :].rearrange("p k c -> p (k c)"), chunks(W)[:, :, CHUNK - 1]))
                    sync()
                    dve.nop().then_inc(sem("dve_stages"), 1)
                if i == 12:
                    go(tt(bk_v[:, :, 0, :], chunks(K), chunks(TMP), ALU.mult))
            def lower_parts():
                sync()
                dve.wait_ge(sem("pool_stages"), R_DECAYED)
                for c in range(NCHUNK):
                    dve.wait_ge(sem("lab_done"), c + 1)
                    dst = lab_t[:, 16 * c:16 * c + 16, :].rearrange("s (m h) t -> s h m t", h=2)
                    for h in range(2):
                        ins = tt(dst[:, h], pb[4 + 2 * h + c % 2][0:CHUNK, 0:T].rearrange("s (m t) -> s m t", t=CHUNK),
                                 g_mask[0:CHUNK, CHUNK:2 * CHUNK].unsqueeze(1).broadcast_to([CHUNK, 8, CHUNK]), ALU.mult)
                        if h:
                            ins.then_inc(sem("lab_ready"), 1)
                        else:
                            go(ins)
                dve.wait_ge(sem("lab_ready"), NCHUNK)

            def substitute(first, last):
                for t in range(first, min(last, CHUNK)):
                    if t == 1:
                        dve.wait_ge(sem("sub_dma"), 32)
                        link(dve.memset(mt, 0.0))
                        link(dve.memset(mt.rearrange("p s t -> p (s t)")[:, 0:CHUNK * CHUNK:CHUNK + 1], 1.0))
                    link(tt(prod[:, 0:t, 0:t], mt[:, 0:t, 0:t], lt[:, 0:t, t].unsqueeze(1).broadcast_to([P, t, t]), ALU.mult))
                    link(dve.tensor_reduce(mt[:, 0:t, t], prod[:, 0:t, 0:t], AX_X, ALU.add))

            def v_hook(u, m):
                prep(M_PER_UNIT * u + m)

            def ug_hook(u, m):
                i = M_PER_UNIT * u + m
                prep(M_PER_UNIT * len(L["v"]) + i)
                if i == LAB_BLOCK:
                    lower_parts()
                if i >= SUB_BLOCK:
                    substitute(1 + SUB_STEPS * (i - SUB_BLOCK), 1 + SUB_STEPS * (i - SUB_BLOCK + 1))

            def z_rest(j):
                dve_rest(dve, L["z"], j // M_PER_UNIT, j // M_PER_UNIT % 2, j % M_PER_UNIT)

            def z_rests(first, last):
                for j in range(first, min(last, len(L["z"]) * M_PER_UNIT)):
                    z_rest(j)

            def z_evac(first, last):
                for j in range(first, min(last, len(L["z"]) * M_PER_UNIT)):
                    dve.wait_ge(sem("block_done"), L["z"].item0 + j + 1 + BANKS)
                    if j == KC:
                        dve.wait_ge(sem("tap_summed"), CONV_TAPS - 1)
                    o = slot(ZR)[:, j, :] if j < KC else slot(ZC)[:, j - KC, :]
                    tt(o, z_bank(j), rstd[:, :], ALU.mult).then_inc(sem("evac_done"), 1)
            dve_layer(dve, L["v"], scaled(lambda j: tile(16, j)), v_hook, nxt=L["ug"])
            dve_layer(dve, L["ug"], scaled(lambda j: tile(24, j)), ug_hook)
            z_rests(0, BANKS)
            done = 1 + SUB_STEPS * (M_PER_UNIT * len(L["ug"]) - SUB_BLOCK)
            substitute(done, (done + CHUNK) // 2)
            z_evac(0, Z_EARLY)
            z_rests(BANKS, BANKS + Z_EARLY)
            substitute((done + CHUNK) // 2, CHUNK)
            dve.nop().then_inc(sem("dve_stages"), 1)

            def conv_taps(first, last):
                for s in range(first, min(last, CONV_TAPS)):
                    for k in range(POOL_TILES, KC):
                        w = par_col("conv_dw", KC * (CONV_TAPS - 1 - s) + k)
                        o, c = slot(GATE)[:, k, :], slot(U)[:, k, :]
                        if s == 0:
                            go(ts(o, c, w, par_col("conv_b", k), ALU.mult, ALU.add))
                        else:
                            go(stt(o[:, s:T], c[:, 0:T - s], w, o[:, s:T], ALU.mult, ALU.add))
                    sync()
            dve.wait_ge(sem("pool_stages"), GLU_MADE)

            def mask_products(c):
                dve.wait_ge(sem("g_done"), c + 1)
                if c >= 2:
                    dve.wait_ge(sem("y2_done"), c - 1)
                for h in range(2):
                    go(tt(g_buf[c % 2][:, h::2, :], pb[h][64:128, :].rearrange("s (m n) -> s m n", n=64),
                          g_mask[64:128, :].unsqueeze(1).broadcast_to([64, 8, 64]), ALU.mult))
                sync()
                dve.nop().then_inc(sem("g_masked"), 1)
                v = bk[:, :, c, :, :].rearrange("p k j s -> p k (j s)")
                tt(v, v, chunk_decay[:, :, c:c + 1].broadcast_to([P, KC, 2 * CHUNK]), ALU.mult).then_inc(sem("bk_scaled"), 1)

            def state_sum(c):
                dve.wait_ge(sem("s_done"), c + 1)
                for h in range(2):
                    rows = slice(64 * h, 64 * h + 64)
                    go(tt(state[rows, :, rows], state[rows, :, rows],
                          pb[6][rows, :].rearrange("k (m v) -> k m v", v=64), ALU.add))
                sync()
                dve.nop().then_inc(sem("state_ready"), 1)

            mask_products(0)
            dve.wait_ge(sem("pool_stages"), STATE_ZEROED)
            dve.nop().then_inc(sem("state_ready"), 1)
            conv_taps(0, DVE_EARLY)
            cv = slot(GATE)
            for c in range(NCHUNK):
                dve.wait_ge(sem("x_done"), c + 1)
                dve.tensor_copy(x_buf[:, 0:512], pb[4][0:CHUNK, :]).then_inc(sem("x_rows_v"), 1)
                z_evac(Z_EARLY + Z_CHUNK * c, Z_EARLY + Z_CHUNK * (c + 1))
                if c + 1 < NCHUNK:
                    dve.wait_ge(sem("y1_done"), c + 1)
                    go(tt(state, state, chunk_decay[:, :, c:c + 1].broadcast_to([P, KC, P]), ALU.mult))
                    mask_products(c + 1)
                    if c == NCHUNK - 2:
                        dve.wait_ge(sem("ln_mean"), 1)
                        link(ts(rs[:, :], pb[6][:, 0:T], 1.0 / D, None, ALU.mult))
                else:
                    link(tt(cv, cv, rs[:, :].unsqueeze(1).broadcast_to([P, KC, T]), ALU.subtract))
                    dve.nop().then_inc(sem("ln_centred"), 1)
                dve.wait_ge(sem("u_done"), c + 1)
                dve.tensor_copy(uv[c % 2][CHUNK:2 * CHUNK, 0:512], pb[4][0:CHUNK, :]).then_inc(sem("u_rows_v"), 1)
                if c + 1 < NCHUNK:
                    state_sum(c)
                dve.wait_ge(sem("y2_done"), c + 1)
                dve.tensor_copy(slot(R)[:, :, CHUNK * c:CHUNK * c + CHUNK],
                                pb[7][:, 0:T].rearrange("p (m t) -> p m t", t=CHUNK)).then_inc(sem("y_out"), 1)
                conv_taps(DVE_EARLY + DVE_CHUNK * c, DVE_EARLY + DVE_CHUNK * (c + 1))
                if c == NCHUNK - 3:
                    dve.nop().then_inc(sem("conv_ready"), 1)
                if c == NCHUNK - 2:
                    ahead(dve_rest, dve, L["conv_out"])
                z_rests(BANKS + Z_EARLY + Z_CHUNK * c, BANKS + Z_EARLY + Z_CHUNK * (c + 1))
            dve.wait_ge(sem("y_out"), NCHUNK)

            y = slot(R)
            def mix_rest(i, tiles, src, hi, lo):
                for k in tiles:
                    dve.wait_ge(sem("x_hi_ready"), KC * (i + 1) + k + 1)
                    tt(lo[:, k, :], slot(src)[:, k, :], hi[:, k, :].bitcast(F32), ALU.subtract).then_inc(sem("x_lo_ready"), 1)

            dve.wait_ge(sem("ln_root"), 1)
            for k in range(KC):
                tt(cv[:, k, :], cv[:, k, :], rs[:, :], ALU.mult).then_inc(sem("ln_ready"), 1)
            dve.wait_ge(sem("gn_mean"), 1)
            for b in range(4):
                yb = y[:, 2 * b:2 * b + 2, :].rearrange("p k t -> p (k t)")
                stt(yb, pb[b][:, :], -1.0 / HEAD, yb, ALU.mult, ALU.add).then_inc(sem("gn_centred"), 1)
            for k in range(KC):
                dve.wait_ge(sem("ln_sig"), k + 1)
                tt(cv[:, k, :], slot(TMP)[:, k, :], slot(U)[:, k, :], ALU.mult).then_inc(sem("mix_in"), 1)
                if k:
                    mix_rest(0, [k - 1], GATE, x_hi, x_lo)
            mix_rest(0, [KC - 1], GATE, x_hi, x_lo)
            dve.wait_ge(sem("bonus_out"), 1)
            for b in range(4):
                go(tt(slot(W)[:, 2 * b:2 * b + 2, :].rearrange("p k t -> p (k t)"),
                      slot(V)[:, 2 * b:2 * b + 2, :].rearrange("p k t -> p (k t)"), pb[4 + b][:, :], ALU.mult))

            def gate_conv(u, m):
                o = slot(ZC)[:, M_PER_UNIT * u + m, :]
                tt(o, o, pb[m][:, 0:T], ALU.mult).then_inc(sem("evac_done"), 1)

            def gn_steps(u, m):
                i = M_PER_UNIT * u + m
                if i == 2:
                    dve.wait_ge(sem("gn_root"), 4 + 1 + KC)
                    sync()
                    link(tt(y, y, slot(W), ALU.add))
                if i == 3:
                    link(tt(y, y, slot(G), ALU.mult))
                    dve.nop().then_inc(sem("mix_in"), 1)
                if i >= 4:
                    mix_rest(1, range(2 * (i - 4), 2 * (i - 3)), R, y_hi, y_lo)
            dve.wait_ge(sem("z_ready"), 2)
            dve_layer(dve, L["conv_out"], gate_conv, gn_steps, nxt=L["rwkv_out"])

            def gate_rwkv(u, m):
                o, z = slot(ZC)[:, M_PER_UNIT * u + m, :], slot(ZR)[:, M_PER_UNIT * u + m, :]
                tt(z, z, pb[m][:, 0:T], ALU.mult).then_inc(sem("evac_done"), 1)
                dve.wait_ge(sem("evac_done"), L["rwkv_out"].evac0 + M_PER_UNIT * u + m + 1 + BANKS)
                tt(o, o, z, ALU.add).then_inc(sem("mix_in"), 1)

            def mixed_rests(u, m):
                j = M_PER_UNIT * u + m
                if j >= 2:
                    mix_rest(2, [j - 2], ZC, x_hi, x_lo)
            dve_layer(dve, L["rwkv_out"], gate_rwkv, mixed_rests, nxt=L["w_out"])
            mix_rest(2, range(KC - 2, KC), ZC, x_hi, x_lo)

            def plain(dst):
                def out_block(u, m):
                    dve.tensor_copy(tile(dst, M_PER_UNIT * u + m), pb[m][:, 0:T]).then_inc(sem("evac_done"), 1)
                return out_block

            def post_norm(i, src, name):
                dve.wait_ge(sem("rstd_ready"), RSTD_BRANCH[i])
                n = ch.n
                for k in range(KC + 1):
                    if k < KC:
                        go(stt(tile(src, k), tile(src, k), par_col(name, k), rstd[:, :], ALU.mult, ALU.mult))
                    if k:
                        dve.wait_ge(sem("dve_chain"), n + k)
                        tt(x_res[:, k - 1, :], x_res[:, k - 1, :], tile(src, k - 1), ALU.add).then_inc(sem("x_ready"), 1)

            dve_layer(dve, L["w_out"], plain(0), nxt=L["up0"])
            post_norm(0, 0, "post_mix_norm")
            norm_rest(1)

            def ffn(n, up, down, out_block, nxt=None):
                w = lambda tap, j: par_col("ffn_conv_w_2", (n - 1) * GLU_TAPS * FC + tap * FC + j)

                def hidden(u, m):
                    if m < 2:
                        tt(g_tile[m], pb[m][:, 0:T], rstd[:, :], ALU.mult).then_inc(sem("evac_done"), 1)
                        if n and m == 1:
                            glu_conv(u)
                    else:
                        dve.wait_ge(sem("glu_silu"), FC * n + 2 * u + m - 1)
                        tt(a_tile[m - 2], pb[m][:, 0:T], s_tile[m - 2], ALU.mult).then_inc(sem("evac_done"), 1)
                    if m == 3:
                        for i in range(2):
                            j = 2 * u + i
                            if isinstance(u, int):
                                hi_, lo_ = act_hi[:, j, :], act_lo[:, j, :]
                            else:
                                hi_, lo_ = (t[:, bass.ds(j, 1), :].rearrange("p a b -> p (a b)") for t in (act_hi, act_lo))
                            dve.wait_ge(sem("act_hi_ready"), FC * n + j + 1)
                            tt(lo_, a_tile[i], hi_.bitcast(F32), ALU.subtract).then_inc(sem("act_lo_ready"), 1)

                def glu_conv(u):
                    for s in range(GLU_TAPS):
                        for m in range(2):
                            j = 2 * u + m
                            if s == 0:
                                dve.wait_ge(sem("evac_done"), up.evac0 + M_PER_UNIT * u + m + 1 + BANKS)
                                ins = ts(c_tile[m], g_tile[m], w(2, j), par_col("ffn_conv_b_2", (n - 1) * FC + j), ALU.mult, ALU.add)
                            else:
                                dve.wait_ge(sem("glu_step"), 4 * (len(up) * (n - 1) + u) + 2 * s + m - 1)
                                ins = stt(c_tile[m][:, s:T], g_tile[m][:, 0:T - s], w(2 - s, j), c_tile[m][:, s:T], ALU.mult, ALU.add)
                            ins.then_inc(sem("glu_gate" if s == GLU_TAPS - 1 else "glu_step"), 1)
                dve_layer(dve, up, hidden, rest_last=True, nxt=down, begin=lambda: norm_scale((1, 3, 5)[n]))
                dve_layer(dve, down, out_block, nxt=nxt)

            def residual(u, m):
                x = x_res[:, M_PER_UNIT * u + m, :]
                ins = tt(x, x, pb[m][:, 0:T], ALU.add)
                ins.then_inc(sem("x_ready"), 1)
                dve.nop().then_inc(sem("evac_done"), 1)

            ffn(0, L["up0"], L["down0"], plain(64), L["ssd_z"])
            post_norm(1, 64, "post_ffn_norm")
            norm_rest(2)

            def gain_in(n):
                name, o = NORMS[n]
                for k in range(KC):
                    ts(x_gain[:, k, :], x_res[:, k, :], par_col(name, o + k), None, ALU.mult).then_inc(sem("gain_ready"), 1)


            def z_gain(u, m):
                if (u, m) == (1, 0):
                    gain_in(2)
            dve_layer(dve, L["ssd_z"], scaled(lambda j: z_t[:, j, :]), z_gain, begin=lambda: norm_scale(2), nxt=L["ssd_xbc"])
            ly = L["ssd_xbc"]
            n_xbc = SSD_XBC

            def xbc_tile(j):
                return xbc[:, j, :] if isinstance(j, int) else pj[:, bass.ds(SSD_Z + j, 1), :].rearrange("p a b -> p (a b)")

            for m in range(M_PER_UNIT):
                dve.nop().then_inc(sem("xbc_conv"), 1)

            def xbc_block(u, m):
                dve.wait_ge(sem("xbc_conv"), M_PER_UNIT * u + m + 1)
                tt(conv_in[m], pb[m][:, 0:T], rstd[:, :], ALU.mult).then_inc(sem("evac_done"), 1)
                if m >= 2:
                    xbc_taps(u, 2 * (m - 2))

            def xbc_taps(u, first):
                for s in range(1, SSD_TAPS):
                    for i in range(2):
                        m = first + i
                        j = M_PER_UNIT * u + m
                        t = xbc_tile(j)
                        if s == 1:
                            dve.wait_ge(sem("xbc_begun"), j + 1)
                        else:
                            dve.wait_ge(sem("xbc_step"), 8 * u + 2 * first + 2 * (s - 2) + i + 1)
                        stt(t[:, s:T], conv_in[m][:, 0:T - s], par_col("ssd_conv_w_2", (SSD_TAPS - 1 - s) * n_xbc + j), t[:, s:T],
                            ALU.mult, ALU.add).then_inc(sem("xbc_conv" if s == SSD_TAPS - 1 else "xbc_step"), 1)
            dve_layer(dve, ly, xbc_block, rest_last=True)
            dve.wait_ge(sem("narrow_done"), 1)
            dve.wait_ge(sem("small_loaded"), 16 * 9)
            link(tt(dt_z, pb[4][0:SSD_HEADS, 0:T], rstd[0:SSD_HEADS, :], ALU.mult))
            link(ts(dt_z, dt_z, heads_col[:, 0:1], None, ALU.add))
            stt(dt_e, dt_z, -1.0, dt_z, ALU.mult, ALU.max).then_inc(sem("abs_ready"), 1)
            dve.wait_ge(sem("log_ready"), 1)
            link(stt(dt, dt_z, 0.0, dt_e, ALU.max, ALU.add))
            link(ts(dt_z, dt, heads_col[:, 3:4], -1.0, ALU.mult, ALU.mult))
            for c in range(2):
                s = slice(c * P, c * P + P)
                dve.tensor_tensor_scan(acs[:, s], ones[0:SSD_HEADS, :], dt_z[:, s], 0.0, ALU.mult, ALU.add).then_inc(sem("acs_ready"), 1)
            for c in range(2):
                dve.wait_ge(sem("cb_done"), c + 1)
                tt(cbm[:, c], pb[6 + c][:, :].rearrange("p (g l) -> p g l", l=P),
                   tri[:, :].unsqueeze(1).broadcast_to([P, SSD_GROUPS, P]), ALU.mult).then_inc(sem("cbm_ready"), 1)
            dve.wait_ge(sem("b_turned"), 1)
            dve.tensor_copy(b_tok.rearrange("p g n -> p (g n)"), pb[5][:, :]).then_inc(sem("b_tok_ready"), 1)
            dve.wait_ge(sem("heads_turned"), 1)
            flat_heads = tok_heads[:, :, :].rearrange("p a h -> p (a h)")
            link(dve.tensor_copy(flat_heads, pb[4][:, 0:5 * SSD_HEADS]))
            dve.nop().then_inc(sem("heads_ready"), 1)
            for i in range(8):
                c, b = divmod(i, 4)
                dve.wait_ge(sem("xs_turned"), i + 1)
                tt(xdt[:, c, 512 * b:512 * b + 512].rearrange("p (h d) -> p h d", d=HEAD),
                   pb[6 + i % 2][:, :].rearrange("p (h d) -> p h d", d=HEAD),
                   tok_heads[:, 2 + c, 8 * b:8 * b + 8].unsqueeze(2).broadcast_to([P, 8, HEAD]), ALU.mult).then_inc(sem("xdt_ready"), 1)
            for g in range(SSD_GROUPS):
                dve.wait_ge(sem("st_done"), g + 1)
                dve.tensor_copy(st_ssd[:, 512 * g:512 * g + 512], pb[6 + g % 2][:, :]).then_inc(sem("st_ready"), 1)
            for b in range(4):
                dve.wait_ge(sem("yoff_done"), b + 1)
                dve.wait_ge(sem("eab_ready"), b + 1)
                tt(y_ssd[:, 4 * b:4 * b + 4, P:T], pb[4 + b % 2][:, :].rearrange("p (m l) -> p m l", l=P),
                   eab[:, 4 * b:4 * b + 4, :], ALU.mult).then_inc(sem("eab_used"), 1)
            dve.wait_ge(sem("eab_used"), 4)

            def yz_norm(g):
                dve.wait_ge(sem("yz_root"), g + 1)
                for m in range(4 * g, 4 * g + 4):
                    stt(y_ssd[:, m, :], y_ssd[:, m, :], par_col("ssd_norm_g_2", m), sub[:, 8 + g, :], ALU.mult, ALU.mult).then_inc(sem("yn_ready"), 1)

            for i in range(17):
                if i < 16:
                    c, hq = divmod(i, 8)
                    dve.wait_ge(sem("att_exp"), i + 1)
                    t = att[i % NATT]
                    tt(t, t, cbm[:, c, hq // 2, :].unsqueeze(1).broadcast_to([P, 4, P]), ALU.mult).then_inc(sem("att_ready"), 1)
                if i >= 1:
                    c, hq = divmod(i - 1, 8)
                    dve.wait_ge(sem("y_done"), i)
                    src = pb[2 + (i - 1) % 2][:, 0:T].rearrange("p (m l) -> p m l", l=P)
                    if c == 0:
                        for r in range(2):
                            m = 2 * hq + r
                            ins = stt(y_ssd[:, m, 0:P], xbc[:, m, 0:P], d_skip[:, m:m + 1], src[:, r, :], ALU.mult, ALU.add)
                            if r == 0:
                                go(ins)
                        ins.then_inc(sem("y_out_ssd"), 1)
                    else:
                        yy = y_ssd[:, 2 * hq:2 * hq + 2, :]
                        tt(yy[:, :, P:T], yy[:, :, P:T], src, ALU.add).then_inc(sem("y_out_ssd"), 1)
                        dve.wait_ge(sem("z_silu"), 4)
                        dve.wait_ge(sem("y_out_ssd"), i)
                        tt(yy, yy, z_t[:, 2 * hq:2 * hq + 2, :], ALU.mult).then_inc(sem("yz_ready"), 1)
                if i < 8:
                    for m in (2 * i, 2 * i + 1):
                        go(stt(y_ssd[:, m, P:T], xbc[:, m, P:T], d_skip[:, m:m + 1], y_ssd[:, m, P:T], ALU.mult, ALU.add))
                if i == 8:
                    sync()
                if 4 <= i < 4 + LOOKAHEAD:
                    dve_rest(dve, L["ssd_out"], 0, 0, i - 4)
                if i == 15:
                    yz_norm(0)

            def yz_rest(g):
                for m in range(4 * g, 4 * g + 4):
                    dve.wait_ge(sem("yz_hi_ready"), m + 1)
                    tt(yz_lo[:, m, :], y_ssd[:, m, :], yz_hi[:, m, :].bitcast(F32), ALU.subtract).then_inc(sem("yz_lo_ready"), 1)

            yz_norm(1)
            for g in (0, 1):
                yz_rest(g)
            for g in (2, 3):
                yz_norm(g)
            for g in (2, 3):
                yz_rest(g)
            dve_layer(dve, L["ssd_out"], residual, nxt=L["up1"])
            norm_rest(3)
            ffn(1, L["up1"], L["down1"], residual, L["fox_qk"])
            norm_rest(4)

            dve.nop().then_inc(sem("fox_arena_free"), 1)
            nh = FOX_HEADS

            def norm_head(i):
                t, g = ((q_t, fox_g[:, 2:3]), (k_t, fox_g[:, 1:2]))[i]
                dve.wait_ge(sem("fox_rms"), i + 1)
                stt(t, t, g, tmp2, ALU.mult, ALU.mult).then_inc(sem("qk_ready"), 1)

            def qk_hook(u, m):
                if (u, m) == (1, 0):
                    gain_in(4)
                    go(ts(fox_g[:, 2:3], fox_g[:, 0:1], HEAD ** -0.5, None, ALU.mult))
                if (u, m) == (3, 2):
                    sync()
                    norm_head(0)
            dve_layer(dve, L["fox_qk"], scaled(lambda j: tile(0, j)), qk_hook, begin=lambda: norm_scale(4))
            ahead(dve_rest, dve, L["fox_vg"])

            def vg_hook(u, m):
                if (u, m) == (0, 0):
                    dve.wait_ge(sem("narrow_done"), 2)
                    link(tt(dt_z[0:nh, :], pb[4][0:nh, 0:T], rstd[0:nh, :], ALU.mult))
                    link(ts(dt_z[0:nh, :], dt_z[0:nh, :], heads_col[0:nh, 2:3], None, ALU.add))
                    stt(dt_e[0:nh, :], dt_z[0:nh, :], -1.0, dt_z[0:nh, :], ALU.mult, ALU.max).then_inc(sem("abs_ready"), 1)
                if (u, m) == (1, 0):
                    dve.wait_ge(sem("log_ready"), 2)
                    link(stt(dt[0:nh, :], dt_z[0:nh, :], 0.0, dt_e[0:nh, :], ALU.min, ALU.subtract))
                    link(dve.tensor_tensor_scan(acs[0:nh, 0:P], ones[0:nh, :], dt[0:nh, 0:P], 0.0, ALU.mult, ALU.add))
                    link(dve.tensor_tensor_scan(acs[0:nh, P:T], ones[0:nh, :], dt[0:nh, P:T], acs[0:nh, P - 1:P], ALU.mult, ALU.add))
                    link(ts(cum_neg[0:nh, :], acs[0:nh, :], -1.0, None, ALU.mult))
                    dve.nop().then_inc(sem("cum_fox"), 1)
                if (u, m) == (1, 3):
                    norm_head(1)
                if (u, m) == (2, 1):
                    dve.wait_ge(sem("cq_turned"), 1)
                    dve.tensor_copy(tok_heads[:, 0:2, 0:nh], pb[4][:, 0:2 * nh].rearrange("p (c h) -> p c h", c=2)).then_inc(sem("cq_ready"), 1)
                if u == 3:
                    dve.wait_ge(sem("v_fox_turned"), m + 1)
                    dve.tensor_copy(v_tok[:, m // 2, 512 * (m % 2):512 * (m % 2) + 512], pb[4 + m][:, :]).then_inc(sem("v_fox_ready"), 1)
            dve_layer(dve, L["fox_vg"], scaled(lambda j: tile(16, j)), vg_hook)
            dve.wait_ge(sem("fox_mask_ready"), 1)
            dve.wait_ge(sem("cq_ready"), 1)

            def o_rest(k):
                dve.wait_ge(sem("x_hi_ready"), X_BASE["fox"] + k + 1)
                tt(x_lo[:, k, :], o_fox[:, k, :], x_hi[:, k, :].bitcast(F32), ALU.subtract).then_inc(sem("x_lo_ready"), 1)

            steps = 2 * nh
            for i in range(steps + 4):
                if i < steps:
                    h, qc = divmod(i, 2)
                    n, s = (qc + 1) * P, i % NS
                    dve.wait_ge(sem("score_done"), i + 1)
                    if i >= NS:
                        dve.wait_ge(sem("turned"), i - NS + 1)
                    stt(sc[s][:, 1, 0:n], pb[score_banks[s]][:, 0:n], tok_heads[:, qc, h:h + 1], fox_mask[:, T - n:T],
                        ALU.add, ALU.add).then_inc(sem("masked"), 1)
                if 1 <= i <= steps:
                    h, qc = divmod(i - 1, 2)
                    dve.wait_ge(sem("exp_ready"), i)
                    dve.reciprocal(fox_stat[:, 4 + qc, h:h + 1], fox_stat[:, 2 * qc + 1, h:h + 1]).then_inc(sem("share_ready"), 1)
                if i < steps:
                    h, qc = divmod(i, 2)
                    n, s = (qc + 1) * P, i % NS
                    dve.wait_ge(sem("masked"), i + 1)
                    link(dve.tensor_reduce(fox_stat[:, 6, h:h + 1], sc[s][:, 1, 0:n], AX_X, ALU.max))
                    ts(fox_stat[:, 2 * qc, h:h + 1], fox_stat[:, 6, h:h + 1], -1.0, None, ALU.mult).then_inc(sem("max_ready"), 1)
                if 6 <= i < 6 + 2 * LOOKAHEAD and i % 2 == 0:
                    dve_rest(dve, L["fox_out"], 0, 0, (i - 6) // 2)
                if 3 <= i < steps + 3:
                    j = i - 3
                    n, s = (j % 2 + 1) * P, j % NS
                    dve.wait_ge(sem("turned"), j + 1)
                    if j >= NS:
                        dve.wait_ge(sem("pv_done"), j - NS + 1)
                    dve.tensor_copy(pt[s][:, 0:n], pb[2 + j % 2][:, 0:n]).then_inc(sem("pt_ready"), 1)
                if i >= 4 and (i - 4) % 4 == 3:
                    m = (i - 4) // 4
                    dve.wait_ge(sem("pv_done"), 4 * (m + 1))
                    dve.wait_ge(sem("fox_gate"), 1)
                    tt(o_fox[:, m, :], pb[4 + m % 2][:, 0:T], gate_t[:, m, :], ALU.mult).then_inc(sem("o_ready"), 1)
                    if m >= 1:
                        o_rest(m - 1)
            o_rest(KC - 1)
            dve_layer(dve, L["fox_out"], residual, nxt=L["up2"])
            norm_rest(5)
            ffn(2, L["up2"], L["down2"], residual)
            dve.wait_ge(sem("x_ready"), KC * 7)
            norm_scale(6)
            for k in range(KC):
                stt(tile(16, k), x_res[:, k, :], par_col("final_norm_g_2", k), rstd[:, :], ALU.mult, ALU.mult).then_inc(sem("y_ready"), 1)
            for i in range(4):
                c, b = divmod(i, 2)
                dve.wait_ge(sem("x_turned"), 4 + i + 1)
                dve.tensor_copy(y_tok[:, c, 512 * b:512 * b + 512], pb[3 + i][:, :]).then_inc(sem("y_tok_ready"), 1)

        @block.tensor
        def _(pe):
            mm = pe.matmul

            def sum_squares(n, bank=7):
                pe.wait_ge(sem("sq_added"), n + 1)
                mm(pb[bank][:, 0:T], ones[:, :], sub[:, 0, :], start=True, stop=True).then_inc(sem("ssq_done"), 1)

            def sum_tiles(n, bank=7):
                for k in range(KC):
                    pe.wait_ge(sem("sq_ready"), KC * n + k + 1)
                    ins = mm(pb[bank][:, 0:T], ones[:, :], sub[:, k, :], start=k == 0, stop=k == KC - 1)
                ins.then_inc(sem("ssq_done"), 1)

            def head_sums(src, bank0=4):
                for k in range(KC):
                    ins = mm(pb[bank0 + k // 2][:, T * (k % 2):T * (k % 2) + T], blk[:, :], src[:, k, :], start=True, stop=True)
                return ins

            def feature_sums(o, src):
                for k in range(KC):
                    ins = mm(o, ones[:, :], src[:, k, :], start=k == 0, stop=k == KC - 1)
                return ins

            def turn(o, i):
                n = i.shape[0]
                return pe.transpose(o, i, ident[0:n, 0:n])

            for i in range(BANKS):
                pe.nop().then_inc(sem("block_done"), 1)
            pe.wait_ge(sem("const_ready"), 1)
            pe.wait_ge(sem("x_loaded"), 16)
            for k in range(KC):
                for c in range(2):
                    ins = turn(pb[3 + k // 2][:, T * (k % 2) + P * c:T * (k % 2) + P * c + P], x_tok[:, c, P * k:P * k + P])
                if k % 2:
                    ins.then_inc(sem("x_turned"), 1)
            pe.wait_ge(sem("par_first"), 16 * n_pieces(range(1)))
            turn(pb[1][:, 0:P], par_tok[:, 0, :]).then_inc(sem("par_turned"), 1)

            def first_sums():
                sum_squares(0)
                pe.wait_ge(sem("par_loaded"), 16 * n_pieces(range(1, par_tiles)))
                for t in range(1, par_tiles):
                    n, i = min(P, n_rows - P * t), t - 1
                    ins = turn(pb[4 + i // 4][:, P * (i % 4):P * (i % 4) + n], par_tok[0:n, t, :])
                    if i % 4 == 3 or t == par_tiles - 1:
                        ins.then_inc(sem("par_turned"), 1)
            pe_layer(pe, L["rk"], x_hi, x_lo, "x_lo_ready", X_BASE[0], after_two=first_sums)

            s = L["lora_in"].u0 % 2
            pe.wait_ge(sem(f"landed{s}0"), L["lora_in"].landed[0][0])
            for i, (c, n, src) in enumerate(((0, 64, KK), (64, 64, A), (128, 128, G))):
                pe.wait_ge(sem("lora_x"), i + 1)
                for k in range(KC):
                    ins = mm(pb[4 + i][0:n, 0:T], raw[s][:, k, c:c + n], slot(src)[:, k, :], start=k == 0, stop=k == KC - 1)
                ins.then_inc(sem("lora1_done"), 1)
            s = L["lora_out"].u0 % 2
            pe.wait_ge(sem(f"landed{s}0"), L["lora_out"].landed[0][0])
            w2 = raw[s][:, :, :].rearrange("p k n -> p (k n)")
            for f, (rows, src) in enumerate(((64, lora_w), (64, lora_a), (128, lora_g))):
                pe.wait_ge(sem("lora_mid"), 3)
                for j in range(4):
                    i = 4 * f + j
                    if i >= 3:
                        pe.wait_ge(sem("lora_ready"), i - 2)
                    for m in (2 * j, 2 * j + 1):
                        ins = mm(pb[4 + i % 3][:, T * (m % 2):T * (m % 2) + T], w2[0:rows, D * f + P * m:D * f + P * m + P], src,
                                 start=True, stop=True)
                    ins.then_inc(sem("lora2_done"), 1)
            pe.wait_ge(sem("lora_ready"), 12)
            pe.wait_ge(sem("kk_sq"), 1)
            head_sums(slot(TMP)).then_inc(sem("kk_sum"), 1)

            def bonus_sums(u, m):
                if M_PER_UNIT * u + m == 1:
                    pe.wait_ge(sem("dve_stages"), BONUS_MADE)
                    for k in range(KC):
                        ins = mm(pb[4][0:RWKV_HEADS, 0:T], head_sel[:, k, :], mix_tmp[:, k, :], start=k == 0, stop=k == KC - 1)
                    ins.then_inc(sem("bonus_done"), 1)
            pe_layer(pe, L["v"], x_hi, x_lo, "x_lo_ready", X_BASE[0], bonus_sums)

            def lower_products(u, m):
                if M_PER_UNIT * u + m != LAB_BLOCK:
                    return
                pe.wait_ge(sem("dve_stages"), PAIRS_MADE)
                for c in range(NCHUNK):
                    if c >= 2:
                        pe.wait_ge(sem("lab_ready"), c - 1)
                    for h in range(RWKV_HEADS):
                        k, rows = h // 2, slice(64 * (h % 2), 64 * (h % 2) + 64)
                        ins = mm(pb[4 + 2 * (h % 2) + c % 2][0:CHUNK, CHUNK * k:CHUNK * k + CHUNK], bk[rows, k, c, 1, :],
                                 slot(KK)[rows, k, CHUNK * c:CHUNK * c + CHUNK], start=True, stop=True)
                    ins.then_inc(sem("lab_done"), 1)
            pe_layer(pe, L["ug"], x_hi, x_lo, "x_lo_ready", X_BASE[0], lower_products)

            def z_blocks(first, last):
                ly = L["z"]
                for j in range(first, min(last, len(ly) * M_PER_UNIT)):
                    m = j % M_PER_UNIT
                    pe.wait_ge(sem("w_lo_ready"), ly.item0 + j + 1)
                    if j >= 2:
                        pe.wait_ge(sem("evac_done"), ly.evac0 + BANKS + j - 1)
                    for k in range(KC):
                        mm(z_bank(j), w_hi[m][:, k, :], x_hi[:, k, :], start=k == 0, stop=False)
                        mm(z_bank(j), w_hi[m][:, k, :], x_lo[:, k, :], start=False, stop=False)
                        ins = mm(z_bank(j), w_lo[m][:, k, :], x_hi[:, k, :], start=False, stop=k == KC - 1)
                    ins.then_inc(sem("block_done"), 1)

            def z_out(last):
                pe.wait_ge(sem("evac_done"), L["z"].evac0 + BANKS + min(last, len(L["z"]) * M_PER_UNIT))

            def chunk_products(c):
                if c == 0:
                    pe.wait_ge(sem("pool_stages"), R_DECAYED)
                if c:
                    pe.wait_ge(sem("bk_rows"), c)
                    pe.wait_ge(sem("v_rows"), c)
                t = slice(CHUNK * c, CHUNK * c + CHUNK)
                for h in range(RWKV_HEADS):
                    m, rows = h // 2, slice(64 * (h % 2), 64 * (h % 2) + 64)
                    ins = mm(pb[h % 2][64:128, 64 * m:64 * m + 64], bk[rows, m, c, :, :].rearrange("p j s -> p (j s)"),
                             pj4[rows, 0:KK + 1:KK, m, t], start=True, stop=True)
                ins.then_inc(sem("g_done"), 1)
                for m in range(KC):
                    ins = turn(pb[2 + m // 4][0:CHUNK, P * (m % 4):P * (m % 4) + P], slot(V)[:, m, t])
                ins.then_inc(sem("v_turned"), 1)

            def chunk_keys(c):
                pe.wait_ge(sem("g_masked"), c + 1)
                pe.wait_ge(sem("bk_scaled"), c + 1)
                for m in range(KC):
                    ins = turn(pb[m // 4][0:64, P * (m % 4):P * (m % 4) + P], bk[:, m, c, :, :].rearrange("p j s -> p (j s)"))
                ins.then_inc(sem("bk_turned"), 1)

            pe.wait_ge(sem("lab_ready"), NCHUNK)
            z_blocks(0, Z_EARLY)
            pe.wait_ge(sem("evac_done"), L["ug"].evac1 + BANKS)
            chunk_products(0)
            pe.wait_ge(sem("dve_stages"), INVERSES_MADE)
            z_out(Z_EARLY)
            for i in range(CHUNK // INV_GROUP):
                if i >= 4:
                    pe.wait_ge(sem("inverse_rows"), i - 3)
                for r in range(INV_GROUP):
                    ins = turn(pb[4 + i % 4][0:CHUNK, P * r:P * r + P], mt[:, :, INV_GROUP * i + r])
                ins.then_inc(sem("inverse_turned"), 1)
            chunk_keys(0)
            pe.wait_ge(sem("inverse_rows"), CHUNK // INV_GROUP)
            for c in range(NCHUNK):
                t, q = slice(CHUNK * c, CHUNK * c + CHUNK), c % 2
                pe.wait_ge(sem("v_rows"), c + 1)
                pe.wait_ge(sem("g_masked"), c + 1)
                if c:
                    pe.wait_ge(sem("u_rows_v"), c)
                    pe.wait_ge(sem("u_rows_a"), c)
                for h in range(RWKV_HEADS):
                    mm(pb[4 + h // 8][0:CHUNK, 64 * (h % 8):64 * (h % 8) + 64], g_buf[q][0:CHUNK, h, CHUNK:2 * CHUNK],
                       uv[q][0:CHUNK, 64 * h:64 * h + 64], start=h % 8 == 0, stop=False, skip_group_check=True)
                pe.wait_ge(sem("state_ready"), c + 1)
                for m in range(KC):
                    ins = mm(pb[4 + m // 4][0:CHUNK, P * (m % 4):P * (m % 4) + P], slot(KK)[:, m, t], state[:, m, :],
                             start=False, stop=m % 4 == 3, skip_group_check=True)
                ins.then_inc(sem("x_done"), 1)
                if c:
                    pe.wait_ge(sem("y_out"), c)
                z_blocks(Z_EARLY + Z_CHUNK * c, Z_EARLY + Z_CHUNK * (c + 1))
                z_out(Z_EARLY + Z_CHUNK * (c + 1) - 1)
                for m in range(KC):
                    ins = mm(pb[7][:, CHUNK * m:CHUNK * m + CHUNK], state[:, m, :], slot(R)[:, m, t],
                             start=m == 0, stop=False, skip_group_check=True)
                ins.then_inc(sem("y1_done"), 1)
                if c == NCHUNK - 2:
                    z_out(len(L["z"]) * M_PER_UNIT)
                    pe.wait_ge(sem("conv_ready"), 1)
                    pe.wait_ge(sem("tap_summed"), CONV_TAPS - 1)
                    feature_sums(pb[6][:, 0:T], slot(GATE)).then_inc(sem("ln_mean"), 1)
                if c + 1 < NCHUNK:
                    chunk_products(c + 1)
                pe.wait_ge(sem("x_rows_v"), c + 1)
                pe.wait_ge(sem("x_rows_a"), c + 1)
                for h in range(RWKV_HEADS):
                    ins = mm(pb[4 + h // 8][0:CHUNK, 64 * (h % 8):64 * (h % 8) + 64], lab_t[:, 16 * c + h, :],
                             x_buf[:, 64 * h:64 * h + 64], start=True, stop=True)
                ins.then_inc(sem("u_done"), 1)
                if c + 1 < NCHUNK:
                    chunk_keys(c + 1)
                else:
                    pe.wait_ge(sem("ln_sq"), 1)
                    feature_sums(pb[6][:, 0:T], slot(U)).then_inc(sem("ln_var"), 1)
                pe.wait_ge(sem("u_rows_v"), c + 1)
                pe.wait_ge(sem("u_rows_a"), c + 1)
                pe.wait_ge(sem("bk_rows"), c + 1)
                if c + 1 < NCHUNK:
                    z_out(Z_EARLY + Z_CHUNK * (c + 1))
                    for h in range(RWKV_HEADS):
                        ins = mm(pb[6][64 * (h % 2):64 * (h % 2) + 64, 64 * (h // 2):64 * (h // 2) + 64],
                                 bk_t[q][:, 64 * h:64 * h + 64], uv[q][:, 64 * h:64 * h + 64], start=True, stop=True)
                    ins.then_inc(sem("s_done"), 1)
                for h in range(RWKV_HEADS):
                    ins = mm(pb[7][64 * (h % 2):64 * (h % 2) + 64, CHUNK * (h // 2):CHUNK * (h // 2) + CHUNK],
                             uv[q][:, 64 * h:64 * h + 64], g_buf[q][:, h, 0:CHUNK], start=False, stop=h >= 14, skip_group_check=True)
                ins.then_inc(sem("y2_done"), 1)
            pe.wait_ge(sem("y_out"), NCHUNK)
            head_sums(slot(R), 0).then_inc(sem("gn_mean"), 1)
            pe.wait_ge(sem("ln_root"), 1)
            for h in range(RWKV_HEADS):
                m = h // 2
                ins = mm(pb[4 + m // 2][64 * (h % 2):64 * (h % 2) + 64, T * (m % 2):T * (m % 2) + T],
                         ident[0:RWKV_HEADS, h:h + 1].broadcast_to([RWKV_HEADS, 64]), bonus, start=True, stop=True)
            ins.then_inc(sem("bonus_out"), 1)
            pe.wait_ge(sem("gn_centred"), 4)
            pe.wait_ge(sem("pool_stages"), GN_SQUARED)
            head_sums(tmp2, 0).then_inc(sem("gn_var"), 1)
            pe.wait_ge(sem("gn_root"), 4)

            pe_layer(pe, L["conv_out"], x_hi, x_lo, "x_lo_ready", KC)
            pe_layer(pe, L["rwkv_out"], y_hi, y_lo, "x_lo_ready", 2 * KC)
            pe_layer(pe, L["w_out"], x_hi, x_lo, "x_lo_ready", 3 * KC)

            def post_squares(i):
                for k in range(KC):
                    pe.wait_ge(sem("osq_ready"), KC * i + k + 1)
                    ins = mm(pb[7][:, 0:T], ones[:, :], sub[:, k, :], start=k == 0, stop=k == KC - 1)
                ins.then_inc(sem("osum_done"), 1)

            post_squares(0)
            pe_layer(pe, L["up0"], x_hi, x_lo, "x_lo_ready", X_BASE[1], after_two=lambda: sum_squares(1))
            pe_layer(pe, L["down0"], act_hi, act_lo, "act_lo_ready", 0)
            post_squares(1)

            def narrow_product(ly, n, nth):
                s = ly.u0 % 2
                pe.wait_ge(sem(f"landed{s}0"), ly.landed[0][0])
                pe.wait_ge(sem("gain_ready"), KC * nth)
                for k in range(KC):
                    ins = mm(pb[4][0:n, 0:T], raw[s][:, k, 0:n], x_gain[:, k, :], start=k == 0, stop=k == KC - 1)
                ins.then_inc(sem("narrow_done"), 1)

            pe_layer(pe, L["ssd_z"], x_hi, x_lo, "x_lo_ready", X_BASE[2], after_two=lambda: sum_squares(2))
            pe_layer(pe, L["ssd_xbc"], x_hi, x_lo, "x_lo_ready", X_BASE[2])
            narrow_product(L["ssd_dt"], SSD_HEADS, 1)
            pe.wait_ge(sem("xbc_ready"), M_PER_UNIT + SSD_XBC)
            for c in range(2):
                t = slice(P * c, P * c + P)
                for g in range(SSD_GROUPS):
                    ins = mm(pb[6 + c][:, P * g:P * g + P], xbc[:, 16 + g, t], xbc[:, 20 + g, t], start=True, stop=True)
                ins.then_inc(sem("cb_done"), 1)
            for g in range(SSD_GROUPS):
                ins = turn(pb[5][:, P * g:P * g + P], xbc[:, 16 + g, 0:P])
            ins.then_inc(sem("b_turned"), 1)
            pe.wait_ge(sem("da_ready"), 1)
            for i, src in enumerate((dt_z[:, 0:P], dt_z[:, P:T], dt[:, 0:P], dt[:, P:T], da_end)):
                ins = turn(pb[4][:, SSD_HEADS * i:SSD_HEADS * i + SSD_HEADS], src)
            ins.then_inc(sem("heads_turned"), 1)
            pe.wait_ge(sem("cbm_ready"), 2)
            for i in range(8):
                c, b = divmod(i, 4)
                if i >= 2:
                    pe.wait_ge(sem("xdt_ready"), i - 1)
                for r in range(4):
                    ins = turn(pb[6 + i % 2][:, P * r:P * r + P], xbc[:, 4 * b + r, P * c:P * c + P])
                ins.then_inc(sem("xs_turned"), 1)
            pe.wait_ge(sem("heads_ready"), 1)
            pe.wait_ge(sem("b_tok_ready"), 1)

            def on_head(o, h, src):
                return mm(o, ident[0:SSD_HEADS, h:h + 1].broadcast_to([SSD_HEADS, o.shape[0]]), src, start=True, stop=True)

            for b in range(4):
                if b >= 2:
                    pe.wait_ge(sem("eab_ready"), b - 1)
                for h in range(8 * b, 8 * b + 8):
                    m = h // 2
                    ins = on_head(pb[4 + b % 2][64 * (h % 2):64 * (h % 2) + 64, P * (m % 4):P * (m % 4) + P], h, da_exp)
                ins.then_inc(sem("eab_done"), 1)
            pe.wait_ge(sem("xdt_end_ready"), 1)
            pe.wait_ge(sem("xdt_ready"), 8)
            for g in range(SSD_GROUPS):
                if g >= 2:
                    pe.wait_ge(sem("st_ready"), g - 1)
                mm(pb[6 + g % 2][:, :], b_tok[:, g, :], xdt_end[:, 512 * g:512 * g + 512], start=True, stop=True).then_inc(sem("st_done"), 1)
            pe.wait_ge(sem("eab_ready"), 4)
            for b in range(4):
                pe.wait_ge(sem("st_ready"), b + 1)
                if b >= 2:
                    pe.wait_ge(sem("eab_used"), b - 1)
                for m in range(4 * b, 4 * b + 4):
                    ins = mm(pb[4 + b % 2][:, P * (m % 4):P * (m % 4) + P], st_ssd[:, P * m:P * m + P], xbc[:, 20 + b, P:T], start=True, stop=True)
                ins.then_inc(sem("yoff_done"), 1)
            pe.wait_ge(sem("evac_done"), L["ssd_xbc"].evac1 + BANKS)
            def group_squares(g):
                pe.wait_ge(sem("yz_sq"), 2 * (g + 1))
                for m in range(4):
                    ins = mm(pb[4 + g][:, 0:T], ones[:, :], sub[:, 4 * (g % 2) + m, :], start=m == 0, stop=m == 3)
                ins.then_inc(sem("yz_sum"), 1)

            for i in range(17):
                if i < 16:
                    c, hq = divmod(i, 8)
                    if i >= 2:
                        pe.wait_ge(sem("att_exp"), i - 1)
                    pe.wait_ge(sem("seg_ready"), i + 1)
                    mm(pb[i % 2][:, :], later[:, :], seg[i % 2], start=True, stop=True).then_inc(sem("bc_done"), 1)
                if i >= 1:
                    j = i - 1
                    c, hq = divmod(j, 8)
                    pe.wait_ge(sem("att_ready"), j + 1)
                    if j >= 2:
                        pe.wait_ge(sem("y_out_ssd"), j - 1)
                    for r in range(4):
                        h = 4 * hq + r
                        ins = mm(pb[2 + j % 2][64 * (h % 2):64 * (h % 2) + 64, P * (r // 2):P * (r // 2) + P],
                                 xdt[:, c, 64 * h:64 * h + 64], att[j % NATT][:, r, :], start=True, stop=True)
                    ins.then_inc(sem("y_done"), 1)
                if i in (13, 15):
                    group_squares((i - 13) // 2)
            for g in (2, 3):
                group_squares(g)
            pe.wait_ge(sem("y_out_ssd"), 16)
            pe_layer(pe, L["ssd_out"], yz_hi, yz_lo, "yz_lo_ready", 0)
            pe_layer(pe, L["up1"], x_hi, x_lo, "x_lo_ready", X_BASE[3], after_two=lambda: sum_squares(3))
            pe_layer(pe, L["down1"], act_hi, act_lo, "act_lo_ready", FC * 1)

            def q_sums(u, m):
                if (u, m) == (2, 2):
                    pe.wait_ge(sem("fox_sq"), 1)
                    head_sums(fox_tmp).then_inc(sem("fox_sum"), 1)
            pe_layer(pe, L["fox_qk"], x_hi, x_lo, "x_lo_ready", X_BASE[4], q_sums, after_two=lambda: sum_squares(4))
            pe.wait_ge(sem("fox_root"), 4)
            narrow_product(L["fox_f"], FOX_HEADS, 2)

            def vg_products(u, m):
                if (u, m) == (0, 2):
                    pe.wait_ge(sem("fox_sq"), 2)
                    pe.wait_ge(sem("abs_ready"), 2)
                    head_sums(fox_tmp).then_inc(sem("fox_sum"), 1)
                if (u, m) == (2, 0):
                    pe.wait_ge(sem("cum_fox"), 1)
                    pe.wait_ge(sem("fox_root"), 8)
                    for c in range(2):
                        ins = turn(pb[4][:, FOX_HEADS * c:FOX_HEADS * c + FOX_HEADS], acs[0:FOX_HEADS, P * c:P * c + P])
                    ins.then_inc(sem("cq_turned"), 1)
                if (u, m) == (2, 3):
                    pe.wait_ge(sem("cq_ready"), 1)
                    for i in range(4):
                        for r in range(4):
                            t = 4 * (i % 2) + r
                            ins = turn(pb[4 + i][:, P * r:P * r + P], v_t[:, t, P * (i // 2):P * (i // 2) + P])
                        ins.then_inc(sem("v_fox_turned"), 1)
            pe_layer(pe, L["fox_vg"], x_hi, x_lo, "x_lo_ready", X_BASE[4], vg_products)
            pe.wait_ge(sem("evac_done"), L["fox_vg"].evac1 + BANKS - 2)
            pe.wait_ge(sem("qk_ready"), 2)
            steps = 2 * FOX_HEADS
            for i in range(steps + 4):
                if i < steps:
                    h, qc = divmod(i, 2)
                    m, rows, n = h // 2, slice(64 * (h % 2), 64 * (h % 2) + 64), (qc + 1) * P
                    bank = pb[score_banks[i % NS]]
                    if i == 2:
                        pe.wait_ge(sem("evac_done"), L["fox_vg"].evac1 + BANKS)
                        pe.wait_ge(sem("v_fox_ready"), 4)
                    if i >= NS:
                        pe.wait_ge(sem("masked"), i - NS + 1)
                    mm(bank[:, 0:n], q_t[rows, m, P * qc:P * qc + P], k_t[rows, m, 0:n], start=True, stop=False)
                    mm(bank[:, 0:n], ident[0:FOX_HEADS, h:h + 1].broadcast_to([FOX_HEADS, P]), cum_neg[0:FOX_HEADS, 0:n],
                       start=False, stop=True).then_inc(sem("score_done"), 1)
                if 3 <= i < steps + 3:
                    j = i - 3
                    pe.wait_ge(sem("p_ready"), j + 1)
                    if j >= 2:
                        pe.wait_ge(sem("pt_ready"), j - 1)
                    for b in range(j % 2 + 1):
                        ins = turn(pb[2 + j % 2][:, P * b:P * b + P], sc[j % NS][:, 0, P * b:P * b + P])
                    ins.then_inc(sem("turned"), 1)
                if i >= 4:
                    j = i - 4
                    h, qc = divmod(j, 2)
                    m = h // 2
                    pe.wait_ge(sem("pt_ready"), j + 1)
                    if m >= 2:
                        pe.wait_ge(sem("o_ready"), m - 1)
                    for b in range(qc + 1):
                        ins = mm(pb[4 + m % 2][64 * (h % 2):64 * (h % 2) + 64, P * qc:P * qc + P],
                                 v_tok[:, b, 64 * h:64 * h + 64], pt[j % NS][:, P * b:P * b + P], start=b == 0, stop=b == qc)
                    ins.then_inc(sem("pv_done"), 1)
            pe_layer(pe, L["fox_out"], x_hi, x_lo, "x_lo_ready", X_BASE["fox"])
            pe_layer(pe, L["up2"], x_hi, x_lo, "x_lo_ready", X_BASE[5], after_two=lambda: sum_squares(5))
            pe_layer(pe, L["down2"], act_hi, act_lo, "act_lo_ready", FC * 2)
            sum_tiles(6)
            for i in range(4):
                c, b = divmod(i, 2)
                pe.wait_ge(sem("y_ready"), 4 * b + 4)
                for r in range(4):
                    ins = turn(pb[3 + i][:, P * r:P * r + P], tile(16, 4 * b + r)[:, P * c:P * c + P])
                ins.then_inc(sem("x_turned"), 1)


def kernel(**inputs):
    import numpy as _np
    import concourse.bacc as _bacc
    from concourse import mybir as _mybir
    from concourse.bass_utils import run_bass_kernel_spmd as _run

    nc = _bacc.Bacc("TRN2", target_bir_lowering=False, num_devices=1)
    arrays, args = {}, {}
    for name, value in inputs.items():
        v = _np.ascontiguousarray(value)
        if v.size == 0:
            continue
        arrays[f"in_{name}_dram"] = v
        args[name] = nc.dram_tensor(f"in_{name}_dram", v.shape, _mybir.dt.from_np(v.dtype), kind="ExternalInput").ap()
    out = nc.dram_tensor("out_0_dram", (1, T, D), F32, kind="ExternalOutput").ap()
    build(nc, args, out)
    r = _run(nc, [arrays], core_ids=[0])
    return r.results[0]["out_0_dram"]
```
